# Optimizing a Trainium2 kernel written in Bass

```python
import math
import jax, jax.numpy as jnp
from jax import lax
import numpy as np

D_MODEL = 2048
BATCH = 1
SEQ = 256
DEPTH = 1

N_MIXERS = 2
N_HEADS = 16
HEAD_DIM = 128
N_KV_GROUPS = 4
HEADS_PER_GROUP = N_HEADS // N_KV_GROUPS
CMP_BLOCK = 32
CMP_STRIDE = 16
CMP_HIDDEN = 2 * HEAD_DIM
SEL_BLOCK = 64
SEL_TOPK = 16
WINDOW = 512
Q_BLOCK = 128
N_GATES = 3
KV_WIDTH = N_KV_GROUPS * HEAD_DIM
NSA_IN_COLS = N_HEADS * HEAD_DIM + 6 * KV_WIDTH + N_GATES * N_HEADS
REL_BUCKETS = 32
REL_MAX_DIST = 128
SSM_GROUP = 16
SSM_GROUPS = D_MODEL // SSM_GROUP
SSM_STATE = 64
D_FF = ((8 * D_MODEL + 2) // 3 + 255) // 256 * 256
N_NSA_LAYERS = (DEPTH + N_MIXERS - 1) // N_MIXERS
N_S5_LAYERS = DEPTH // N_MIXERS
RMS_EPS = 1e-6
NEG_INF = -1e30
FORCE_SCORE = 1e9


def rmsnorm(x, g):
    x32 = x.astype(jnp.float32)
    y = x32 * lax.rsqrt(jnp.mean(x32 * x32, axis=-1, keepdims=True) + RMS_EPS)
    return (y * g.astype(jnp.float32)).astype(x.dtype)

def rel_bucket(dist):
    n = jnp.maximum(dist, 0)
    max_exact = REL_BUCKETS // 2
    large = max_exact + (jnp.log(jnp.maximum(n, 1).astype(jnp.float32) / max_exact)
                         / math.log(REL_MAX_DIST / max_exact)
                         * (REL_BUCKETS - max_exact)).astype(jnp.int32)
    large = jnp.minimum(large, REL_BUCKETS - 1)
    return jnp.where(n < max_exact, n, large)

def masked_softmax(s, mask):
    s = jnp.where(mask, s.astype(jnp.float32), NEG_INF)
    p = jax.nn.softmax(s, axis=-1)
    return jnp.where(mask, p, 0.0)

def nsa_mixer(h, rel_bias, w_in, w_out, pos_k, w1_k, w2_k, pos_v, w1_v, w2_v):
    Bsz, S, _ = h.shape
    G, HPG, DH = N_KV_GROUPS, HEADS_PER_GROUP, HEAD_DIM
    proj = h @ w_in
    qe = N_HEADS * DH
    bounds = [qe + i * KV_WIDTH for i in range(7)]
    q, kc, vc, ks, vs, kw, vw, gl = jnp.split(proj, bounds, axis=-1)
    q = q.reshape(Bsz, S, G, HPG, DH) * (DH ** -0.5)
    kc, vc, ks, vs, kw, vw = [a.reshape(Bsz, S, G, DH) for a in (kc, vc, ks, vs, kw, vw)]
    gates = jax.nn.sigmoid(gl.astype(jnp.float32)).astype(h.dtype).reshape(Bsz, S, N_GATES, G, HPG)
    t = jnp.arange(S, dtype=jnp.int32)

    n_cmp = (S - CMP_BLOCK) // CMP_STRIDE + 1
    starts = jnp.arange(n_cmp, dtype=jnp.int32) * CMP_STRIDE
    gidx = starts[:, None] + jnp.arange(CMP_BLOCK, dtype=jnp.int32)[None, :]

    def compress(kv, pos, w1, w2):
        blk = kv[:, gidx] + pos[None, None, :, None, :]
        blk = jnp.moveaxis(blk, 3, 2).reshape(Bsz, n_cmp, G, CMP_BLOCK * DH)
        return jax.nn.gelu(blk @ w1) @ w2

    kcc = compress(kc, pos_k, w1_k, w2_k)
    vcc = compress(vc, pos_v, w1_v, w2_v)
    dist_c = t[:, None] - (starts + CMP_BLOCK - 1)[None, :]
    mask_c = dist_c >= 0
    bias_c = rel_bias[rel_bucket(dist_c)].transpose(2, 0, 1).reshape(G, HPG, S, n_cmp)
    s_c = jnp.einsum('btghd,bcgd->bghtc', q, kcc).astype(jnp.float32) + bias_c
    p_c = masked_softmax(s_c, mask_c)
    o_c = jnp.einsum('bghtc,bcgd->btghd', p_c.astype(vcc.dtype), vcc)

    imp = p_c.sum(axis=2)
    n_sel = S // SEL_BLOCK
    ratio = SEL_BLOCK // CMP_STRIDE
    lo = CMP_BLOCK // CMP_STRIDE - 1
    count = ratio + lo
    right = max(0, (count - 1) + ratio * n_sel - lo - n_cmp)
    imp_pad = jnp.pad(imp, ((0, 0), (0, 0), (0, 0), (lo, right)))
    imp_slc = sum(imp_pad[..., k:k + ratio * n_sel:ratio] for k in range(count))
    j = jnp.arange(n_sel, dtype=jnp.int32)
    t_blk = t // SEL_BLOCK
    forced = (j[None, :] == 0) | (j[None, :] == t_blk[:, None]) | (j[None, :] == t_blk[:, None] - 1)
    causal_blk = (j * SEL_BLOCK)[None, :] <= t[:, None]
    score = jnp.where(forced, FORCE_SCORE, imp_slc)
    score = jnp.where(causal_blk, score, NEG_INF)
    k_top = min(SEL_TOPK, n_sel)
    _, sel_idx = lax.top_k(score, k_top)

    ks_blocks = ks.reshape(Bsz, n_sel, SEL_BLOCK, G, DH).transpose(0, 3, 1, 2, 4)
    vs_blocks = vs.reshape(Bsz, n_sel, SEL_BLOCK, G, DH).transpose(0, 3, 1, 2, 4)
    nq = S // Q_BLOCK
    q_chunks = q.reshape(Bsz, nq, Q_BLOCK, G, HPG, DH).transpose(1, 0, 2, 3, 4, 5)
    idx_chunks = sel_idx.reshape(Bsz, G, nq, Q_BLOCK, k_top).transpose(2, 0, 1, 3, 4)
    t0s = jnp.arange(nq, dtype=jnp.int32) * Q_BLOCK
    table_g = rel_bias.T.reshape(G, HPG, REL_BUCKETS)
    bi = jnp.arange(Bsz)[:, None, None, None]
    gi = jnp.arange(G)[None, :, None, None]
    gi5 = jnp.arange(G)[None, :, None, None, None]
    hi5 = jnp.arange(HPG)[None, None, :, None, None]
    in_blk = jnp.arange(SEL_BLOCK, dtype=jnp.int32)

    def sel_chunk(args):
        qc, ic, t0 = args
        kg = ks_blocks[bi, gi, ic].reshape(Bsz, G, Q_BLOCK, k_top * SEL_BLOCK, DH)
        vg = vs_blocks[bi, gi, ic].reshape(Bsz, G, Q_BLOCK, k_top * SEL_BLOCK, DH)
        kpos = (ic[..., None] * SEL_BLOCK + in_blk).reshape(Bsz, G, Q_BLOCK, k_top * SEL_BLOCK)
        tq = t0 + jnp.arange(Q_BLOCK, dtype=jnp.int32)
        dist = tq[None, None, :, None] - kpos
        bias = table_g[gi5, hi5, rel_bucket(dist)[:, :, None]]
        s = jnp.einsum('bqghd,bgqkd->bghqk', qc, kg).astype(jnp.float32) + bias
        p = masked_softmax(s, (dist >= 0)[:, :, None])
        return jnp.einsum('bghqk,bgqkd->bqghd', p.astype(vg.dtype), vg)

    o_s = lax.map(sel_chunk, (q_chunks, idx_chunks, t0s))
    o_s = o_s.transpose(1, 0, 2, 3, 4, 5).reshape(Bsz, S, G, HPG, DH)

    nb = S // Q_BLOCK
    n_band = WINDOW // Q_BLOCK

    def band(kv):
        padded = jnp.pad(kv, ((0, 0), (WINDOW, 0), (0, 0), (0, 0))).reshape(Bsz, nb + n_band, Q_BLOCK, G, DH)
        return jnp.concatenate([padded[:, i:i + nb] for i in range(n_band + 1)], axis=2)

    kwb, vwb = band(kw), band(vw)
    qi = jnp.arange(Q_BLOCK, dtype=jnp.int32)
    ki = jnp.arange((n_band + 1) * Q_BLOCK, dtype=jnp.int32)
    dist_w = qi[:, None] + WINDOW - ki[None, :]
    key_abs = jnp.arange(nb, dtype=jnp.int32)[:, None] * Q_BLOCK - WINDOW + ki[None, :]
    mask_w = ((dist_w >= 0) & (dist_w < WINDOW))[None] & (key_abs >= 0)[:, None, :]
    bias_w = rel_bias[rel_bucket(dist_w)].transpose(2, 0, 1).reshape(G, HPG, Q_BLOCK, -1)
    qw = q.reshape(Bsz, nb, Q_BLOCK, G, HPG, DH)
    s_w = jnp.einsum('bjqghd,bjkgd->bjghqk', qw, kwb).astype(jnp.float32) + bias_w
    p_w = masked_softmax(s_w, mask_w[:, None, None])
    o_w = jnp.einsum('bjghqk,bjkgd->bjqghd', p_w.astype(vwb.dtype), vwb).reshape(Bsz, S, G, HPG, DH)

    o = (gates[:, :, 0, :, :, None] * o_c + gates[:, :, 1, :, :, None] * o_s
         + gates[:, :, 2, :, :, None] * o_w)
    return o.reshape(Bsz, S, N_HEADS * DH) @ w_out

def s5_mixer(h, A_re, A_im, log_dt, B_re, B_im, C_re, C_im, D_skip, w_glu):
    Bsz, S, D = h.shape
    f32 = jnp.float32
    A_re, A_im, log_dt = A_re.astype(f32), A_im.astype(f32), log_dt.astype(f32)
    B_re, B_im, C_re, C_im = B_re.astype(f32), B_im.astype(f32), C_re.astype(f32), C_im.astype(f32)
    u = h.astype(f32).reshape(Bsz, S, SSM_GROUPS, SSM_GROUP)
    dt = jnp.exp(log_dt)[:, None]
    decay = jnp.exp(A_re * dt)
    ab_re = decay * jnp.cos(A_im * dt)
    ab_im = decay * jnp.sin(A_im * dt)
    pr, pi_ = ab_re - 1.0, ab_im
    den = A_re * A_re + A_im * A_im
    cf_re = (pr * A_re + pi_ * A_im) / den
    cf_im = (pi_ * A_re - pr * A_im) / den
    bb_re = cf_re[..., None] * B_re - cf_im[..., None] * B_im
    bb_im = cf_re[..., None] * B_im + cf_im[..., None] * B_re
    bu_re = jnp.einsum('bsgc,gnc->bsgn', u, bb_re)
    bu_im = jnp.einsum('bsgc,gnc->bsgn', u, bb_im)
    a_re = jnp.broadcast_to(ab_re, bu_re.shape)
    a_im = jnp.broadcast_to(ab_im, bu_im.shape)

    def combine(e1, e2):
        a1r, a1i, b1r, b1i = e1
        a2r, a2i, b2r, b2i = e2
        return (a1r * a2r - a1i * a2i, a1r * a2i + a1i * a2r,
                a2r * b1r - a2i * b1i + b2r, a2r * b1i + a2i * b1r + b2i)

    _, _, x_re, x_im = lax.associative_scan(combine, (a_re, a_im, bu_re, bu_im), axis=1)
    y = (jnp.einsum('bsgn,gcn->bsgc', x_re, C_re) - jnp.einsum('bsgn,gcn->bsgc', x_im, C_im)
         + D_skip.astype(f32).reshape(SSM_GROUPS, SSM_GROUP) * u)
    y = jax.nn.gelu(y).reshape(Bsz, S, D).astype(h.dtype)
    z = y @ w_glu
    return z[..., :D] * jax.nn.sigmoid(z[..., D:])

def swiglu(h, w_in, w_out):
    z = h @ w_in
    a, b = z[..., :D_FF], z[..., D_FF:]
    return (jax.nn.silu(a) * b) @ w_out

def first_inputs(seed: int = 0) -> dict:
    key = jax.random.key(seed)
    ks = jax.random.split(key, 32)

    def nrm(k, shape, scale):
        return jax.random.normal(k, shape, jnp.float32) * scale

    D, H, DH, G, N, C = D_MODEL, N_HEADS, HEAD_DIM, SSM_GROUPS, SSM_STATE, SSM_GROUP
    n_idx = jnp.arange(N, dtype=jnp.float32)
    return {
        "x": nrm(ks[0], (BATCH, SEQ, D), 1.0),
        "rel_bias": nrm(ks[1], (REL_BUCKETS, H), 0.2),
        "mix_norm_g": 1.0 + nrm(ks[2], (DEPTH, D), 0.02),
        "ffn_norm_g": 1.0 + nrm(ks[3], (DEPTH, D), 0.02),
        "final_norm_g": 1.0 + nrm(ks[4], (D,), 0.02),
        "nsa_w_in": nrm(ks[5], (N_NSA_LAYERS, D, NSA_IN_COLS), D ** -0.5),
        "nsa_w_out": nrm(ks[6], (N_NSA_LAYERS, H * DH, D), (H * DH) ** -0.5),
        "cmp_pos_k": nrm(ks[7], (N_NSA_LAYERS, CMP_BLOCK, DH), 0.1),
        "cmp_w1_k": nrm(ks[8], (N_NSA_LAYERS, CMP_BLOCK * DH, CMP_HIDDEN), (CMP_BLOCK * DH) ** -0.5),
        "cmp_w2_k": nrm(ks[9], (N_NSA_LAYERS, CMP_HIDDEN, DH), CMP_HIDDEN ** -0.5),
        "cmp_pos_v": nrm(ks[10], (N_NSA_LAYERS, CMP_BLOCK, DH), 0.1),
        "cmp_w1_v": nrm(ks[11], (N_NSA_LAYERS, CMP_BLOCK * DH, CMP_HIDDEN), (CMP_BLOCK * DH) ** -0.5),
        "cmp_w2_v": nrm(ks[12], (N_NSA_LAYERS, CMP_HIDDEN, DH), CMP_HIDDEN ** -0.5),
        "s5_A_re": -0.5 + nrm(ks[13], (N_S5_LAYERS, G, N), 0.01),
        "s5_A_im": math.pi * n_idx + nrm(ks[14], (N_S5_LAYERS, G, N), 0.01),
        "s5_log_dt": jax.random.uniform(ks[15], (N_S5_LAYERS, G), jnp.float32,
                                        math.log(1e-3), math.log(1e-1)),
        "s5_B_re": nrm(ks[16], (N_S5_LAYERS, G, N, C), (2 * C) ** -0.5),
        "s5_B_im": nrm(ks[17], (N_S5_LAYERS, G, N, C), (2 * C) ** -0.5),
        "s5_C_re": nrm(ks[18], (N_S5_LAYERS, G, C, N), (2 * N) ** -0.5),
        "s5_C_im": nrm(ks[19], (N_S5_LAYERS, G, C, N), (2 * N) ** -0.5),
        "s5_D": nrm(ks[20], (N_S5_LAYERS, D), 1.0),
        "s5_w_glu": nrm(ks[21], (N_S5_LAYERS, D, 2 * D), D ** -0.5),
        "ffn_w_in": nrm(ks[22], (DEPTH, D, 2 * D_FF), D ** -0.5),
        "ffn_w_out": nrm(ks[23], (DEPTH, D_FF, D), D_FF ** -0.5),
    }

def first_block(x, rel_bias, mix_norm_g, ffn_norm_g, final_norm_g, nsa_w_in, nsa_w_out,
              cmp_pos_k, cmp_w1_k, cmp_w2_k, cmp_pos_v, cmp_w1_v, cmp_w2_v,
              s5_A_re, s5_A_im, s5_log_dt, s5_B_re, s5_B_im, s5_C_re, s5_C_im, s5_D, s5_w_glu,
              ffn_w_in, ffn_w_out):
    h = x
    for i in range(DEPTH):
        hn = rmsnorm(h, mix_norm_g[i])
        li = i // N_MIXERS
        if i % N_MIXERS == 0:
            h = h + nsa_mixer(hn, rel_bias, nsa_w_in[li], nsa_w_out[li],
                              cmp_pos_k[li], cmp_w1_k[li], cmp_w2_k[li],
                              cmp_pos_v[li], cmp_w1_v[li], cmp_w2_v[li])
        else:
            h = h + s5_mixer(hn, s5_A_re[li], s5_A_im[li], s5_log_dt[li], s5_B_re[li], s5_B_im[li],
                             s5_C_re[li], s5_C_im[li], s5_D[li], s5_w_glu[li])
        h = h + swiglu(rmsnorm(h, ffn_norm_g[i]), ffn_w_in[i], ffn_w_out[i])
    return rmsnorm(h, final_norm_g)


MIX_WIDTH = D_MODEL
BLOCK = 128
EPS = 1e-6

SWA_HEADS = 16
SWA_KV_HEADS = 2
SWA_HEAD_DIM = 64
SWA_GROUP = SWA_HEADS // SWA_KV_HEADS
WINDOW_2 = 128


MLA_HEADS = 8
MLA_Q_RANK = 384
MLA_KV_RANK = 128
MLA_NOPE_DIM = 128
MLA_ROPE_DIM = 64
MLA_V_DIM = 128
MLA_QK_DIM = MLA_NOPE_DIM + MLA_ROPE_DIM
ROPE_THETA = 10000.0

D_FF_2 = 4 * D_MODEL

SWA_Q_COLS = SWA_HEADS * SWA_HEAD_DIM
SWA_KV_COLS = SWA_KV_HEADS * SWA_HEAD_DIM
OFF_SWA_Q = 0
OFF_SWA_K = OFF_SWA_Q + SWA_Q_COLS
OFF_SWA_V = OFF_SWA_K + SWA_KV_COLS
OFF_MLA_CQ = OFF_SWA_V + SWA_KV_COLS
OFF_MLA_CKV = OFF_MLA_CQ + MLA_Q_RANK
OFF_MLA_KR = OFF_MLA_CKV + MLA_KV_RANK
IN_COLS = OFF_MLA_KR + MLA_ROPE_DIM
SWA_OUT = SWA_HEADS * SWA_HEAD_DIM
MLA_OUT = MLA_HEADS * MLA_V_DIM


def rmsnorm_2(x, g):
    x32 = x.astype(jnp.float32)
    y = x32 * lax.rsqrt(jnp.mean(x32 * x32, axis=-1, keepdims=True) + EPS)
    return y.astype(x.dtype) * g

def t5_causal_bucket(dist):
    n = jnp.maximum(dist, 0)
    max_exact = REL_BUCKETS // 2
    is_small = n < max_exact
    nf = jnp.maximum(n, 1).astype(jnp.float32)
    large = max_exact + (jnp.log(nf / max_exact) / math.log(REL_MAX_DIST / max_exact)
                         * (REL_BUCKETS - max_exact)).astype(jnp.int32)
    large = jnp.minimum(large, REL_BUCKETS - 1)
    return jnp.where(is_small, n, large)

def rope(x, positions):
    half = x.shape[-1] // 2
    inv_freq = ROPE_THETA ** (-jnp.arange(half, dtype=jnp.float32) / half)
    ang = positions.astype(jnp.float32)[:, None] * inv_freq[None, :]
    extra = x.ndim - 3
    ang = ang.reshape((1, ang.shape[0]) + (1,) * extra + (half,))
    cos = jnp.cos(ang).astype(x.dtype)
    sin = jnp.sin(ang).astype(x.dtype)
    x1, x2 = x[..., :half], x[..., half:]
    return jnp.concatenate([x1 * cos - x2 * sin, x2 * cos + x1 * sin], axis=-1)

def swa_sink_attention(q, k, v, sinks, rel_bias):
    B, S = q.shape[0], q.shape[1]
    nb = S // BLOCK
    qb = q.reshape(B, nb, BLOCK, SWA_KV_HEADS, SWA_GROUP, SWA_HEAD_DIM)
    kb = k.reshape(B, nb, BLOCK, SWA_KV_HEADS, SWA_HEAD_DIM)
    vb = v.reshape(B, nb, BLOCK, SWA_KV_HEADS, SWA_HEAD_DIM)
    zero = jnp.zeros_like(kb[:, :1])
    k_band = jnp.concatenate([jnp.concatenate([zero, kb[:, :-1]], axis=1), kb], axis=2)
    v_band = jnp.concatenate([jnp.concatenate([zero, vb[:, :-1]], axis=1), vb], axis=2)
    s = jnp.einsum('bnqhgd,bnkhd->bnhgqk', qb, k_band).astype(jnp.float32) * (SWA_HEAD_DIM ** -0.5)

    q_loc = jnp.arange(BLOCK)[:, None]
    k_loc = jnp.arange(2 * BLOCK)[None, :]
    dist = q_loc + BLOCK - k_loc
    in_window = (dist >= 0) & (dist < WINDOW_2)
    blk = jnp.arange(nb)[:, None]
    key_valid = (blk * BLOCK - BLOCK + k_loc) >= 0
    mask = in_window[None] & key_valid[:, None, :]

    bias = rel_bias.astype(jnp.float32)[t5_causal_bucket(dist)]
    bias = bias.transpose(2, 0, 1).reshape(SWA_KV_HEADS, SWA_GROUP, BLOCK, 2 * BLOCK)
    s = s + bias[None, None]
    s = jnp.where(mask[None, :, None, None], s, -jnp.inf)

    sink = sinks.astype(jnp.float32).reshape(SWA_KV_HEADS, SWA_GROUP)[None, None, :, :, None, None]
    m = jnp.maximum(jnp.max(s, axis=-1, keepdims=True), sink)
    p = jnp.exp(s - m)
    p = p / (jnp.sum(p, axis=-1, keepdims=True) + jnp.exp(sink - m))
    o = jnp.einsum('bnhgqk,bnkhd->bnqhgd', p.astype(v.dtype), v_band)
    return o.reshape(B, S, SWA_OUT)

def mla_attention(q_nope, q_rope, k_nope, k_rope, v):
    B, S = q_nope.shape[0], q_nope.shape[1]
    nb = S // BLOCK
    qn = q_nope.reshape(B, nb, BLOCK, MLA_HEADS, MLA_NOPE_DIM).transpose(1, 0, 2, 3, 4)
    qr = q_rope.reshape(B, nb, BLOCK, MLA_HEADS, MLA_ROPE_DIM).transpose(1, 0, 2, 3, 4)
    key_pos = jnp.arange(S)
    scale = MLA_QK_DIM ** -0.5

    def one_block(args):
        i, qn_i, qr_i = args
        s = (jnp.einsum('bqhd,bkhd->bhqk', qn_i, k_nope)
             + jnp.einsum('bqhd,bkd->bhqk', qr_i, k_rope)).astype(jnp.float32) * scale
        q_pos = i * BLOCK + jnp.arange(BLOCK)
        causal = key_pos[None, :] <= q_pos[:, None]
        s = jnp.where(causal[None, None], s, -jnp.inf)
        p = jax.nn.softmax(s, axis=-1)
        return jnp.einsum('bhqk,bkhd->bqhd', p.astype(v.dtype), v)

    o = lax.map(one_block, (jnp.arange(nb), qn, qr))
    return o.transpose(1, 0, 2, 3, 4).reshape(B, S, MLA_OUT)

def second_inputs(seed: int = 0) -> dict:
    key = jax.random.key(seed)
    ks = jax.random.split(key, 20)
    f32 = jnp.float32
    nrm = lambda k, shape, s: jax.random.normal(k, shape, f32) * s
    return {
        "x": nrm(ks[0], (BATCH, SEQ, D_MODEL), 1.0),
        "c": nrm(ks[1], (BATCH, D_MODEL), 1.0),
        "w_mod": nrm(ks[2], (DEPTH, D_MODEL, 6 * D_MODEL), 0.5 * D_MODEL ** -0.5),
        "b_mod": nrm(ks[3], (DEPTH, 6 * D_MODEL), 0.01),
        "attn_norm_g": 1.0 + nrm(ks[4], (DEPTH, D_MODEL), 0.02),
        "w_in": nrm(ks[5], (DEPTH, D_MODEL, IN_COLS), D_MODEL ** -0.5),
        "swa_sinks": nrm(ks[6], (DEPTH, SWA_HEADS), 1.0),
        "rel_bias": nrm(ks[7], (REL_BUCKETS, SWA_HEADS), 0.5),
        "mla_q_norm_g": 1.0 + nrm(ks[8], (DEPTH, MLA_Q_RANK), 0.02),
        "w_uq": nrm(ks[9], (DEPTH, MLA_Q_RANK, MLA_HEADS * MLA_QK_DIM), MLA_Q_RANK ** -0.5),
        "mla_kv_norm_g": 1.0 + nrm(ks[10], (DEPTH, MLA_KV_RANK), 0.02),
        "w_ukv": nrm(ks[11], (DEPTH, MLA_KV_RANK, MLA_HEADS * (MLA_NOPE_DIM + MLA_V_DIM)), MLA_KV_RANK ** -0.5),
        "w_out": nrm(ks[12], (DEPTH, MIX_WIDTH, D_MODEL), MIX_WIDTH ** -0.5),
        "mlp_norm_g": 1.0 + nrm(ks[13], (DEPTH, D_MODEL), 0.02),
        "w_ff1": nrm(ks[14], (DEPTH, D_MODEL, D_FF_2), D_MODEL ** -0.5),
        "w_ff2": nrm(ks[15], (DEPTH, D_FF_2, D_MODEL), D_FF_2 ** -0.5),
        "final_norm_g": 1.0 + nrm(ks[16], (D_MODEL,), 0.02),
    }

def second_block(x, c, w_mod, b_mod, attn_norm_g, w_in, swa_sinks, rel_bias, mla_q_norm_g, w_uq,
              mla_kv_norm_g, w_ukv, w_out, mlp_norm_g, w_ff1, w_ff2, final_norm_g):
    B, S, _ = x.shape
    positions = jnp.arange(S)
    c_act = jax.nn.silu(c)
    for l in range(DEPTH):
        mod = c_act @ w_mod[l] + b_mod[l]
        sh1, sc1, g1, sh2, sc2, g2 = [m[:, None, :] for m in jnp.split(mod, 6, axis=-1)]

        h = rmsnorm_2(x, attn_norm_g[l]) * (1.0 + sc1) + sh1
        proj = jnp.einsum('bsd,df->bsf', h, w_in[l])

        q_a = proj[..., OFF_SWA_Q:OFF_SWA_K].reshape(B, S, SWA_HEADS, SWA_HEAD_DIM)
        k_a = proj[..., OFF_SWA_K:OFF_SWA_V].reshape(B, S, SWA_KV_HEADS, SWA_HEAD_DIM)
        v_a = proj[..., OFF_SWA_V:OFF_MLA_CQ].reshape(B, S, SWA_KV_HEADS, SWA_HEAD_DIM)
        o_a = swa_sink_attention(q_a, k_a, v_a, swa_sinks[l], rel_bias)

        c_q = rmsnorm_2(proj[..., OFF_MLA_CQ:OFF_MLA_CKV], mla_q_norm_g[l])
        c_kv = rmsnorm_2(proj[..., OFF_MLA_CKV:OFF_MLA_KR], mla_kv_norm_g[l])
        k_rope = rope(proj[..., OFF_MLA_KR:IN_COLS], positions)
        q_b = jnp.einsum('bsr,rf->bsf', c_q, w_uq[l]).reshape(B, S, MLA_HEADS, MLA_QK_DIM)
        q_nope = q_b[..., :MLA_NOPE_DIM]
        q_rope = rope(q_b[..., MLA_NOPE_DIM:], positions)
        kv_b = jnp.einsum('bsr,rf->bsf', c_kv, w_ukv[l]).reshape(B, S, MLA_HEADS, MLA_NOPE_DIM + MLA_V_DIM)
        k_nope = kv_b[..., :MLA_NOPE_DIM]
        v_b = kv_b[..., MLA_NOPE_DIM:]
        o_b = mla_attention(q_nope, q_rope, k_nope, k_rope, v_b)

        mix = jnp.concatenate([o_a, o_b], axis=-1)
        x = x + g1 * jnp.einsum('bsm,md->bsd', mix, w_out[l])

        h = rmsnorm_2(x, mlp_norm_g[l]) * (1.0 + sc2) + sh2
        u = jax.nn.relu(jnp.einsum('bsd,df->bsf', h, w_ff1[l]))
        x = x + g2 * jnp.einsum('bsf,fd->bsd', u * u, w_ff2[l])
    return rmsnorm_2(x, final_norm_g)


def setup_inputs(seed=0):
    out = dict(first_inputs(seed))
    for name, value in second_inputs(seed + 1).items():
        if name != "x":
            out[name + "_2"] = value
    return out


def reference(
    x, rel_bias, mix_norm_g, ffn_norm_g, final_norm_g, nsa_w_in, nsa_w_out, cmp_pos_k, cmp_w1_k,
    cmp_w2_k, cmp_pos_v, cmp_w1_v, cmp_w2_v, s5_A_re, s5_A_im, s5_log_dt, s5_B_re, s5_B_im,
    s5_C_re, s5_C_im, s5_D, s5_w_glu, ffn_w_in, ffn_w_out, c_2, w_mod_2, b_mod_2, attn_norm_g_2,
    w_in_2, swa_sinks_2, rel_bias_2, mla_q_norm_g_2, w_uq_2, mla_kv_norm_g_2, w_ukv_2, w_out_2,
    mlp_norm_g_2, w_ff1_2, w_ff2_2, final_norm_g_2,
):
    x = first_block(
        x, rel_bias, mix_norm_g, ffn_norm_g, final_norm_g, nsa_w_in, nsa_w_out, cmp_pos_k,
        cmp_w1_k, cmp_w2_k, cmp_pos_v, cmp_w1_v, cmp_w2_v, s5_A_re, s5_A_im, s5_log_dt, s5_B_re,
        s5_B_im, s5_C_re, s5_C_im, s5_D, s5_w_glu, ffn_w_in, ffn_w_out,
    )
    return second_block(
        x, c_2, w_mod_2, b_mod_2, attn_norm_g_2, w_in_2, swa_sinks_2, rel_bias_2,
        mla_q_norm_g_2, w_uq_2, mla_kv_norm_g_2, w_ukv_2, w_out_2, mlp_norm_g_2, w_ff1_2,
        w_ff2_2, final_norm_g_2,
    )


_drawn_inputs = setup_inputs


def setup_inputs(seed=0):
    import zlib

    import numpy as np

    out = dict(_drawn_inputs(seed))
    spreads = {}
    factors = {'mix_norm_g': 7.388,
     'ffn_norm_g': 4.024,
     'final_norm_g': 2.806,
     'cmp_pos_k': 8.0,
     'b_mod_2': 3.729,
     'attn_norm_g_2': 8.0,
     'swa_sinks_2': 45.867,
     'rel_bias_2': 3.033,
     'mla_q_norm_g_2': 8.0,
     'mla_kv_norm_g_2': 8.0,
     'mlp_norm_g_2': 6.159,
     'final_norm_g_2': 7.775}
    for name, (base, spread) in spreads.items():
        noise = np.random.default_rng([zlib.crc32(name.encode()), seed]).standard_normal(out[name].shape)
        drawn = base * np.exp(spread * noise) if base else spread * noise
        out[name] = __import__('jax').numpy.asarray(drawn.astype(out[name].dtype))
    for name, factor in factors.items():
        out[name] = (out[name] * factor).astype(out[name].dtype)
    return out
```

```python
import math

import numpy as np

import concourse.bass as bass
from concourse import mybir

F32 = mybir.dt.float32
F32R = mybir.dt.float32r
ALU = mybir.AluOpType
ACT = mybir.ActivationFunctionType
AX_X = mybir.AxisListType.X

S = 256
D = 2048
KT = D // 128
FF1 = 5632
FF2 = 8192
NEG = -1e30
EPS = 1e-6
NRAW = 3
KB = 1024
BASE = 16 * KB + 128

IN_NAMES = [
    "x", "rel_bias", "mix_norm_g", "ffn_norm_g", "final_norm_g", "nsa_w_in", "nsa_w_out",
    "cmp_pos_k", "cmp_w1_k", "cmp_w2_k", "cmp_pos_v", "cmp_w1_v", "cmp_w2_v", "ffn_w_in", "ffn_w_out",
    "c_2", "w_mod_2", "b_mod_2", "attn_norm_g_2", "w_in_2", "swa_sinks_2", "rel_bias_2",
    "mla_q_norm_g_2", "w_uq_2", "mla_kv_norm_g_2", "w_ukv_2", "w_out_2", "mlp_norm_g_2",
    "w_ff1_2", "w_ff2_2", "final_norm_g_2",
]


def shape_constants():
    n = np.arange(0, 256)
    large = 16 + (np.log(np.maximum(n, 1).astype(np.float32) / np.float32(16))
                  / np.float32(math.log(128 / 16)) * np.float32(16)).astype(np.int32)
    bucket = np.where(n < 16, n, np.minimum(large, 31))

    def onehot(dist, far):
        t = np.zeros((33, len(dist)), np.float32)
        for i, d in enumerate(dist):
            if 0 <= d < far:
                t[bucket[d], i] = 1.0
            else:
                t[32, i] = 1.0
        return t

    up = np.clip(np.arange(512) - 255, -255, 255)
    down = np.clip(255 - np.arange(384), -127, 255)
    oh = np.concatenate([onehot(up, 256), onehot(down, 256), onehot(down, 128)], axis=1)
    inv = (10000.0 ** (-np.arange(32, dtype=np.float32) / np.float32(32))).astype(np.float32)
    ang = inv[:, None] * np.arange(S, dtype=np.float32)[None, :]
    cos, sin = np.cos(ang).astype(np.float32), np.sin(ang).astype(np.float32)
    t = np.arange(128)[:, None]
    j = np.arange(256)[None, :]
    return {
        "c_ident": np.eye(128, dtype=np.float32),
        "c_ones": np.ones((128, 128), np.float32),
        "c_onehot": oh,
        "c_cos": np.concatenate([cos] * 4, axis=0),
        "c_sin": np.concatenate([-sin, sin, -sin, sin], axis=0),
        "c_causal": np.where(128 + t - j >= 0, 0.0, NEG).astype(np.float32),
    }


def flat(waits):
    for w in waits:
        if w is None:
            continue
        if isinstance(w, list):
            yield from flat(w)
        else:
            yield w


class Queue:

    def __init__(self, sem):
        self.sem, self.n, self.ops = sem, 0, []

    def __call__(self, fn, *waits, inc=True):
        self.n += inc
        self.ops.append((fn, list(flat(waits)), inc))
        return (self.sem, self.n) if inc else None

    def play(self, eng):
        seen = {}
        for fn, waits, inc in self.ops:
            need = {}
            for sem, v in waits:
                if v > seen.get(sem.num, 0) and v > need.get(sem.num, (sem, 0))[1]:
                    need[sem.num] = (sem, v)
            for num, (sem, v) in need.items():
                eng.wait_ge(sem, v)
                seen[num] = v
            ins = fn(eng)
            if inc:
                ins.then_inc(self.sem, 1)


class Landing:

    def __init__(self, sem):
        self.sem, self.n = sem, 0

    def start(self, q, dst, src, *waits):
        self.n += 16
        q(lambda e: e.dma_start(dst, src).then_inc(self.sem, 16), *waits, inc=False)
        return (self.sem, self.n)


def build(nc, A, out):
    sems = [0]

    def sem(name):
        sems[0] += 1
        return nc.alloc_semaphore(name)

    at = [BASE]

    def sb(name, shape, dt=F32, offset=None):
        size = int(np.prod(shape[1:])) * 4
        if offset is None:
            offset = at[0]
            at[0] += (size + 31) // 32 * 32
        return nc.alloc_sbuf_tensor_at("m_" + name, shape, dt, offset=offset)

    pe, act, dve = Queue(sem("s_pe")), Queue(sem("s_act")), Queue(sem("s_dve"))
    pool, sp = Queue(sem("s_pool")), Queue(sem("s_sp"))

    xT = sb("xT", [128, KT, S])
    HI = sb("HI", [128, KT, S], F32R)
    LO = sb("LO", [128, KT, S], F32R)
    RAW = [sb(f"RAW{i}", [128, 2048]) for i in range(NRAW)]
    WHI = [sb(f"WHI{i}", [128, 2048], F32R) for i in range(2)]
    WLO = [sb(f"WLO{i}", [128, 2048], F32R) for i in range(2)]
    ACC = sb("ACC", [128, 2048])
    ident = sb("ident", [128, 128])
    ones = sb("ones", [128, 128])
    cols = sb("cols", [128, 116])
    cact = sb("cact", [128, 16])
    bmod = sb("bmod", [128, 96])
    mod = sb("mod", [128, 96])
    G1c = sb("G1c", [128, 16])
    G2c = sb("G2c", [128, 16])
    gates = sb("gates", [128, 3, 16, 4])
    cmpb = sb("cmpb", [128, 32, 15])
    rstd = sb("rstd", [128, S])
    std = sb("std", [128, S])
    causal = sb("causal", [128, S])
    w2 = sb("w2", [128, 2, 2, 128])
    hidT = sb("hidT", [128, 2, 2, 60])
    kccT = sb("kccT", [128, 60])
    posT = sb("posT", [128, 64])
    epsc = sb("epsc", [128, 1])
    sinkr = sb("sinkr", [128, 16])
    SK = sb("SK", [128, 8, 4])
    rela = sb("rela", [33, 16])
    relb = sb("relb", [33, 16])
    stat = sb("stat", [128, 3, 6, 4])
    cst = sb("cst", [128, 4, 32])
    U = at[0]
    assert U + 76 * KB <= 229344, (U, 229344 - U)

    def un(name, shape, kb, dt=F32):
        return sb(name, shape, dt, offset=U + int(kb * KB))

    XROW = un("XROW", [128, 2, D], 0)
    OH = un("OH", [33, 1280], 16)
    rowsA = un("rowsA", [116, 128], 21)
    rowsB = un("rowsB", [96, 128], 21.5)
    rowsP = un("rowsP", [64, 128], 22)
    R16a = un("R16a", [16, 384], 22.5)
    R16b = un("R16b", [16, 384], 24)
    qT = un("qT", [128, 16, S], 0)
    ksT = un("ksT", [128, 4, S], 16)
    kwT = un("kwT", [128, 4, S], 20)
    vs = un("vs", [128, 2, 512], 24)
    vw = un("vw", [128, 2, 512], 28)
    biasA = un("biasA", [128, 16, S], 32)
    Vpad = un("Vpad", [128, 16, 128], 48)
    PcT = un("PcT", [128, 4, S], 56)
    kcT = un("kcT", [128, 4, S], 60)
    vcT = un("vcT", [128, 4, S], 64)
    Z = un("Z", [128, 32, 60], 68)
    SP1 = [un(f"SP1_{i}", [128, 768], 60 + 3 * i) for i in range(3)]
    PT1 = [un(f"PT1_{i}", [128, 2, 384], 69 + 3 * i) for i in range(2)]
    Pc = un("Pc", [128, 2, 16, 32], 72)
    HIDH = un("HIDH", [128, 24, S], 0, F32R)
    HIDL = un("HIDL", [128, 24, S], 24, F32R)
    SA = [un(f"SA{i}", [128, 4, S], 48 + 4 * i) for i in range(2)]
    HT = [un(f"HT{i}", [128, 4, S], 56 + 4 * i) for i in range(2)]
    SQ = [un(f"SQ{i}", [128, 4, S], 64 + 4 * i) for i in range(2)]
    qaT = un("qaT", [128, 8, S], 0)
    Kpad = un("Kpad", [128, 2, 2, S], 8)
    Vpad2 = un("Vpad2", [128, 2, 2, 2, 128], 12)
    CQH = un("CQH", [128, 4, S], 16, F32R)
    CQL = un("CQL", [128, 4, S], 20, F32R)
    krp = un("krp", [128, S], 24)
    SP2 = [un(f"SP2_{i}", [128, 768], 64 + 3 * i) for i in range(3)]
    PT2 = [un("PT2_0", [128, 2, 384], 73), un("PT2_1", [128, 2, 384], 25)]
    ropeX = un("ropeX", [128, 2, S], 25)
    ropeT = un("ropeT", [128, 2, S], 72)
    ropeU = un("ropeU", [128, 2, S], 74)
    cosT = un("cosT", [128, S], 29)
    sinT = un("sinT", [128, S], 30)
    biasB = un("biasB", [128, 16, S], 32)
    CQ = un("CQ", [128, 4, S], 64)
    CSQ = un("CSQ", [128, 4, S], 68)
    qnT = un("qnT", [128, 8, S], 48)
    qrT = un("qrT", [128, 8, S], 56)
    knT = un("knT", [128, 8, S], 32)
    vb = un("vb", [128, 2, 1024], 40)
    YROW = un("YROW", [128, 2, D], 0)

    bank = [nc.alloc_psum_tensor(f"bank{i}", [128, 512], F32) for i in range(8)]
    region = [(bank[0], bank[1]), (bank[2], bank[3])]

    toepA = nc.dram_tensor("toepA", [16, 128, 384], F32, kind="Internal").ap()
    toepB = nc.dram_tensor("toepB", [16, 128, 384], F32, kind="Internal").ap()

    L_x = [Landing(sem(f"l_x{i}")) for i in range(2)]
    L_c = Landing(sem("l_c"))
    L_rows = Landing(sem("l_rows"))
    L_w2 = Landing(sem("l_w2"))
    x_rows = A["x"][0].rearrange("(t p) d -> t p d", p=128)
    x_in = [L_x[t].start(sp, XROW[:, t, :], x_rows[t]) for t in range(2)]
    L_c.start(act, ident[:, :], A["c_ident"])
    L_c.start(act, ones[:, :], A["c_ones"])
    L_c.start(act, OH[:, :], A["c_onehot"])
    L_c.start(act, rela[0:32, :], A["rel_bias"])
    L_c.start(act, relb[0:32, :], A["rel_bias_2"])
    L_c.start(act, causal[:, :], A["c_causal"])
    sk = A["swa_sinks_2"][0]
    c_in = L_c.start(act, sinkr[:, :], bass.AP(tensor=sk.tensor, offset=sk.offset, ap=[[0, 128], [1, 16]]))
    r = 0
    for name in ("mix_norm_g", "ffn_norm_g", "final_norm_g", "attn_norm_g_2", "mlp_norm_g_2",
                 "final_norm_g_2", "c_2", "mla_q_norm_g_2", "mla_kv_norm_g_2"):
        a = A[name]
        v = a if len(a.shape) == 1 else a[0]
        n = v.shape[0] // 128
        L_rows.start(act, rowsA[r:r + n, :], v.rearrange("(r c) -> r c", c=128))
        r += n
    L_rows.start(act, rowsB[:, :], A["b_mod_2"][0].rearrange("(r c) -> r c", c=128))
    L_rows.start(act, rowsP[0:32, :], A["cmp_pos_k"][0])
    rows_in = L_rows.start(act, rowsP[32:64, :], A["cmp_pos_v"][0])
    L_w2.start(act, w2[:, 0, :, :], A["cmp_w2_k"][0].rearrange("(k p) n -> p k n", p=128))
    w2_in = L_w2.start(act, w2[:, 1, :, :], A["cmp_w2_v"][0].rearrange("(k p) n -> p k n", p=128))

    eps_set = dve(lambda e: e.memset(epsc[:, :], EPS))
    relm = [dve(lambda e, t=t: e.memset(t[32:33, :], NEG)) for t in (rela, relb)]

    L_raw = [Landing(sem(f"l_raw{i}")) for i in range(NRAW)]
    raw_free = [None] * NRAW
    n_loads = [0]

    def load(view, src):
        slot = n_loads[0] % NRAW
        n_loads[0] += 1
        tok = L_raw[slot].start(sp, view(RAW[slot]), src, raw_free[slot])
        return RAW[slot], tok, slot

    slabs, chunks = [], []

    def slab(w, row0, kts, c0, nc_, groups, rhs, evac, per=None):
        per = per or max(1, min(8, 2048 // nc_))
        s = dict(w=w, row0=row0, nc=nc_, groups=groups, rhs=rhs, evac=evac, n=len(slabs), per=per)
        slabs.append(s)
        s["first"] = len(chunks)
        for k in range(0, kts, per):
            chunks.append((s, k, min(per, kts - k), k + per >= kts))

    def feat(c, b, off):
        return ("f", lambda v, k: v[:, k, c:c + 128], b, off, S)

    def tokh(c, n, half, b, off):
        return ("t%d" % half, lambda v, k: v[:, k, c:c + n], b, off, n)

    FEAT4 = [feat(128 * i, i // 2, 256 * (i % 2)) for i in range(4)]
    TOK512 = [tokh(0, 512, 0, 0, 0), tokh(0, 512, 1, 1, 0)]

    split_tok = {}
    chunk_done = {}

    def split(n):
        if n >= len(chunks) or n in split_tok:
            return
        s, k, nk, _ = chunks[n]
        ncol = s["nc"]
        src = s["w"][(s["row0"] + k) * 128:(s["row0"] + k + nk) * 128, :]
        src = src[:, s["c0"]:s["c0"] + ncol] if "c0" in s else src
        src = src.rearrange("(k p) n -> p k n", p=128)
        m = nk * ncol
        raw, landed, slot = load(lambda t: t[:, 0:m].rearrange("p (k n) -> p k n", k=nk), src)
        hi, lo = WHI[n % 2], WLO[n % 2]
        free = chunk_done.get(n - 2)
        t_hi = act(lambda e: e.activation(hi[:, 0:m], raw[:, 0:m], ACT.Copy), landed, free)
        t_lo = dve(lambda e: e.tensor_tensor(lo[:, 0:m], raw[:, 0:m], hi[:, 0:m].bitcast(F32), ALU.subtract),
                   landed, free, t_hi)
        raw_free[slot] = [t_hi, t_lo]
        split_tok[n] = [t_hi, t_lo]

    region_free = [None, None]
    later = []

    def pe_later():
        todo = later[:]
        later.clear()
        for f in todo:
            f()

    cursor = [0]
    fillers = []

    def run_slab(s):
        while True:
            n = cursor[0]
            cursor[0] += 1
            assert chunks[n][0] is s
            split(n)
            split(n + 1)
            _, k, nk, last = chunks[n]
            reg = region[s["n"] % 2]
            view = [t[:, 0:nk * s["nc"]].rearrange("p (k n) -> p k n", k=nk) for t in (WHI[n % 2], WLO[n % 2])]
            waits = [split_tok[n], region_free[s["n"] % 2] if k == 0 else None]
            opened = set()
            todo = []
            for kk in range(nk):
                xh, xl, x_tok = s["rhs"](k + kk)
                for g in s["groups"]:
                    kind, cut, b, off, w = g
                    start = k + kk == 0 and b not in opened
                    opened.add(b)
                    for i, (wv, xv) in enumerate(((view[0], xh), (view[0], xl), (view[1], xh))):
                        wa = cut(wv, kk)
                        if kind == "f":
                            lhs, rhs = wa, xv
                        else:
                            h = 128 * int(kind[1])
                            lhs, rhs = xv[:, h:h + 128], wa
                        o = reg[b][:, off:off + w]
                        fin = last and kk == nk - 1 and i == 2
                        todo.append((o, lhs, rhs, start and i == 0, fin, x_tok))
            for j, (o, lhs, rhs, st, fin, x_tok) in enumerate(todo):
                end = j == len(todo) - 1
                tk = pe(lambda e, o=o, lhs=lhs, rhs=rhs, st=st, fin=fin: e.matmul(
                    o, lhs, rhs, start=st, stop=fin, skip_group_check=True),
                    waits if j == 0 else None, x_tok, inc=end)
            chunk_done[n] = tk
            pe_later()
            split(n + 2)
            if last:
                region_free[s["n"] % 2] = s["evac"](reg, tk)
            if fillers:
                f = fillers.pop(0)
                if f is not None:
                    f()
            if last:
                return

    ss_free = [None]
    sq_free = [None, None]
    sq_n = [0]
    ss = bank[6][:, 0:S]

    def ssq_add(m0, x_tok, first, last, now=False, src=None, count=4):
        b = sq_n[0] % 2
        sq_n[0] += 1
        t_sq = act(lambda e: e.activation(SQ[b][:, 0:count, :], (src or xT)[:, m0:m0 + count, :], ACT.Square),
                   x_tok, sq_free[b])
        box = {}

        def go():
            for i in range(count):
                tk = pe(lambda e, i=i: e.matmul(ss, ones[:, :], SQ[b][:, i, :], start=first and i == 0,
                                                stop=last and i == count - 1, skip_group_check=True),
                        [t_sq, c_in, ss_free[0] if first else None] if i == 0 else None, inc=i == count - 1)
            sq_free[b] = tk
            box["tok"] = tk
        sq_free[b] = None
        if now:
            go()
        else:
            later.append(go)
        return box

    rstd_free = [None]

    def rstd_of(box, n):
        t_std = act(lambda e: e.activation(std[:, :], ss, ACT.Sqrt, bias=epsc[:, 0:1], scale=1.0 / n),
                    box["tok"], eps_set, rstd_free[0])
        ss_free[0] = t_std
        return dve(lambda e: e.reciprocal(rstd[:, :], std[:, :]), t_std, rstd_free[0])

    ht_free = [None, None]

    def norm_apply(gcol, g_tok, t_rstd, free, shcol=None):
        toks = []
        for b in range(4):
            ht = HT[b % 2]
            t = None
            for i in range(4):
                m = 4 * b + i
                t = dve(lambda e, m=m, i=i, ht=ht: e.scalar_tensor_tensor(
                    ht[:, i, :], xT[:, m, :], gcol[:, m:m + 1], rstd[:, :], ALU.mult, ALU.mult),
                    t_rstd, g_tok, ht_free[b % 2])
            sl = slice(4 * b, 4 * b + 4)
            if shcol is None:
                t_hi = act(lambda e, ht=ht, sl=sl: e.activation(HI[:, sl, :], ht[:, :, :], ACT.Copy), t, free)
                t_lo = dve(lambda e, ht=ht, sl=sl: e.tensor_tensor(
                    LO[:, sl, :], ht[:, :, :], HI[:, sl, :].bitcast(F32), ALU.subtract), t, t_hi, free)
            else:
                for i in range(4):
                    m = 4 * b + i
                    t_hi = act(lambda e, ht=ht, m=m, i=i: e.activation(
                        HI[:, m, :], ht[:, i, :], ACT.Identity, bias=shcol[:, m:m + 1]), t, free)
                for i in range(4):
                    m = 4 * b + i
                    t_lo = dve(lambda e, ht=ht, m=m, i=i: e.scalar_tensor_tensor(
                        LO[:, m, :], ht[:, i, :], shcol[:, m:m + 1], HI[:, m, :].bitcast(F32),
                        ALU.add, ALU.subtract), t, t_hi, free)
            ht_free[b % 2] = [t_hi, t_lo]
            toks.append([t_hi, t_lo])
        rstd_free[0] = t
        return toks

    def rhs_of(hi, lo, toks, base=0):
        return lambda k: (hi[:, base + k, :], lo[:, base + k, :], toks["t"][(base + k) // 4])

    t_rowA = pe(lambda e: e.transpose(bank[4][:, 0:116], rowsA[:, :], ident[0:116, 0:116]), c_in, rows_in)
    t_rowB = pe(lambda e: e.transpose(bank[4][:, 128:224], rowsB[:, :], ident[0:96, 0:96]))
    t_rowP = pe(lambda e: e.transpose(bank[4][:, 256:320], rowsP[:, :], ident[0:64, 0:64]))
    t_cols = act(lambda e: e.activation(cols[:, :], bank[4][:, 0:116], ACT.Copy), t_rowP)
    t_bmod = act(lambda e: e.activation(bmod[:, :], bank[4][:, 128:224], ACT.Copy))
    t_posT = act(lambda e: e.activation(posT[:, :], bank[4][:, 256:320], ACT.Copy))
    t_cact = act(lambda e: e.activation(cact[:, :], cols[:, 96:112], ACT.Silu), t_cols)
    g_mix, g_ffn, g_fin, g_att2, g_mlp2, g_fin2 = [cols[:, 16 * i:16 * i + 16] for i in range(6)]
    gq, gkv = cols[:, 112:115], cols[:, 115:116]

    pe(lambda e: e.matmul(bank[5][0:16, 0:384], rela[:, :], OH[:, 512:896], start=True, stop=True),
       c_in, relm, inc=False)
    t_ra = pe(lambda e: e.matmul(bank[6][0:16, 0:384], relb[:, :], OH[:, 896:1280], start=True, stop=True))
    t_R16a = act(lambda e: e.activation(R16a[:, :], bank[5][0:16, 0:384], ACT.Copy), t_ra)
    t_R16b = act(lambda e: e.activation(R16b[:, :], bank[6][0:16, 0:384], ACT.Copy))
    for b in range(2):
        for c in range(15):
            o = 255 + 128 * b - 16 * c - 31
            n = 16 * (15 * b + c)
            t_cb = pe(lambda e, o=o, n=n: e.matmul(bank[7][:, n:n + 16], OH[:, o:o + 128], rela[:, :],
                                                   start=n == 0, stop=True, skip_group_check=True),
                      inc=(b, c) == (1, 14))
    t_cmpb = None
    for b in range(2):
        t_cmpb = act(lambda e, b=b: e.activation(
            cmpb[:, 16 * b:16 * b + 16, :],
            bank[7][:, 240 * b:240 * b + 240].rearrange("p (c h) -> p h c", c=15), ACT.Copy), t_cb)

    L_tA, L_tB = Landing(sem("l_tA")), Landing(sem("l_tB"))
    L_bA, L_bB = Landing(sem("l_bA")), Landing(sem("l_bB"))

    def repeated(t):
        a = t[:, :]
        return bass.AP(tensor=a.tensor, offset=a.offset, ap=[list(a.ap[0]), [0, 128], [1, 384]])

    def toeplitz(t):
        return bass.AP(tensor=t.tensor, offset=t.offset + 127, ap=[[383, 128], [128 * 384, 16], [1, 256]])

    t_tA = L_tA.start(pool, toepA, repeated(R16a), t_R16a)
    t_tB = L_tB.start(pool, toepB, repeated(R16b), t_R16b)
    biasA_in = L_bA.start(pool, biasA[:, :, :], toeplitz(toepA), t_tA)

    ss_free[0] = t_R16b
    x_free = [None] * 4
    x_new = []
    for m0 in range(0, KT, 4):
        tt = []
        for t in range(2):
            i = (m0 // 4 * 2 + t) % 4
            for j in range(4):
                m = m0 + j
                tp = pe(lambda e, i=i, j=j, m=m, t=t: e.transpose(
                    bank[i][:, 128 * j:128 * j + 128], XROW[:, t, 128 * m:128 * m + 128], ident[:, :]),
                    x_in[t], x_free[i], c_in, inc=j == 3)
            eng = act if t == 0 else dve
            dst = xT[:, m0:m0 + 4, 128 * t:128 * t + 128]
            src = bank[i][:, :].rearrange("p (m s) -> p m s", m=4)
            if t == 0:
                tc = act(lambda e, dst=dst, src=src: e.activation(dst, src, ACT.Copy), tp)
            else:
                tc = dve(lambda e, dst=dst, src=src: e.tensor_copy(dst, src), tp)
            x_free[i] = tc
            tt.append(tc)
        x_new.append(tt)
    region_free[0] = [x_free[0], x_free[1]]
    region_free[1] = [x_free[2], x_free[3]]
    for i in range(4):
        box = ssq_add(4 * i, x_new[i], i == 0, i == 3, now=True)
    xrow_done = x_new[3]

    mod_tok = [None] * 6
    acc_free = [None]

    def gemv(p, k):
        def go():
            raw, landed, slot = load(lambda t: t[:, :],
                                     A["w_mod_2"][0][k * 128:(k + 1) * 128, p * 2048:(p + 1) * 2048])
            if k == 0:
                t = dve(lambda e: e.tensor_scalar(ACC[:, :], raw[:, :], cact[:, 0:1], None, ALU.mult),
                        landed, t_cact, acc_free[0])
            else:
                t = dve(lambda e: e.scalar_tensor_tensor(ACC[:, :], raw[:, :], cact[:, k:k + 1], ACC[:, :],
                                                         ALU.mult, ALU.add), landed, acc_tok[0])
            acc_tok[0] = t
            raw_free[slot] = t
            if k == 15:
                def reduce():
                    for j in range(16):
                        tk = pe(lambda e, j=j: e.matmul(
                            bank[7][:, j:j + 1], ACC[:, 128 * j:128 * j + 128], ones[:, 0:1],
                            start=j == 0, stop=True, skip_group_check=True),
                            [t, mod_tok[p - 1] if p else t_cmpb] if j == 0 else None, inc=j == 15)
                    acc_free[0] = tk
                    sl = slice(16 * p, 16 * p + 16)
                    mod_tok[p] = dve(lambda e: e.tensor_tensor(mod[:, sl], bank[7][:, 0:16], bmod[:, sl], ALU.add),
                                     tk, t_bmod)
                later.append(reduce)
        return go

    acc_tok = [None]
    gemvs = []
    for p in range(6):
        gemvs += [gemv(p, k) for k in range(16)] + [None, None]

    def declare(w, row0, kts, c0, ncol, groups, rhs, evac, per=None):
        slab(w, row0, kts, c0, ncol, groups, rhs, evac, per)
        slabs[-1]["c0"] = c0
        return slabs[-1]

    h1 = {}
    rhs1 = rhs_of(HI, LO, h1)
    tk1 = {}

    def to_feat(dst, name, scale=None, tiles=4, free=None):
        def evac(reg, done):
            t = None
            for b in range(tiles // 2):
                src = reg[b][:, :].rearrange("p (m s) -> p m s", m=2)
                d = dst[:, 2 * b:2 * b + 2, :]
                t = act(lambda e, d=d, src=src: e.activation(d, src, ACT.Copy, scale=1.0 if scale is None else scale),
                        done, free)
            tk1[name] = t
            return t
        return evac

    def to_tok(dst, name, free=None):
        def evac(reg, done):
            t = None
            for b in range(2):
                t = act(lambda e, b=b: e.activation(dst[:, b, :], reg[b][:, :], ACT.Copy), done, free)
            tk1[name] = t
            return t
        return evac

    def gate_evac(reg, done):
        t = None
        for b in range(2):
            for br in range(3):
                o = gates[:, br, :, b] if br == 0 else gates[:, 1, :, 2 * (1 - b) + br - 1]
                src = reg[b][:, 16 * br:16 * br + 16]
                t = act(lambda e, o=o, src=src: e.activation(o, src, ACT.Sigmoid), done)
        tk1["gates"] = t
        return t

    W = A["nsa_w_in"][0]
    nsa = [
        declare(W, 0, KT, 2048, 512, FEAT4, rhs1, to_feat(kcT, "kc")),
        declare(W, 0, KT, 2560, 512, FEAT4, rhs1, to_feat(vcT, "vc")),
        declare(W, 0, KT, 3072, 512, FEAT4, rhs1, to_feat(ksT, "ks", free=[t_R16a, t_R16b, t_cmpb, t_tA, t_tB, t_posT])),
        declare(W, 0, KT, 3584, 512, TOK512, rhs1, to_tok(vs, "vs", free=[t_tA, t_tB])),
        declare(W, 0, KT, 4096, 512, FEAT4, rhs1, to_feat(kwT, "kw", free=[t_tA, t_tB])),
        declare(W, 0, KT, 4608, 512, TOK512, rhs1, to_tok(vw, "vw")),
        declare(W, 0, KT, 5120, 48, [tokh(0, 48, 0, 0, 0), tokh(0, 48, 1, 1, 0)], rhs1, gate_evac),
    ]
    for i in range(4):
        nsa.append(declare(W, 0, KT, 512 * i, 512, FEAT4, rhs1,
                           to_feat(qT[:, 4 * i:4 * i + 4, :], f"q{i}", scale=128.0 ** -0.5, free=xrow_done)))

    def residual(xbox, gcol=None, g_tok=None, ssq=True):
        def at_tile(m0, first, last):
            def evac(reg, done):
                t = None
                for b in range(2):
                    src = reg[b][:, :].rearrange("p (m s) -> p m s", m=2)
                    x = xT[:, m0 + 2 * b:m0 + 2 * b + 2, :]
                    if gcol is None:
                        t = dve(lambda e, x=x, src=src: e.tensor_tensor(x, src, x, ALU.add), done, xbox.get("free"))
                    else:
                        for i in range(2):
                            m = m0 + 2 * b + i
                            t = dve(lambda e, m=m, b=b, i=i: e.scalar_tensor_tensor(
                                xT[:, m, :], reg[b][:, 256 * i:256 * i + 256], gcol[:, m:m + 1], xT[:, m, :],
                                ALU.mult, ALU.add), done, xbox.get("free"), mod_tok[g_tok])
                if ssq:
                    xbox["box"] = ssq_add(m0, t, first, last)
                xbox["x"] = t
                return t
            return evac
        return at_tile

    xb1, xb2, xb3, xb4 = {}, {}, {}, {}

    def declare_out(w, row0, kts, rhs, maker):
        return [declare(w, row0, kts, 512 * i, 512, FEAT4, rhs, maker(4 * i, i == 0, i == 3)) for i in range(4)]

    h2 = {}
    out1 = declare_out(A["nsa_w_out"][0], 0, KT, rhs_of(HI, LO, h2), residual(xb1))

    hid = {}
    sa_n, sa_tok = [0], [None, None]
    ht2_n = [0]

    def hid_split(ht, b, base, t_h):
        t_hi = act(lambda e: e.activation(HIDH[:, base:base + 4, :], ht[:, :, :], ACT.Copy), t_h, hid["free"])
        t_lo = dve(lambda e: e.tensor_tensor(HIDL[:, base:base + 4, :], ht[:, :, :],
                                             HIDH[:, base:base + 4, :].bitcast(F32), ALU.subtract),
                   t_h, t_hi, hid["free"])
        ht_free[b] = [t_hi, t_lo]
        hid["t"][base // 4] = [t_hi, t_lo]

    def silu_evac(reg, done):
        i = sa_n[0] % 2
        t = None
        for b in range(2):
            t = act(lambda e, b=b: e.activation(SA[i][:, 2 * b:2 * b + 2, :],
                                                reg[b][:, :].rearrange("p (m s) -> p m s", m=2), ACT.Silu),
                    done, sa_tok[i], hid.get("ufree"))
        hid["sa"] = t
        return t

    def glu_evac(base):
        def evac(reg, done):
            i = sa_n[0] % 2
            sa_n[0] += 1
            t = None
            for b in range(2):
                t = dve(lambda e, b=b: e.tensor_tensor(
                    HT[i][:, 2 * b:2 * b + 2, :], reg[b][:, :].rearrange("p (m s) -> p m s", m=2),
                    SA[i][:, 2 * b:2 * b + 2, :], ALU.mult), done, hid["sa"], ht_free[i])
            sa_tok[i] = t
            hid_split(HT[i], i, base, t)
            return t
        return evac

    def relu2_evac(base):
        def evac(reg, done):
            i = sa_n[0] % 2
            sa_n[0] += 1
            t = None
            for b in range(2):
                t = act(lambda e, b=b: e.activation(SA[i][:, 2 * b:2 * b + 2, :],
                                                    reg[b][:, :].rearrange("p (m s) -> p m s", m=2), ACT.Relu),
                        done, sa_tok[i])
            t_h = dve(lambda e: e.tensor_tensor(HT[i][:, :, :], SA[i][:, :, :], SA[i][:, :, :], ALU.mult),
                      t, ht_free[i])
            sa_tok[i] = t_h
            hid_split(HT[i], i, base, t_h)
            return t
        return evac

    h3 = {}
    rhs3 = rhs_of(HI, LO, h3)
    ffn1 = []
    W1, W2 = A["ffn_w_in"][0], A["ffn_w_out"][0]
    parts1 = [(0, 6), (6, 5)]
    hidv = {"t": [None] * 6}
    hid["t"] = [None] * 6
    for pi, (s0, n) in enumerate(parts1):
        up = []
        for j in range(n):
            c = 512 * (s0 + j)
            up.append(declare(W1, 0, KT, c, 512, FEAT4, rhs3, silu_evac))
            up.append(declare(W1, 0, KT, FF1 + c, 512, FEAT4, rhs3, glu_evac(4 * j)))
        down = declare_out(W2, 4 * s0, 4 * n, rhs_of(HIDH, HIDL, hid),
                           residual(xb2, ssq=pi == len(parts1) - 1))
        ffn1.append((up, down))

    h4 = {}
    rhs4 = rhs_of(HI, LO, h4)
    W = A["w_in_2"][0]

    att2 = {}

    def ka_evac(reg, done):
        t = None
        for kv in range(2):
            for par in range(2):
                t = act(lambda e, kv=kv, par=par: e.activation(
                    Kpad[64 * par:64 * par + 64, kv, par, :], reg[0][64 * kv:64 * kv + 64, 0:S], ACT.Copy),
                    done, att2["pad0"])
                for half in range(2):
                    src = reg[0][:, 256 + 64 * kv:320 + 64 * kv] if half == 0 else reg[1][:, 64 * kv:64 * kv + 64]
                    t = act(lambda e, kv=kv, par=par, half=half, src=src: e.activation(
                        Vpad2[:, kv, par, half, 64 * par:64 * par + 64], src, ACT.Copy), done, att2["pad0"])
        att2["kv"] = t
        return t

    def cq_evac(reg, done):
        t = None
        for m in range(3):
            t = act(lambda e, m=m: e.activation(CQ[:, m, :], reg[m // 2][:, 256 * (m % 2):256 * (m % 2) + 256],
                                                ACT.Copy), done, att2["free"])
        att2["cq"] = t
        return t

    def rope_apply(src, n, dst, done, free):
        for q in (2, 3):
            p = q ^ 1
            t = act(lambda e, q=q, p=p: e.activation(
                ropeX[32 * q:32 * q + 32, 0:n, :], src[32 * p:32 * p + 32, :].rearrange("p (h s) -> p h s", h=n), ACT.Copy),
                done, att2.get("ropefree"), att2["free"])
        t1 = t2 = None
        for h in range(n):
            t1 = dve(lambda e, h=h: e.tensor_tensor(ropeT[64:128, h, :], src[64:128, S * h:S * h + S], cosT[64:128, :], ALU.mult),
                     done, t, att2["rope_in"], att2.get("ropefree"))
            t2 = dve(lambda e, h=h: e.tensor_tensor(ropeU[64:128, h, :], ropeX[64:128, h, :], sinT[64:128, :], ALU.mult),
                     t, att2["rope_in"], att2.get("ropefree"))
        t3 = dve(lambda e: e.tensor_tensor(dst3(dst), ropeT[64:128, 0:n, :], ropeU[64:128, 0:n, :], ALU.add), t1, t2, free)
        att2["ropefree"] = t3
        return t1, t3

    def dst3(d):
        return d if len(d.shape) == 3 else d.rearrange("p (h s) -> p h s", h=1)

    def ckv_evac(reg, done):
        t = act(lambda e: e.activation(CQ[:, 3, :], reg[0][:, 0:S], ACT.Copy), done, att2["free"])
        att2["ckv"] = t
        t1, t3 = rope_apply(reg[0][:, 256:512], 1, krp[64:128, :], [done, t], att2["pad0"])
        att2["kr"] = t3
        return [t, t1]

    inp2 = [declare(W, 0, KT, 512 * i, 512, FEAT4, rhs4,
                    to_feat(qaT[:, 4 * i:4 * i + 4, :], f"qa{i}", scale=0.125)) for i in range(2)]
    inp2 += [
        declare(W, 0, KT, 1664, 192, [feat(0, 0, 0), feat(64, 0, 256)], rhs4, ckv_evac),
        declare(W, 0, KT, 1280, 384, [feat(0, 0, 0), feat(128, 0, 256), feat(256, 1, 0)], rhs4, cq_evac, per=4),
        declare(W, 0, KT, 1024, 256, [feat(0, 0, 0), tokh(128, 128, 0, 0, 256), tokh(128, 128, 1, 1, 0)], rhs4, ka_evac),
    ]
    hq = {}

    def uq_evac(j):
        def evac(reg, done):
            ta = act(lambda e: e.activation(qnT[:, 2 * j:2 * j + 2, :],
                                            reg[0][:, :].rearrange("p (m s) -> p m s", m=2), ACT.Copy),
                     done, att2["free"])
            t1, t3 = rope_apply(reg[1][:, :], 2, qrT[64:128, 2 * j:2 * j + 2, :], done, att2["pad0"])
            tk1[f"qm{j}"] = [ta, t3]
            return [ta, t1]
        return evac

    uq = [declare(A["w_uq_2"][0], 0, 3, 384 * j, 384,
                  [feat(0, 0, 0), feat(192, 0, 256), feat(64, 1, 0), feat(256, 1, 256)],
                  lambda k: (CQH[:, k, :], CQL[:, k, :], hq["q"]), uq_evac(j), per=3) for j in range(4)]

    def ukv_evac(j):
        def evac(reg, done):
            ta = act(lambda e: e.activation(knT[:, 2 * j:2 * j + 2, :],
                                            reg[0][:, :].rearrange("p (m s) -> p m s", m=2), ACT.Copy),
                     done, att2["swa_done"])
            tb = act(lambda e: e.activation(vb[:, :, 256 * j:256 * j + 256],
                                            reg[1][:, :].rearrange("p (t c) -> p t c", t=2), ACT.Copy),
                     done, att2["swa_done"])
            tk1[f"km{j}"] = tb
            return tb
        return evac

    def ukv_v(half):
        return ("t%d" % half, lambda v, k: v[:, k, :].rearrange("p (h c) -> p h c", h=2)[:, :, 128:256],
                1, 256 * half, 256)

    ukv = [declare(A["w_ukv_2"][0], 0, 1, 512 * j, 512,
                   [feat(0, 0, 0), feat(256, 0, 256), ukv_v(0), ukv_v(1)],
                   lambda k: (CQH[:, 3, :], CQL[:, 3, :], hq["kv"]), ukv_evac(j), per=1) for j in range(4)]

    h5, h6 = {}, {}
    out2 = declare_out(A["w_out_2"][0], 0, KT, rhs_of(HI, LO, h5), residual(xb3, mod[:, 32:48], 2))
    rhs6 = rhs_of(HI, LO, h6)
    ffn2 = []
    W1, W2 = A["w_ff1_2"][0], A["w_ff2_2"][0]
    parts2 = [(0, 6), (6, 5), (11, 5)]
    for pi, (s0, n) in enumerate(parts2):
        up = [declare(W1, 0, KT, 512 * (s0 + j), 512, FEAT4, rhs6, relu2_evac(4 * j)) for j in range(n)]
        down = declare_out(W2, 4 * s0, 4 * n, rhs_of(HIDH, HIDL, hid),
                           residual(xb4, mod[:, 80:96], 5, ssq=pi == len(parts2) - 1))
        ffn2.append((up, down))

    def attention(units, SPb, PTb, free):
        st = [dict() for _ in units]
        bfree = {"S": [free, free], "PT": free, "O": [free, free], "SP": [free] * 3, "PTS": [free, free]}

        def scores(i):
            u, p = units[i], i % 2
            for br, b in enumerate(u["br"]):
                for blk, bk, o, n in ((0, bank[p], 128 * br, 128), (1, bank[2 + p], 256 * br, 256)):
                    pr = b["qk"](blk, n)
                    for j, (l, r_) in enumerate(pr):
                        tk = pe(lambda e, bk=bk, o=o, n=n, l=l, r_=r_, j=j, pr=pr: e.matmul(
                            bk[:, o:o + n], l, r_, start=j == 0, stop=j == len(pr) - 1, skip_group_check=True),
                            [bfree["S"][p], u["ready"]] if (br, blk, j) == (0, 0, 0) else None,
                            inc=(br, blk, j) == (len(u["br"]) - 1, 1, len(pr) - 1))
            st[i]["S"] = tk

        def softmax1(i):
            u, p, q = units[i], i % 2, i % 3
            nb = len(u["br"])
            stt = stat[:, q, :, :]
            ts = []
            for br, b in enumerate(u["br"]):
                for blk in (1, 0):
                    n = 128 * (blk + 1)
                    j = br if blk else 2 + br
                    o = 256 * br if blk else 512 + 128 * br
                    src = bank[2 + p][:, 256 * br:256 * br + 256] if blk else bank[p][:, 128 * br:128 * br + 128]
                    bias = b["bias"] if blk else b["bias"][:, 128:256]
                    least = b["least"](j) if b["least"] else -3.0e38
                    ts.append(dve(lambda e, n=n, j=j, o=o, src=src, bias=bias, b=b, least=least: e.tensor_tensor_reduce(
                        out=SPb[q][:, o:o + n], in0=src, in1=bias, scale=b["scale"], scalar=least,
                        op0=ALU.add, op1=ALU.max, accum_out=stt[:, 0, j:j + 1]),
                        st[i]["S"], bfree["SP"][q], u["bias_tok"]))
            bfree["S"][p] = ts[-1]
            t = dve(lambda e: e.tensor_scalar(stt[:, 1, :], stt[:, 0, :], -1.0, None, ALU.mult), ts) if nb == 2 else \
                dve(lambda e: e.tensor_scalar(stt[:, 1, 0:3:2], stt[:, 0, 0:3:2], -1.0, None, ALU.mult), ts)
            st[i]["nm"] = t
            if u["sink"] is not None:
                st[i]["sk"] = dve(lambda e: e.tensor_tensor(stt[:, 4, :], stt[:, 1, :], u["sink"], ALU.add), t)

        def softmax2(i):
            u, q = units[i], i % 3
            stt = stat[:, q, :, :]
            t = None
            for br in range(len(u["br"])):
                for blk in (1, 0):
                    n = 128 * (blk + 1)
                    j = br if blk else 2 + br
                    o = 256 * br if blk else 512 + 128 * br
                    t = act(lambda e, n=n, j=j, o=o: e.activation(
                        SPb[q][:, o:o + n], SPb[q][:, o:o + n], ACT.Exp, bias=stt[:, 1, j:j + 1],
                        accum_out=stt[:, 2, j:j + 1]), st[i]["nm"])
            if u["sink"] is not None:
                t = act(lambda e: e.activation(stt[:, 5, :], stt[:, 4, :], ACT.Exp), st[i]["sk"])
            st[i]["exp"] = t

        def softmax3(i):
            u, q = units[i], i % 3
            stt = stat[:, q, :, :]
            step = slice(0, 4) if len(u["br"]) == 2 else slice(0, 3, 2)
            t = st[i]["exp"]
            if u["sink"] is not None:
                t = dve(lambda e: e.tensor_tensor(stt[:, 2, :], stt[:, 2, :], stt[:, 5, :], ALU.add), t)
            t = dve(lambda e: e.reciprocal(stt[:, 3, step], stt[:, 2, step]), t)
            if u["gate"] is not None:
                t = dve(lambda e: e.tensor_tensor(stt[:, 3, :], stt[:, 3, :], u["gate"], ALU.mult), t, u["gate_tok"])
            ts = []
            for br in range(len(u["br"])):
                for blk in (1, 0):
                    n = 128 * (blk + 1)
                    j = br if blk else 2 + br
                    o = 256 * br if blk else 512 + 128 * br
                    ts.append(dve(lambda e, n=n, j=j, o=o: e.tensor_scalar(
                        SPb[q][:, o:o + n], SPb[q][:, o:o + n], stt[:, 3, j:j + 1], None, ALU.mult), t))
            st[i]["P"] = ts[-1]

        def turn(i):
            u, q = units[i], i % 3
            tk = None
            for br in range(len(u["br"])):
                bk = bank[4 + br]
                for n, (dst, src) in enumerate(((0, 512 + 128 * br), (128, 256 * br), (256, 256 * br + 128))):
                    tk = pe(lambda e, bk=bk, dst=dst, src=src: e.transpose(
                        bk[:, dst:dst + 128], SPb[q][:, src:src + 128], ident[:, :]),
                        [st[i]["P"], bfree["PT"]], inc=(br, n) == (len(u["br"]) - 1, 2))
            st[i]["T"] = tk
            bfree["SP"][q] = tk

        def evac_turn(i):
            u, p = units[i], i % 2
            t = None
            for br in range(len(u["br"])):
                t = act(lambda e, br=br: e.activation(PTb[p][:, br, :], bank[4 + br][:, 0:384], ACT.Copy),
                        st[i]["T"], bfree["PTS"][p])
            bfree["PT"] = t
            st[i]["PT"] = t

        def values(i):
            u, p = units[i], i % 2
            o = bank[6 + p]
            mm = []
            if u["more"] is not None:
                mm.append((o[:, 0:S], *u["more"]))
            for br, b in enumerate(u["br"]):
                mm.append((o[:, 0:S], b["v"](0), PTb[p][:, br, 0:256]))
                mm.append((o[:, 128:S], b["v"](1), PTb[p][:, br, 256:384]))
            for j, (dst, l, r_) in enumerate(mm):
                tk = pe(lambda e, dst=dst, l=l, r_=r_, j=j: e.matmul(
                    dst, l, r_, start=j == 0, stop=j == len(mm) - 1, skip_group_check=True),
                    [st[i]["PT"], bfree["O"][p], u["v_ready"]] if j == 0 else None, inc=j == len(mm) - 1)
            st[i]["O"] = tk
            bfree["PTS"][p] = tk

        def finish(i):
            u, p = units[i], i % 2
            k = u["dst"]
            t_hi = act(lambda e: e.activation(HI[:, k, :], bank[6 + p][:, 0:S], ACT.Copy), st[i]["O"], u["dst_free"])
            t_lo = dve(lambda e: e.tensor_tensor(LO[:, k, :], bank[6 + p][:, 0:S], HI[:, k, :].bitcast(F32),
                                                 ALU.subtract), t_hi, st[i]["O"], u["dst_free"])
            bfree["O"][p] = [t_hi, t_lo]
            st[i]["done"] = [t_hi, t_lo]

        n = len(units)
        for i in range(n + 3):
            if i < n:
                scores(i)
                softmax1(i)
                softmax2(i)
            if 0 <= i - 1 < n:
                softmax3(i - 1)
                turn(i - 1)
                evac_turn(i - 1)
            if 0 <= i - 2 < n:
                values(i - 2)
            if 0 <= i - 3 < n:
                finish(i - 3)
        done = [s["done"] for s in st]
        return done

    t_rstd = rstd_of(box, D)
    h1["t"] = norm_apply(g_mix, t_cols, t_rstd, None)
    h_done = {}

    gq_iter = iter(gemvs)

    def next_gemv():
        f = next(gq_iter, None)
        if f is not None:
            f()

    zfree = [None]
    cz = {}

    def make_z(kv):
        src = (kcT, vcT)[kv][:, :, :]
        ap0 = list(src.ap[0])
        win = bass.AP(tensor=src.tensor, offset=src.offset, ap=[ap0, [S, 4], [1, 32], [16, 15]])
        ps = posT[:, 32 * kv:32 * kv + 32]
        pos = bass.AP(tensor=ps.tensor, offset=ps.offset, ap=[list(ps.ap[0]), [0, 4], [1, 32], [0, 15]])
        z = Z[:, :, :]
        o = bass.AP(tensor=z.tensor, offset=z.offset, ap=[list(z.ap[0]), [15, 4], [60, 32], [1, 15]])
        t = None
        for g in range(4):
            def sub(a, g=g):
                return bass.AP(tensor=a.tensor, offset=a.offset + g * a.ap[1][0], ap=[list(a.ap[0])] + [list(d) for d in a.ap[2:]])
            t = dve(lambda e, o=sub(o), w=sub(win), q=sub(pos): e.tensor_tensor(o, w, q, ALU.add),
                    tk1["kc" if kv == 0 else "vc"], t_posT, zfree[0])
        cz["z"] = t

    def cmp_step(kv, i):
        def go():
            if i == 0:
                make_z(kv)
            w = A["cmp_w1_k" if kv == 0 else "cmp_w1_v"][0]
            src = w[i * 1024:(i + 1) * 1024, :].rearrange("(l p) n -> p l n", p=128)
            raw, landed, slot = load(lambda t: t[:, :].rearrange("p (l n) -> p l n", l=8), src)
            rv = raw[:, :].rearrange("p (l n) -> p l n", l=8)
            for l in range(8):
                for m in range(2):
                    tk = pe(lambda e, l=l, m=m: e.matmul(
                        bank[4][:, 60 * m:60 * m + 60], rv[:, l, 128 * m:128 * m + 128], Z[:, 8 * i + l, :],
                        start=(i, l, m) == (0, 0, 0), stop=(i, l) == (3, 7), skip_group_check=True),
                        [landed, cz["z"], cz.get("b4")] if (l, m) == (0, 0) else None, inc=(l, m) == (7, 1))
            raw_free[slot] = tk
            if i == 3:
                zfree[0] = tk
                t = act(lambda e: e.activation(hidT[:, kv, :, :], bank[4][:, 0:120].rearrange("p (m c) -> p m c", m=2),
                                               ACT.Gelu_apprx_tanh), tk)
                cz["b4"] = t
                cz[f"hid{kv}"] = t
        return go

    cmps = [cmp_step(0, i) for i in range(4)] + [cmp_step(1, i) for i in range(4)]
    cz["b4"] = [t_cols, t_bmod, t_posT]

    def fill(seq):
        fillers.extend(seq)

    for s in nsa:
        if s is nsa[3]:
            fill([c for c in cmps])
        run_slab(s)
    while fillers:
        fillers.pop(0)()
    nsa_done = chunk_done[cursor[0] - 1]

    for k in range(2):
        tk = pe(lambda e, k=k: e.matmul(bank[4][:, 128:188], w2[:, 0, k, :], hidT[:, 0, k, :], start=k == 0, stop=k == 1,
                                        skip_group_check=True), [w2_in, cz["hid0"], cz["hid1"]], inc=k == 1)
    t_kcc = act(lambda e: e.activation(kccT[:, :], bank[4][:, 128:188], ACT.Copy), tk)
    for g in range(4):
        for k in range(2):
            tk = pe(lambda e, g=g, k=k: e.matmul(bank[5][0:15, 128 * g:128 * g + 128], hidT[:, 1, k, 15 * g:15 * g + 15],
                                                 w2[:, 1, k, :], start=k == 0, stop=k == 1, skip_group_check=True),
                    t_R16a, inc=(g, k) == (3, 1))
    t_vz = dve(lambda e: e.memset(Vpad[:, :, :], 0.0))
    t_vp = None
    for g in range(4):
        for j in range(4):
            t_vp = dve(lambda e, g=g, j=j: e.tensor_copy(Vpad[32 * j:32 * j + 15, 4 * g + j, :],
                                                         bank[5][0:15, 128 * g:128 * g + 128]), tk, t_vz)

    for b in range(2):
        for h in range(16):
            n = 15 * (16 * b + h)
            g = h // 4
            tk = pe(lambda e, b=b, h=h, n=n, g=g: e.matmul(
                bank[7][:, n:n + 15], qT[:, h, 128 * b:128 * b + 128], kccT[:, 15 * g:15 * g + 15],
                start=n == 0, stop=True, skip_group_check=True),
                [t_kcc, tk1["q3"], t_cmpb, mod_tok], inc=(b, h) == (1, 15))
    tz = dve(lambda e: e.memset(Pc[:, :, :, :], 0.0), nsa_done, zfree[0])
    pcv = Pc[:, :, :, 0:15].rearrange("p b h c -> p (b h) c")
    t = dve(lambda e: e.tensor_tensor(pcv, bank[7][:, 0:480].rearrange("p (n c) -> p n c", c=15), cmpb[:, :, :], ALU.add),
            tk, tz, t_cmpb)
    t_c7 = t
    t = dve(lambda e: e.tensor_reduce(cst[:, 0, :], pcv, AX_X, ALU.max), t)
    t = dve(lambda e: e.tensor_scalar(cst[:, 1, :], cst[:, 0, :], -1e29, None, ALU.max), t)
    mx = cst[:, 1, :]

    def spread(a):
        return bass.AP(tensor=a.tensor, offset=a.offset, ap=[list(a.ap[0]), list(a.ap[1]), [0, 15]])

    t = dve(lambda e: e.tensor_tensor(pcv, pcv, spread(mx), ALU.subtract), t)
    t = act(lambda e: e.activation(pcv, pcv, ACT.Exp), t)
    t = dve(lambda e: e.tensor_reduce(cst[:, 2, :], pcv, AX_X, ALU.add), t)
    t = dve(lambda e: e.tensor_scalar(cst[:, 2, :], cst[:, 2, :], 1e-30, None, ALU.max), t)
    t = dve(lambda e: e.reciprocal(cst[:, 3, :], cst[:, 2, :]), t)
    t = dve(lambda e: e.tensor_tensor(cst[:, 3, :].rearrange("p (b h) -> p b h", b=2),
                                      cst[:, 3, :].rearrange("p (b h) -> p b h", b=2),
                                      gates[:, 0, :, 0:2].rearrange("p h b -> p b h"), ALU.mult), t, tk1["gates"])
    t = dve(lambda e: e.tensor_tensor(pcv, pcv, spread(cst[:, 3, :]), ALU.mult), t)
    for g in range(4):
        for b in range(2):
            i = (2 * g + b) // 4
            o = 128 * ((2 * g + b) % 4)
            tk = pe(lambda e, g=g, b=b, i=i, o=o: e.transpose(
                bank[4 + i][:, o:o + 128], Pc[:, b, 4 * g:4 * g + 4, :], ident[:, :]), t, t_vp, t_kcc, inc=(g, b) == (3, 1))
    t_pct = None
    for i in range(2):
        t_pct = act(lambda e, i=i: e.activation(
            PcT[:, 2 * i:2 * i + 2, :], bank[4 + i][:, :].rearrange("p (g s) -> p g s", g=2), ACT.Copy), tk)

    ready1 = [tk1[n] for n in ("ks", "kw", "q0", "q1", "q2", "q3")]
    units = []
    for h in range(16):
        g = h // 4

        def br(kT, v, h=h, g=g):
            return dict(qk=lambda blk, n: [(qT[:, h, 128 * blk:128 * blk + 128], kT[:, g, 0:n])],
                        bias=biasA[:, h, :], scale=1.0, least=None,
                        v=lambda k: v[:, k, 128 * g:128 * g + 128])
        units.append(dict(br=[br(ksT, vs), br(kwT, vw)], ready=ready1, v_ready=[tk1["vs"], tk1["vw"], t_vp, t_pct],
                          bias_tok=biasA_in, sink=None, gate=gates[:, 1, h, :], gate_tok=tk1["gates"],
                          more=(Vpad[:, h, :], PcT[:, g, :]), dst=h, dst_free=nsa_done))
    free1 = [region_free[0], region_free[1], t_pct, t_vp, t_c7, nsa_done, zfree[0], tk, ss_free[0]]
    done1 = attention(units, SP1, PT1, free1)

    def regroup(done):
        return [done[4 * i:4 * i + 4] for i in range(4)]

    h2["t"] = regroup(done1)
    region_free[0] = region_free[1] = done1
    ss_free[0] = [ss_free[0], done1]
    sq_free[0] = sq_free[1] = done1
    ht_free[0] = ht_free[1] = [ht_free[0], ht_free[1], done1]
    xb1["free"] = rstd_free[0]
    mod_guard = done1

    def with_gemv(pattern):
        i = 0
        while True:
            for p in pattern:
                yield p

    def run_all(ss_, gem=None):
        for s in ss_:
            if gem:
                n = len([c for c in chunks if c[0] is s])
                for _ in range(n):
                    fillers.append(next_gemv if next(gem) else None)
            run_slab(s)

    mod_tok_first = done1
    gem = with_gemv([1, 1, 0, 1])
    t_cmpb = [t_cmpb, done1]
    run_all(out1)
    out1_done = chunk_done[cursor[0] - 1]
    pe_later()

    t_rstd = rstd_of(xb1["box"], D)
    h3["t"] = norm_apply(g_ffn, t_cols, t_rstd, out1_done)
    hid["free"] = [out1_done, done1]
    hid["ufree"] = [out1_done, done1]
    xb2["free"] = rstd_free[0]
    for pi, (up, down) in enumerate(ffn1):
        run_all(up, gem)
        run_all(down, gem)
        hid["free"] = chunk_done[cursor[0] - 1]
    ffn1_done = chunk_done[cursor[0] - 1]
    pe_later()
    while True:
        f = next(gq_iter, 0)
        if f == 0:
            break
        if f is not None:
            f()
        pe_later()

    t_rstd = rstd_of(xb2["box"], D)
    boxes = None
    for b in range(4):
        for i in range(4):
            m = 4 * b + i
            t = dve(lambda e, m=m: e.scalar_tensor_tensor(xT[:, m, :], xT[:, m, :], g_fin[:, m:m + 1], rstd[:, :],
                                                          ALU.mult, ALU.mult), t_rstd, xb2["x"])
        boxes = ssq_add(4 * b, t, b == 0, b == 3, now=True)
    rstd_free[0] = t
    tg = [dve(lambda e, o=o, g=g, c=c: e.scalar_tensor_tensor(o[:, :], mod[:, c:c + 16], 1.0, g, ALU.add, ALU.mult),
              mod_tok, t_cols) for o, g, c in ((G1c, g_att2, 16), (G2c, g_mlp2, 64))]
    t_rstd = rstd_of(boxes, D)
    h4["t"] = norm_apply(G1c, tg, t_rstd, ffn1_done, shcol=mod[:, 0:16])

    att2["free"] = [ffn1_done, h4["t"], hid["t"], sq_free]
    L_rope = Landing(sem("l_rope"))
    L_rope.start(pool, cosT[:, :], A["c_cos"], att2["free"])
    att2["rope_in"] = L_rope.start(pool, sinT[:, :], A["c_sin"], att2["free"])
    biasB_in = L_bB.start(pool, biasB[:, :, :], toeplitz(toepB), t_tB, att2["free"])
    att2["pad0"] = [dve(lambda e, t_=t_: e.memset(t_, 0.0), att2["free"]) for t_ in
                    (Kpad[:, :, :, :], Vpad2[:, :, :, :, :], krp[0:64, :], qrT[0:64, :, :])]
    t_sk = None
    for j in range(4):
        t_sk = dve(lambda e, j=j: e.tensor_copy(SK[:, :, j], sinkr[:, j % 2:16:2]), c_in)

    run_all(inp2[:4])
    sq_t = act(lambda e: e.activation(CSQ[:, 3, :], CQ[:, 3, :], ACT.Square), att2["ckv"], att2["free"])
    sq_t2 = act(lambda e: e.activation(CSQ[:, 0:3, :], CQ[:, 0:3, :], ACT.Square), att2["cq"], att2["free"])

    def latent(ms, name, n, gcols):
        for j, m in enumerate(ms):
            tk = pe(lambda e, m=m, j=j: e.matmul(ss, ones[:, :], CSQ[:, m, :], start=j == 0, stop=j == len(ms) - 1,
                                                 skip_group_check=True), [sq_t, sq_t2, ss_free[0]], inc=j == len(ms) - 1)
        tr = rstd_of({"tok": tk}, n)
        for j, m in enumerate(ms):
            t = dve(lambda e, m=m, j=j: e.scalar_tensor_tensor(CQ[:, m, :], CQ[:, m, :], gcols[:, j:j + 1], rstd[:, :],
                                                               ALU.mult, ALU.mult), tr, sq_t, sq_t2)
        rstd_free[0] = t
        a, b = ms[0], ms[-1] + 1
        t_hi = act(lambda e: e.activation(CQH[:, a:b, :], CQ[:, a:b, :], ACT.Copy), t, att2["free"])
        t_lo = dve(lambda e: e.tensor_tensor(CQL[:, a:b, :], CQ[:, a:b, :], CQH[:, a:b, :].bitcast(F32), ALU.subtract),
                   t, t_hi, att2["free"])
        hq[name] = [t_hi, t_lo]

    later.append(lambda: latent([3], "kv", 128, gkv))
    later.append(lambda: latent([0, 1, 2], "q", 384, gq))
    run_all(inp2[4:])
    in2_done = chunk_done[cursor[0] - 1]
    pe_later()
    run_all(uq)

    units = []
    for i in range(8):
        def br(par, i=i):
            kv = i // 4
            return dict(qk=lambda blk, n: [(qaT[:, i, 128 * blk:128 * blk + 128], Kpad[:, kv, par, 0:n])],
                        bias=biasB[:, 2 * i + par, :], scale=1.0, least=lambda j: SK[:, i, j:j + 1],
                        v=lambda k: Vpad2[:, kv, par, k, :])
        units.append(dict(br=[br(0), br(1)], ready=[tk1["qa0"], tk1["qa1"], att2["kv"], att2["pad0"]], v_ready=att2["kv"],
                          bias_tok=[biasB_in, t_sk], sink=SK[:, i, :], gate=None, gate_tok=None, more=None, dst=i,
                          dst_free=in2_done))
    free2 = [region_free[0], region_free[1], in2_done, ss_free[0], hq["q"], hq["kv"], mod_tok, att2["ropefree"]]
    done2 = attention(units, SP2, PT2, free2)
    att2["swa_done"] = done2
    region_free[0] = region_free[1] = done2
    run_all(ukv)
    units = []
    for h in range(8):
        def br(h=h):
            return dict(qk=lambda blk, n: [(qnT[:, h, 128 * blk:128 * blk + 128], knT[:, h, 0:n]),
                                           (qrT[:, h, 128 * blk:128 * blk + 128], krp[:, 0:n])],
                        bias=causal[:, :], scale=192.0 ** -0.5, least=None,
                        v=lambda k: vb[:, k, 128 * h:128 * h + 128])
        units.append(dict(br=[br()], ready=[tk1[f"qm{h // 2}"], tk1[f"km{h // 2}"], att2["kr"]], v_ready=tk1[f"km{h // 2}"],
                          bias_tok=c_in, sink=None, gate=None, gate_tok=None, more=None, dst=8 + h, dst_free=in2_done))
    done3 = attention(units, SP2, PT2, [done2, region_free[0], region_free[1]])
    h5["t"] = regroup(done2 + done3)
    region_free[0] = region_free[1] = done3
    ss_free[0] = [ss_free[0], done2, done3]
    sq_free[0] = sq_free[1] = [done2, done3]
    ht_free[0] = ht_free[1] = [ht_free[0], ht_free[1], done2, done3]
    xb3["free"] = rstd_free[0]
    run_all(out2)
    out2_done = chunk_done[cursor[0] - 1]
    pe_later()

    t_rstd = rstd_of(xb3["box"], D)
    h6["t"] = norm_apply(G2c, tg, t_rstd, out2_done, shcol=mod[:, 48:64])
    hid["free"] = [out2_done, done3]
    sa_tok[0] = sa_tok[1] = [sa_tok[0], sa_tok[1], done3, out2_done]
    xb4["free"] = rstd_free[0]
    for pi, (up, down) in enumerate(ffn2):
        run_all(up)
        run_all(down)
        hid["free"] = chunk_done[cursor[0] - 1]
    ffn2_done = chunk_done[cursor[0] - 1]
    pe_later()

    t_rstd = rstd_of(xb4["box"], D)
    L_out = Landing(sem("l_out"))
    y_free = [region_free[0], region_free[0], region_free[1], region_free[1]]
    y_tok = None
    out_rows = out[0].rearrange("(t p) d -> p t d", p=128)
    for m0 in range(0, KT, 4):
        for i in range(4):
            m = m0 + i
            t = dve(lambda e, m=m: e.scalar_tensor_tensor(xT[:, m, :], xT[:, m, :], g_fin2[:, m:m + 1], rstd[:, :],
                                                          ALU.mult, ALU.mult), t_rstd, xb4["x"])
        ys = []
        for h in range(2):
            i = (m0 // 4 * 2 + h) % 4
            for j in range(4):
                tk = pe(lambda e, i=i, j=j, m=m0 + j, h=h: e.transpose(
                    bank[i][:, 128 * j:128 * j + 128], xT[:, m, 128 * h:128 * h + 128], ident[:, :]),
                    t, y_free[i], inc=j == 3)
            dst = YROW[:, h, 128 * m0:128 * m0 + 512]
            if h == 0:
                ty = act(lambda e, dst=dst, i=i: e.activation(dst, bank[i][:, :], ACT.Copy), tk, ffn2_done)
            else:
                ty = dve(lambda e, dst=dst, i=i: e.tensor_copy(dst, bank[i][:, :]), tk, ffn2_done)
            y_free[i] = ty
            ys.append(ty)
        y_tok = L_out.start(sp, out_rows[:, :, 128 * m0:128 * m0 + 512], YROW[:, :, 128 * m0:128 * m0 + 512], ys)

    assert cursor[0] == len(chunks)

    with nc.Block() as block:
        @block.tensor
        def _(e):
            pe.play(e)

        @block.scalar
        def _(e):
            act.play(e)

        @block.vector
        def _(e):
            dve.play(e)

        @block.gpsimd
        def _(e):
            pool.play(e)

        @block.sync
        def _(e):
            sp.play(e)
            e.wait_ge(*t_tA)
            e.wait_ge(*t_tB)
            e.wait_ge(*y_tok)


def kernel(**inputs):
    import concourse.bacc as _bacc
    from concourse.bass_utils import run_bass_kernel_spmd as _run

    nc = _bacc.Bacc("TRN2", target_bir_lowering=False, num_devices=1)
    arrays = {n: np.ascontiguousarray(inputs[n]) for n in IN_NAMES}
    arrays.update(shape_constants())
    A = {}
    for name, a in arrays.items():
        A[name] = nc.dram_tensor(f"in_{name}", a.shape, F32, kind="ExternalInput").ap()
    out = nc.dram_tensor("out_y", (1, S, D), F32, kind="ExternalOutput").ap()
    build(nc, A, out)
    r = _run(nc, [{f"in_{n}": a for n, a in arrays.items()}], core_ids=[0])
    return r.results[0]["out_y"]
```

```python
import math
from collections import deque

import numpy as np

import concourse.bass as bass
from concourse import mybir

F32 = mybir.dt.float32
F32R = mybir.dt.float32r
ALU = mybir.AluOpType
ACT = mybir.ActivationFunctionType
AX_X = mybir.AxisListType.X

S = 256
D = 2048
KT = D // 128
FF1 = 5632
FF2 = 8192
NEG = -1e30
EPS = 1e-6
NRAW = 4
KB = 1024
BASE = 16 * KB + 128

IN_NAMES = [
    "x", "rel_bias", "mix_norm_g", "ffn_norm_g", "final_norm_g", "nsa_w_in", "nsa_w_out",
    "cmp_pos_k", "cmp_w1_k", "cmp_w2_k", "cmp_pos_v", "cmp_w1_v", "cmp_w2_v", "ffn_w_in", "ffn_w_out",
    "c_2", "w_mod_2", "b_mod_2", "attn_norm_g_2", "w_in_2", "swa_sinks_2", "rel_bias_2",
    "mla_q_norm_g_2", "w_uq_2", "mla_kv_norm_g_2", "w_ukv_2", "w_out_2", "mlp_norm_g_2",
    "w_ff1_2", "w_ff2_2", "final_norm_g_2",
]


def shape_constants():
    n = np.arange(0, 256)
    large = 16 + (np.log(np.maximum(n, 1).astype(np.float32) / np.float32(16))
                  / np.float32(math.log(128 / 16)) * np.float32(16)).astype(np.int32)
    bucket = np.where(n < 16, n, np.minimum(large, 31))

    def onehot(dist, far):
        t = np.zeros((33, len(dist)), np.float32)
        for i, d in enumerate(dist):
            if 0 <= d < far:
                t[bucket[d], i] = 1.0
            else:
                t[32, i] = 1.0
        return t

    up = np.clip(np.arange(512) - 255, -255, 255)
    down = np.clip(255 - np.arange(384), -127, 255)
    oh = np.concatenate([onehot(up, 256), onehot(down, 256), onehot(down, 128)], axis=1)
    inv = (10000.0 ** (-np.arange(32, dtype=np.float32) / np.float32(32))).astype(np.float32)
    ang = inv[:, None] * np.arange(S, dtype=np.float32)[None, :]
    cos, sin = np.cos(ang).astype(np.float32), np.sin(ang).astype(np.float32)
    t = np.arange(128)[:, None]
    j = np.arange(256)[None, :]
    return {
        "c_ident": np.eye(128, dtype=np.float32),
        "c_ones": np.ones((128, 128), np.float32),
        "c_onehot": oh,
        "c_cos": np.concatenate([cos] * 4, axis=0),
        "c_sin": np.concatenate([-sin, sin, -sin, sin], axis=0),
        "c_causal": np.where(128 + t - j >= 0, 0.0, NEG).astype(np.float32),
    }


def flat(waits):
    for w in waits:
        if w is None:
            continue
        if isinstance(w, list):
            yield from flat(w)
        else:
            yield w


class Queue:

    def __init__(self, sem):
        self.sem, self.n, self.ops = sem, 0, []

    def __call__(self, fn, *waits, inc=True):
        self.n += inc
        self.ops.append((fn, list(flat(waits)), inc))
        return (self.sem, self.n) if inc else None

    def play(self, eng):
        seen = {}
        for fn, waits, inc in self.ops:
            need = {}
            for sem, v in waits:
                if v > seen.get(sem.num, 0) and v > need.get(sem.num, (sem, 0))[1]:
                    need[sem.num] = (sem, v)
            for num, (sem, v) in need.items():
                eng.wait_ge(sem, v)
                seen[num] = v
            ins = fn(eng)
            if inc:
                ins.then_inc(self.sem, 1)


class Landing:

    def __init__(self, sem):
        self.sem, self.n = sem, 0

    def start(self, q, dst, src, *waits):
        self.n += 16
        q(lambda e: e.dma_start(dst, src).then_inc(self.sem, 16), *waits, inc=False)
        return (self.sem, self.n)


def build(nc, A, out):
    sems = [0]

    def sem(name):
        sems[0] += 1
        return nc.alloc_semaphore(name)

    at = [BASE]

    def sb(name, shape, dt=F32, offset=None):
        size = int(np.prod(shape[1:])) * 4
        if offset is None:
            offset = at[0]
            at[0] += (size + 31) // 32 * 32
        return nc.alloc_sbuf_tensor_at("m_" + name, shape, dt, offset=offset)

    pe, act, dve = Queue(sem("s_pe")), Queue(sem("s_act")), Queue(sem("s_dve"))
    pool, sp = Queue(sem("s_pool")), Queue(sem("s_sp"))

    xT = sb("xT", [128, KT, S])
    HI = sb("HI", [128, KT, S], F32R)
    LO = sb("LO", [128, KT, S], F32R)
    RAW = [sb(f"RAW{i}", [128, 2048]) for i in range(NRAW)]
    WHI = [sb(f"WHI{i}", [128, 1024], F32R) for i in range(4)]
    WLO = [sb(f"WLO{i}", [128, 1024], F32R) for i in range(4)]
    acc_at = at[0]
    ACC = sb("ACC", [128, 2048])
    ident = sb("ident", [128, 128])
    ones = sb("ones", [128, 128])
    cols = sb("cols", [128, 116])
    cact = sb("cact", [128, 16])
    bmod = sb("bmod", [128, 96])
    mod = sb("mod", [128, 96])
    G1c = sb("G1c", [128, 16])
    G2c = sb("G2c", [128, 16])
    gates = sb("gates", [128, 3, 16, 4])
    cmpb = sb("cmpb", [128, 32, 15])
    rstd = sb("rstd", [128, S])
    std = sb("std", [128, S])
    w2 = sb("w2", [128, 2, 2, 128])
    hidT = sb("hidT", [128, 2, 2, 60])
    kccT = sb("kccT", [128, 60])
    posT = sb("posT", [128, 64])
    epsc = sb("epsc", [128, 1])
    sinkr = sb("sinkr", [128, 16])
    SK = sb("SK", [128, 8, 4])
    rela = sb("rela", [33, 16])
    relb = sb("relb", [33, 16])
    stat = sb("stat", [128, 3, 6, 4])
    cst = sb("cst", [128, 4, 32])
    U = at[0]
    assert U + 76 * KB <= 229344, (U, 229344 - U)

    def un(name, shape, kb, dt=F32):
        return sb(name, shape, dt, offset=U + int(kb * KB))

    XROW = un("XROW", [128, 2, D], 0)
    OH = un("OH", [33, 1280], 16)
    rowsA = un("rowsA", [116, 128], 21)
    rowsB = un("rowsB", [96, 128], 21.5)
    rowsP = un("rowsP", [64, 128], 22)
    R16a = un("R16a", [16, 384], 22.5)
    R16b = un("R16b", [16, 384], 24)
    qT = un("qT", [128, 16, S], 0)
    ksT = un("ksT", [128, 4, S], 16)
    kwT = un("kwT", [128, 4, S], 20)
    vs = un("vs", [128, 2, 512], 24)
    vw = un("vw", [128, 2, 512], 28)
    biasA = un("biasA", [128, 16, S], 32)
    Vpad = un("Vpad", [128, 16, 128], 48)
    PcT = un("PcT", [128, 4, S], 56)
    kcT = un("kcT", [128, 4, S], 60)
    vcT = un("vcT", [128, 4, S], 64)
    Z = un("Z", [128, 32, 60], 68)
    SP1 = [un(f"SP1_{i}", [128, 768], 60 + 3 * i) for i in range(3)]
    PT1 = [un(f"PT1_{i}", [128, 2, 384], 69 + 3 * i) for i in range(2)]
    Pc = un("Pc", [128, 2, 4, 32], 75)
    HIDH = un("HIDH", [128, 24, S], 0, F32R)
    HIDL = un("HIDL", [128, 24, S], 24, F32R)
    SA = [un(f"SA{i}", [128, 4, S], 48 + 4 * i) for i in range(2)]
    HT = [un(f"HT{i}", [128, 4, S], 56 + 4 * i) for i in range(2)]
    SQ = [un(f"SQ{i}", [128, 4, S], 64 + 4 * i) for i in range(2)]
    SR = [un(f"SR{i}", [128, S], 72 + i) for i in range(2)]
    qaT = un("qaT", [128, 8, S], 0)
    Kpad = un("Kpad", [128, 2, 2, S], 8)
    Vpad2 = un("Vpad2", [128, 2, 2, 2, 128], 12)
    CQH = un("CQH", [128, 4, S], 16, F32R)
    CQL = un("CQL", [128, 4, S], 20, F32R)
    krp = un("krp", [128, S], 24)
    SP2 = [un(f"SP2_{i}", [128, 768], 64 + 3 * i) for i in range(3)]
    PT2 = [un("PT2_0", [128, 2, 384], 73), un("PT2_1", [128, 2, 384], 25)]
    ropeX, ropeT, ropeU = [sb(n, [128, 2, S], offset=acc_at + 2 * KB * i) for i, n in enumerate(("ropeX", "ropeT", "ropeU"))]
    causal = un("causal", [128, S], 28)
    cosT = un("cosT", [128, S], 29)
    sinT = un("sinT", [128, S], 30)
    biasB = un("biasB", [128, 16, S], 32)
    CQ = un("CQ", [128, 4, S], 64)
    CSQ = un("CSQ", [128, 4, S], 68)
    qnT = un("qnT", [128, 8, S], 48)
    qrT = un("qrT", [128, 8, S], 56)
    knT = un("knT", [128, 8, S], 32)
    vb = un("vb", [128, 2, 1024], 40)
    YROW = un("YROW", [128, 2, D], 0)

    bank = [nc.alloc_psum_tensor(f"bank{i}", [128, 512], F32) for i in range(8)]
    region = [(bank[0], bank[1]), (bank[2], bank[3])]

    toepA = nc.dram_tensor("toepA", [16, 128, 384], F32, kind="Internal").ap()
    toepB = nc.dram_tensor("toepB", [16, 128, 384], F32, kind="Internal").ap()

    L_x = [Landing(sem(f"l_x{i}")) for i in range(4)]
    L_c, L_k = Landing(sem("l_c")), Landing(sem("l_k"))
    L_rows, L_rowP = Landing(sem("l_rows")), Landing(sem("l_rowP"))
    L_w2 = Landing(sem("l_w2"))
    x_rows = A["x"][0].rearrange("(t p) d -> p t d", p=128)
    L_c.start(act, ident[:, :], A["c_ident"])
    c_in = L_c.start(act, ones[:, :], A["c_ones"])
    x_in = [L_x[i].start(sp, XROW[:, :, 512 * i:512 * i + 512], x_rows[:, :, 512 * i:512 * i + 512]) for i in range(4)]
    r = 0
    for name in ("mix_norm_g", "ffn_norm_g", "final_norm_g", "attn_norm_g_2", "mlp_norm_g_2",
                 "final_norm_g_2", "c_2", "mla_q_norm_g_2", "mla_kv_norm_g_2"):
        a = A[name]
        v = a if len(a.shape) == 1 else a[0]
        n = v.shape[0] // 128
        rows_in = L_rows.start(act, rowsA[r:r + n, :], v.rearrange("(r c) -> r c", c=128))
        r += n
    L_k.start(pool, OH[:, :], A["c_onehot"])
    L_k.start(pool, rela[0:32, :], A["rel_bias"])
    L_k.start(pool, relb[0:32, :], A["rel_bias_2"])
    sk = A["swa_sinks_2"][0]
    k_in = L_k.start(pool, sinkr[:, :], bass.AP(tensor=sk.tensor, offset=sk.offset, ap=[[0, 128], [1, 16]]))
    L_rowP.start(pool, rowsB[:, :], A["b_mod_2"][0].rearrange("(r c) -> r c", c=128))
    L_rowP.start(pool, rowsP[0:32, :], A["cmp_pos_k"][0])
    rowP_in = L_rowP.start(pool, rowsP[32:64, :], A["cmp_pos_v"][0])
    L_w2.start(pool, w2[:, 0, :, :], A["cmp_w2_k"][0].rearrange("(k p) n -> p k n", p=128))
    w2_in = L_w2.start(pool, w2[:, 1, :, :], A["cmp_w2_v"][0].rearrange("(k p) n -> p k n", p=128))

    eps_set = dve(lambda e: e.memset(epsc[:, :], EPS))
    relm = [dve(lambda e, t=t: e.memset(t[32:33, :], NEG)) for t in (rela, relb)]

    L_raw = [Landing(sem(f"l_raw{i}")) for i in range(NRAW)]
    raw_free = [None] * NRAW
    n_loads = [0]

    def load(view, src):
        slot = n_loads[0] % NRAW
        n_loads[0] += 1
        tok = L_raw[slot].start(sp, view(RAW[slot]), src, raw_free[slot])
        return RAW[slot], tok, slot

    slabs, chunks = [], []
    bf = {b: None for b in range(4, 8)}

    def slab(w, row0, kts, c0, ncol, groups, rhs, evac, per=None):
        per = per or max(1, min(8, 2048 // ncol))
        s = dict(w=w, row0=row0, c0=c0, nc=ncol, groups=groups, rhs=rhs, evac=evac, reg=len(slabs) % 2, opened=set())
        slabs.append(s)
        s["list"] = [(s, k, min(per, kts - k), k + per >= kts) for k in range(0, kts, per)]
        return s

    def queue(*together):
        for i in range(max(len(s["list"]) for s in together)):
            chunks.extend(s["list"][i] for s in together if i < len(s["list"]))

    def feat(c, b, off):
        return ("f", lambda v, k: v[:, k, c:c + 128], b, off, S)

    def tokh(c, n, half, b, off):
        return ("t%d" % half, lambda v, k: v[:, k, c:c + n], b, off, n)

    FEAT4 = [feat(128 * i, i // 2, 256 * (i % 2)) for i in range(4)]
    TOK512 = [tokh(0, 512, 0, 0, 0), tokh(0, 512, 1, 1, 0)]

    parts, split_tok, part_done, chunk_done = [], [], [], {}
    chunk_raw = {}

    def split():
        u = len(split_tok)
        while u >= len(parts):
            n = parts[-1][0] + 1 if parts else 0
            if n >= len(chunks):
                return
            nk = chunks[n][2]
            h = (nk + 1) // 2
            parts.extend((n, a, z) for a, z in ((0, h), (h, nk)) if z > a)
        n, a, z = parts[u]
        s, k, nk, _ = chunks[n]
        ncol = s["nc"]
        if a == 0:
            src = s["w"][(s["row0"] + k) * 128:(s["row0"] + k + nk) * 128, :]
            src = src[:, s["c0"]:s["c0"] + ncol].rearrange("(k p) n -> p k n", p=128)
            chunk_raw[n] = load(lambda t: t[:, 0:nk * ncol].rearrange("p (k n) -> p k n", k=nk), src)
        raw, landed, slot = chunk_raw[n]
        hi, lo, m = WHI[u % 4], WLO[u % 4], (z - a) * ncol
        part = raw[:, a * ncol:z * ncol]
        free = part_done[u - 4] if u >= 4 else None
        t_hi = act(lambda e: e.activation(hi[:, 0:m], part, ACT.Copy), landed, free)
        t_lo = dve(lambda e: e.tensor_tensor(lo[:, 0:m], part, hi[:, 0:m].bitcast(F32), ALU.subtract),
                   landed, free, t_hi)
        raw_free[slot] = [t_hi, t_lo]
        split_tok.append([t_hi, t_lo])

    region_free = [None, None]
    later = []
    side = deque()
    cursor = [0]
    extra = {"every": [], "rate": 1, "gemv": 0.0, "credit": 0.0, "due": 0.0}

    def pe_later():
        todo = later[:]
        later.clear()
        for f in todo:
            f()

    def tick():
        extra["due"] += extra["rate"]
        while extra["due"] >= 1:
            extra["due"] -= 1
            if side:
                side.popleft()()

    def drain():
        while side:
            side.popleft()()

    def run_chunk():
        n = cursor[0]
        cursor[0] += 1
        while len(split_tok) < 4:
            split()
        s, k, nk, last = chunks[n]
        reg = region[s["reg"]]
        for kk in range(nk):
            u = len(part_done)
            while len(split_tok) <= u:
                split()
            _, a, z = parts[u]
            view = [t[:, 0:(z - a) * s["nc"]].rearrange("p (k n) -> p k n", k=z - a) for t in (WHI[u % 4], WLO[u % 4])]
            waits = [split_tok[u], region_free[s["reg"]] if k == 0 else None]
            xh, xl, x_tok = s["rhs"](k + kk)
            todo = []
            for kind, cut, b, off, w in s["groups"]:
                start = b not in s["opened"]
                s["opened"].add(b)
                for i, (wv, xv) in enumerate(((view[0], xh), (view[0], xl), (view[1], xh))):
                    wa = cut(wv, kk - a)
                    if kind == "f":
                        lhs, rhs = wa, xv
                    else:
                        h = 128 * int(kind[1])
                        lhs, rhs = xv[:, h:h + 128], wa
                    todo.append((reg[b][:, off:off + w], lhs, rhs, start and i == 0, last and kk == nk - 1 and i == 2))
            for j, (o, lhs, rhs, st, fin) in enumerate(todo):
                end = kk == z - 1 and j == len(todo) - 1
                tk = pe(lambda e, o=o, lhs=lhs, rhs=rhs, st=st, fin=fin: e.matmul(
                    o, lhs, rhs, start=st, stop=fin, skip_group_check=True),
                    waits if j == 0 else None, x_tok if j == 0 else None, inc=end)
            if kk == z - 1:
                part_done.append(tk)
                if kk < nk - 1:
                    split()
            if kk < nk - 1:
                tick()
        chunk_done[n] = tk
        pe_later()
        split()
        if last:
            region_free[s["reg"]] = s["evac"](reg, tk)
        tick()
        if extra["every"]:
            extra["every"].pop(0)()
        extra["credit"] += extra["gemv"]
        while extra["credit"] >= 1:
            extra["credit"] -= 1
            next_gemv()

    def run(*ss_):
        for _ in range(sum(len(s["list"]) for s in ss_)):
            run_chunk()

    sq_free = [None, None]
    sr_free = [None, None]
    sq_n = [0]
    ss = bank[6][:, 0:S]

    def ssq_add(m0, x_tok, first, last, now=False):
        b = sq_n[0] % 2
        sq_n[0] += 1
        t_sq = act(lambda e: e.activation(SQ[b][:, :, :], xT[:, m0:m0 + 4, :], ACT.Square), x_tok, sq_free[b])
        t_sr = dve(lambda e: e.tensor_reduce(SR[b][:, :], SQ[b][:, :, :].rearrange("p m s -> p s m"), AX_X, ALU.add),
                   t_sq, sr_free[b])
        sq_free[b] = t_sr
        box = {}

        def go():
            tk = pe(lambda e: e.matmul(ss, ones[:, :], SR[b][:, :], start=first, stop=last, skip_group_check=True),
                    t_sr, c_in, bf[6] if first else None)
            sr_free[b] = tk
            box["tok"] = tk
        if now:
            go()
        else:
            later.append(go)
        return box

    rstd_free = [None]

    def rstd_of(box, n):
        t_std = act(lambda e: e.activation(std[:, :], ss, ACT.Sqrt, bias=epsc[:, 0:1], scale=1.0 / n),
                    box["tok"], eps_set, rstd_free[0])
        bf[6] = t_std
        return dve(lambda e: e.reciprocal(rstd[:, :], std[:, :]), t_std, rstd_free[0])

    ht_free = [None, None]

    def norm_apply(gcol, g_tok, t_rstd, free, shcol=None):
        toks = []
        for b in range(4):
            ht = HT[b % 2]
            t = None
            for i in range(4):
                m = 4 * b + i
                t = dve(lambda e, m=m, i=i, ht=ht: e.scalar_tensor_tensor(
                    ht[:, i, :], xT[:, m, :], gcol[:, m:m + 1], rstd[:, :], ALU.mult, ALU.mult),
                    t_rstd, g_tok, ht_free[b % 2])
            sl = slice(4 * b, 4 * b + 4)
            if shcol is None:
                t_hi = act(lambda e, ht=ht, sl=sl: e.activation(HI[:, sl, :], ht[:, :, :], ACT.Copy), t, free)
                t_lo = dve(lambda e, ht=ht, sl=sl: e.tensor_tensor(
                    LO[:, sl, :], ht[:, :, :], HI[:, sl, :].bitcast(F32), ALU.subtract), t, t_hi, free)
            else:
                for i in range(4):
                    m = 4 * b + i
                    t_hi = act(lambda e, ht=ht, m=m, i=i: e.activation(
                        HI[:, m, :], ht[:, i, :], ACT.Identity, bias=shcol[:, m:m + 1]), t, free)
                for i in range(4):
                    m = 4 * b + i
                    t_lo = dve(lambda e, ht=ht, m=m, i=i: e.scalar_tensor_tensor(
                        LO[:, m, :], ht[:, i, :], shcol[:, m:m + 1], HI[:, m, :].bitcast(F32),
                        ALU.add, ALU.subtract), t, t_hi, free)
            ht_free[b % 2] = [t_hi, t_lo]
            toks.append([t_hi, t_lo])
        rstd_free[0] = t
        return toks

    def rhs_of(hi, lo, toks, base=0):
        def get(k):
            while toks["t"][(base + k) // 4] is None:
                side.popleft()()
            return hi[:, base + k, :], lo[:, base + k, :], toks["t"][(base + k) // 4]
        return get

    g_mix, g_ffn, g_fin, g_att2, g_mlp2, g_fin2 = [cols[:, 16 * i:16 * i + 16] for i in range(6)]
    gq, gkv = cols[:, 112:115], cols[:, 115:116]
    x_free = [None] * 4
    x_new = []
    for m0 in range(0, KT, 4):
        tt = []
        for t in range(2):
            i = (m0 // 4 * 2 + t) % 4
            for j in range(4):
                m = m0 + j
                tp = pe(lambda e, i=i, j=j, m=m, t=t: e.transpose(
                    bank[i][:, 128 * j:128 * j + 128], XROW[:, t, 128 * m:128 * m + 128], ident[:, :]),
                    x_in[m0 // 4], x_free[i], c_in, inc=j == 3)
            dst = xT[:, m0:m0 + 4, 128 * t:128 * t + 128]
            src = bank[i][:, :].rearrange("p (m s) -> p m s", m=4)
            if t == 0:
                tc = act(lambda e, dst=dst, src=src: e.activation(dst, src, ACT.Copy), tp)
            else:
                tc = dve(lambda e, dst=dst, src=src: e.tensor_copy(dst, src), tp)
            x_free[i] = tc
            tt.append(tc)
        x_new.append(tt)
        pe_later()
        box = ssq_add(m0, tt, m0 == 0, m0 == 12)
    region_free[0] = [x_free[0], x_free[1]]
    region_free[1] = [x_free[2], x_free[3]]
    xrow_done = x_new[3]
    t_rowA = pe(lambda e: e.transpose(bank[4][:, 0:116], rowsA[:, :], ident[0:116, 0:116]), c_in, rows_in)
    pe_later()
    t_cols = act(lambda e: e.activation(cols[:, :], bank[4][:, 0:116], ACT.Copy), t_rowA)
    bf[4] = t_cols

    L_tA, L_tB = Landing(sem("l_tA")), Landing(sem("l_tB"))
    L_bA, L_bB = Landing(sem("l_bA")), Landing(sem("l_bB"))
    T = {}

    def repeated(t):
        a = t[:, :]
        return bass.AP(tensor=a.tensor, offset=a.offset, ap=[list(a.ap[0]), [0, 128], [1, 384]])

    def toeplitz(t):
        return bass.AP(tensor=t.tensor, offset=t.offset + 127, ap=[[383, 128], [128 * 384, 16], [1, 256]])

    def tables_cols():
        pe(lambda e: e.transpose(bank[4][:, 128:224], rowsB[:, :], ident[0:96, 0:96]), rowP_in, bf[4], inc=False)
        tk = pe(lambda e: e.transpose(bank[4][:, 256:320], rowsP[:, :], ident[0:64, 0:64]))
        T["cact"] = act(lambda e: e.activation(cact[:, :], cols[:, 96:112], ACT.Silu), t_cols)
        T["bmod"] = act(lambda e: e.activation(bmod[:, :], bank[4][:, 128:224], ACT.Copy), tk)
        T["posT"] = bf[4] = act(lambda e: e.activation(posT[:, :], bank[4][:, 256:320], ACT.Copy), tk)

    def tables_toeplitz():
        pe(lambda e: e.matmul(bank[5][0:16, 0:384], rela[:, :], OH[:, 512:896], start=True, stop=True),
           k_in, relm, bf[5], inc=False)
        tk = pe(lambda e: e.matmul(bank[7][0:16, 0:384], relb[:, :], OH[:, 896:1280], start=True, stop=True), bf[7])
        ta = bf[5] = act(lambda e: e.activation(R16a[:, :], bank[5][0:16, 0:384], ACT.Copy), tk)
        tb = bf[7] = act(lambda e: e.activation(R16b[:, :], bank[7][0:16, 0:384], ACT.Copy), tk)
        t_tA = L_tA.start(pool, toepA, repeated(R16a), ta)
        T["tB"] = L_tB.start(pool, toepB, repeated(R16b), tb)
        T["tA"] = t_tA
        T["biasA"] = L_bA.start(pool, biasA[:, :, :], toeplitz(toepA), t_tA)

    def tables_cmp(b):
        for c in range(15):
            o = 255 + 128 * b - 16 * c - 31
            n = 16 * c
            tk = pe(lambda e, o=o, n=n: e.matmul(bank[7][:, n:n + 16], OH[:, o:o + 128], rela[:, :],
                                                 start=n == 0, stop=True, skip_group_check=True),
                    [bf[7], k_in, relm] if c == 0 else None, inc=c == 14)
        T["cmpb"] = bf[7] = act(lambda e: e.activation(
            cmpb[:, 16 * b:16 * b + 16, :], bank[7][:, 0:240].rearrange("p (c h) -> p h c", c=15), ACT.Copy), tk)

    side.extend([tables_cols, tables_toeplitz, lambda: tables_cmp(0), lambda: tables_cmp(1)])

    mod_tok = [None] * 6
    acc_free = [None]

    def gemv(p, k):
        def go():
            raw, landed, slot = load(lambda t: t[:, :],
                                     A["w_mod_2"][0][k * 128:(k + 1) * 128, p * 2048:(p + 1) * 2048])
            if k == 0:
                t = dve(lambda e: e.tensor_scalar(ACC[:, :], raw[:, :], cact[:, 0:1], None, ALU.mult),
                        landed, T["cact"], acc_free[0])
            else:
                t = dve(lambda e: e.scalar_tensor_tensor(ACC[:, :], raw[:, :], cact[:, k:k + 1], ACC[:, :],
                                                         ALU.mult, ALU.add), landed, acc_tok[0])
            acc_tok[0] = t
            raw_free[slot] = t
            if k == 15:
                def reduce():
                    for j in range(16):
                        tk = pe(lambda e, j=j: e.matmul(
                            bank[7][:, j:1 + j], ACC[:, 128 * j:128 * j + 128], ones[:, 0:1],
                            start=j == 0, stop=True, skip_group_check=True),
                            [t, bf[7]] if j == 0 else None, inc=j == 15)
                    acc_free[0] = tk
                    sl = slice(16 * p, 16 * p + 16)
                    mod_tok[p] = bf[7] = dve(lambda e: e.tensor_tensor(
                        mod[:, sl], bank[7][:, 0:16], bmod[:, sl], ALU.add), tk, T["bmod"])
                later.append(reduce)
        return go

    acc_tok = [None]
    gemvs = []
    for p in range(6):
        gemvs += [gemv(p, k) for k in range(16)] + [None]

    gq_iter = iter(gemvs)

    def next_gemv():
        f = next(gq_iter, None)
        if f is not None:
            f()

    declare = slab

    h1 = {}
    rhs1 = rhs_of(HI, LO, h1)
    tk1 = {}

    def to_feat(dst, name, scale=1.0, tiles=4, free=lambda: None):
        def evac(reg, done):
            t = None
            for b in range(tiles // 2):
                src = reg[b][:, :].rearrange("p (m s) -> p m s", m=2)
                d = dst[:, 2 * b:2 * b + 2, :]
                t = act(lambda e, d=d, src=src: e.activation(d, src, ACT.Copy, scale=scale), done, free())
            tk1[name] = t
            return t
        return evac

    def to_tok(dst, name, free=lambda: None):
        def evac(reg, done):
            t = None
            for b in range(2):
                t = act(lambda e, b=b: e.activation(dst[:, b, :], reg[b][:, :], ACT.Copy), done, free())
            tk1[name] = t
            return t
        return evac

    def gate_evac(reg, done):
        t = None
        for b in range(2):
            for br in range(3):
                o = gates[:, br, :, b] if br == 0 else gates[:, 1, :, 2 * (1 - b) + br - 1]
                src = reg[b][:, 16 * br:16 * br + 16]
                t = act(lambda e, o=o, src=src: e.activation(o, src, ACT.Sigmoid), done)
        tk1["gates"] = t
        return t

    W = A["nsa_w_in"][0]
    def tables_done():
        return [T[n] for n in ("tA", "tB", "cmpb", "posT", "bmod")]

    nsa = [
        declare(W, 0, KT, 2048, 512, FEAT4, rhs1, to_feat(kcT, "kc", free=lambda: h1["ht"])),
        declare(W, 0, KT, 2560, 512, FEAT4, rhs1, to_feat(vcT, "vc", free=lambda: h1["ht"])),
        declare(W, 0, KT, 3072, 512, FEAT4, rhs1, to_feat(ksT, "ks", free=tables_done)),
        declare(W, 0, KT, 4096, 512, FEAT4, rhs1, to_feat(kwT, "kw", free=tables_done)),
        declare(W, 0, KT, 3584, 512, TOK512, rhs1, to_tok(vs, "vs", free=tables_done)),
        declare(W, 0, KT, 4608, 512, TOK512, rhs1, to_tok(vw, "vw", free=tables_done)),
        declare(W, 0, KT, 5120, 48, [tokh(0, 48, 0, 0, 0), tokh(0, 48, 1, 1, 0)], rhs1, gate_evac),
    ]
    for i in range(4):
        nsa.append(declare(W, 0, KT, 512 * i, 512, FEAT4, rhs1,
                           to_feat(qT[:, 4 * i:4 * i + 4, :], f"q{i}", scale=128.0 ** -0.5, free=lambda: xrow_done)))
    for s_ in nsa:
        queue(s_)

    def residual(xbox, gcol=None, g_tok=None, ssq=True):
        def at_tile(m0, first, last):
            def evac(reg, done):
                t = None
                for b in range(2):
                    src = reg[b][:, :].rearrange("p (m s) -> p m s", m=2)
                    x = xT[:, m0 + 2 * b:m0 + 2 * b + 2, :]
                    if gcol is None:
                        t = dve(lambda e, x=x, src=src: e.tensor_tensor(x, src, x, ALU.add), done, xbox.get("free"))
                    else:
                        for i in range(2):
                            m = m0 + 2 * b + i
                            t = dve(lambda e, m=m, b=b, i=i: e.scalar_tensor_tensor(
                                xT[:, m, :], reg[b][:, 256 * i:256 * i + 256], gcol[:, m:m + 1], xT[:, m, :],
                                ALU.mult, ALU.add), done, xbox.get("free"), mod_tok[g_tok])
                if ssq:
                    xbox["box"] = ssq_add(m0, t, first, last)
                xbox["x"] = t
                return t
            return evac
        return at_tile

    xb1, xb2, xb3, xb4 = {}, {}, {}, {}

    def declare_out(w, row0, kts, rhs, maker, pair=False):
        new = [declare(w, row0, kts, 512 * i, 512, FEAT4, rhs, maker(4 * i, i == 0, i == 3)) for i in range(4)]
        if pair:
            queue(new[0], new[1])
        else:
            queue(new[0])
            queue(new[1])
        queue(new[2])
        queue(new[3])
        return new

    h2 = {}
    out1 = declare_out(A["nsa_w_out"][0], 0, KT, rhs_of(HI, LO, h2), residual(xb1), pair=True)

    hid = {}
    sa_n, sa_tok = [0], [None, None]
    ht2_n = [0]

    def hid_split(ht, b, base, t_h):
        t_hi = act(lambda e: e.activation(HIDH[:, base:base + 4, :], ht[:, :, :], ACT.Copy), t_h, hid["free"])
        t_lo = dve(lambda e: e.tensor_tensor(HIDL[:, base:base + 4, :], ht[:, :, :],
                                             HIDH[:, base:base + 4, :].bitcast(F32), ALU.subtract),
                   t_h, t_hi, hid["free"])
        ht_free[b] = [t_hi, t_lo]
        hid["t"][base // 4] = [t_hi, t_lo]

    def silu_evac(reg, done):
        i = sa_n[0] % 2
        t = None
        for b in range(2):
            t = act(lambda e, b=b: e.activation(SA[i][:, 2 * b:2 * b + 2, :],
                                                reg[b][:, :].rearrange("p (m s) -> p m s", m=2), ACT.Silu),
                    done, sa_tok[i], hid.get("ufree"))
        hid["sa"] = t
        return t

    def glu_evac(base):
        def evac(reg, done):
            i = sa_n[0] % 2
            sa_n[0] += 1
            t = None
            for b in range(2):
                t = dve(lambda e, b=b: e.tensor_tensor(
                    HT[i][:, 2 * b:2 * b + 2, :], reg[b][:, :].rearrange("p (m s) -> p m s", m=2),
                    SA[i][:, 2 * b:2 * b + 2, :], ALU.mult), done, hid["sa"], ht_free[i])
            sa_tok[i] = t
            hid_split(HT[i], i, base, t)
            return t
        return evac

    def relu2_evac(base):
        def evac(reg, done):
            i = sa_n[0] % 2
            sa_n[0] += 1
            t = None
            for b in range(2):
                t = act(lambda e, b=b: e.activation(SA[i][:, 2 * b:2 * b + 2, :],
                                                    reg[b][:, :].rearrange("p (m s) -> p m s", m=2), ACT.Relu),
                        done, sa_tok[i])
            t_h = dve(lambda e: e.tensor_tensor(HT[i][:, :, :], SA[i][:, :, :], SA[i][:, :, :], ALU.mult),
                      t, ht_free[i])
            sa_tok[i] = t_h
            hid_split(HT[i], i, base, t_h)
            return t
        return evac

    h3 = {}
    rhs3 = rhs_of(HI, LO, h3)
    ffn1 = []
    W1, W2 = A["ffn_w_in"][0], A["ffn_w_out"][0]
    parts1 = [(0, 6), (6, 5)]
    hidv = {"t": [None] * 6}
    hid["t"] = [None] * 6
    for pi, (s0, n) in enumerate(parts1):
        up = []
        for j in range(n):
            c = 512 * (s0 + j)
            up.append(declare(W1, 0, KT, c, 512, FEAT4, rhs3, silu_evac))
            up.append(declare(W1, 0, KT, FF1 + c, 512, FEAT4, rhs3, glu_evac(4 * j)))
            queue(up[-2])
            queue(up[-1])
        down = declare_out(W2, 4 * s0, 4 * n, rhs_of(HIDH, HIDL, hid),
                           residual(xb2, ssq=pi == len(parts1) - 1))
        ffn1.append((up, down))

    h4 = {}
    rhs4 = rhs_of(HI, LO, h4)
    W = A["w_in_2"][0]

    att2 = {}

    def ka_evac(reg, done):
        t = None
        for kv in range(2):
            for par in range(2):
                t = act(lambda e, kv=kv, par=par: e.activation(
                    Kpad[64 * par:64 * par + 64, kv, par, :], reg[0][64 * kv:64 * kv + 64, 0:S], ACT.Copy),
                    done, att2["pad0"])
                for half in range(2):
                    src = reg[0][:, 256 + 64 * kv:320 + 64 * kv] if half == 0 else reg[1][:, 64 * kv:64 * kv + 64]
                    t = act(lambda e, kv=kv, par=par, half=half, src=src: e.activation(
                        Vpad2[:, kv, par, half, 64 * par:64 * par + 64], src, ACT.Copy), done, att2["pad0"])
        att2["kv"] = t
        return t

    def cq_evac(reg, done):
        t = None
        for m in range(3):
            t = act(lambda e, m=m: e.activation(CQ[:, m, :], reg[m // 2][:, 256 * (m % 2):256 * (m % 2) + 256],
                                                ACT.Copy), done, att2["free"])
        att2["cq"] = t
        return t

    def rope_apply(src, n, dst, done, free):
        for q in (2, 3):
            p = q ^ 1
            t = act(lambda e, q=q, p=p: e.activation(
                ropeX[32 * q:32 * q + 32, 0:n, :], src[32 * p:32 * p + 32, :].rearrange("p (h s) -> p h s", h=n), ACT.Copy),
                done, att2.get("ropefree"), att2["free"])
        t1 = t2 = None
        for h in range(n):
            t1 = dve(lambda e, h=h: e.tensor_tensor(ropeT[64:128, h, :], src[64:128, S * h:S * h + S], cosT[64:128, :], ALU.mult),
                     done, t, att2["rope_in"], att2.get("ropefree"))
            t2 = dve(lambda e, h=h: e.tensor_tensor(ropeU[64:128, h, :], ropeX[64:128, h, :], sinT[64:128, :], ALU.mult),
                     t, att2["rope_in"], att2.get("ropefree"))
        t3 = dve(lambda e: e.tensor_tensor(dst3(dst), ropeT[64:128, 0:n, :], ropeU[64:128, 0:n, :], ALU.add), t1, t2, free)
        att2["ropefree"] = t3
        return t1, t3

    def dst3(d):
        return d if len(d.shape) == 3 else d.rearrange("p (h s) -> p h s", h=1)

    def ckv_evac(reg, done):
        t = act(lambda e: e.activation(CQ[:, 3, :], reg[0][:, 0:S], ACT.Copy), done, att2["free"])
        att2["ckv"] = t
        t1, t3 = rope_apply(reg[0][:, 256:512], 1, krp[64:128, :], [done, t], att2["pad0"])
        att2["kr"] = t3
        return [t, t1]

    sl_ka = declare(W, 0, KT, 1024, 256, [feat(0, 0, 0), tokh(128, 128, 0, 0, 256), tokh(128, 128, 1, 1, 0)], rhs4, ka_evac)
    sl_cq = declare(W, 0, KT, 1280, 384, [feat(0, 0, 0), feat(128, 0, 256), feat(256, 1, 0)], rhs4, cq_evac, per=4)
    sl_ckv = declare(W, 0, KT, 1664, 192, [feat(0, 0, 0), feat(64, 0, 256)], rhs4, ckv_evac)
    sl_qa = [declare(W, 0, KT, 512 * i, 512, FEAT4, rhs4,
                     to_feat(qaT[:, 4 * i:4 * i + 4, :], f"qa{i}", scale=0.125)) for i in range(2)]
    for s_ in (sl_ka, sl_cq, sl_ckv, *sl_qa):
        queue(s_)
    hq = {}

    def uq_evac(j):
        def evac(reg, done):
            ta = act(lambda e: e.activation(qnT[:, 2 * j:2 * j + 2, :],
                                            reg[0][:, :].rearrange("p (m s) -> p m s", m=2), ACT.Copy),
                     done, att2["free"])
            t1, t3 = rope_apply(reg[1][:, :], 2, qrT[64:128, 2 * j:2 * j + 2, :], done, att2["pad0"])
            tk1[f"qm{j}"] = [ta, t3]
            return [ta, t1]
        return evac

    uq = [declare(A["w_uq_2"][0], 0, 3, 384 * j, 384,
                  [feat(0, 0, 0), feat(192, 0, 256), feat(64, 1, 0), feat(256, 1, 256)],
                  lambda k: (CQH[:, k, :], CQL[:, k, :], hq["q"]), uq_evac(j), per=3) for j in range(4)]

    def ukv_evac(j):
        def evac(reg, done):
            ta = act(lambda e: e.activation(knT[:, 2 * j:2 * j + 2, :],
                                            reg[0][:, :].rearrange("p (m s) -> p m s", m=2), ACT.Copy),
                     done, att2["swa_done"])
            tb = act(lambda e: e.activation(vb[:, :, 256 * j:256 * j + 256],
                                            reg[1][:, :].rearrange("p (t c) -> p t c", t=2), ACT.Copy),
                     done, att2["swa_done"])
            tk1[f"km{j}"] = tb
            return tb
        return evac

    def ukv_v(half):
        return ("t%d" % half, lambda v, k: v[:, k, :].rearrange("p (h c) -> p h c", h=2)[:, :, 128:256],
                1, 256 * half, 256)

    ukv = [declare(A["w_ukv_2"][0], 0, 1, 512 * j, 512,
                   [feat(0, 0, 0), feat(256, 0, 256), ukv_v(0), ukv_v(1)],
                   lambda k: (CQH[:, 3, :], CQL[:, 3, :], hq["kv"]), ukv_evac(j), per=1) for j in range(4)]

    for s_ in uq + ukv:
        queue(s_)

    h5, h6 = {}, {}
    out2 = declare_out(A["w_out_2"][0], 0, KT, rhs_of(HI, LO, h5), residual(xb3, mod[:, 32:48], 2), pair=True)
    rhs6 = rhs_of(HI, LO, h6)
    ffn2 = []
    W1, W2 = A["w_ff1_2"][0], A["w_ff2_2"][0]
    parts2 = [(0, 6), (6, 5), (11, 5)]
    for pi, (s0, n) in enumerate(parts2):
        up = [declare(W1, 0, KT, 512 * (s0 + j), 512, FEAT4, rhs6, relu2_evac(4 * j)) for j in range(n)]
        for s_ in up:
            queue(s_)
        down = declare_out(W2, 4 * s0, 4 * n, rhs_of(HIDH, HIDL, hid),
                           residual(xb4, mod[:, 80:96], 5, ssq=pi == len(parts2) - 1))
        ffn2.append((up, down))

    def attention(SPb, PTb, free):
        units, st = [], []
        used = {"SP": [free] * 3, "PTS": [[free, free], [free, free]]}

        def scores(i):
            u = units[i]
            for br, b in enumerate(u["br"]):
                for blk, bk, o, n in ((0, bank[4], 128 * br, 128), (1, bank[5], 256 * br, 256)):
                    pr = b["qk"](blk, n)
                    for j, (l, r_) in enumerate(pr):
                        tk = pe(lambda e, bk=bk, o=o, n=n, l=l, r_=r_, j=j, pr=pr: e.matmul(
                            bk[:, o:o + n], l, r_, start=j == 0, stop=j == len(pr) - 1, skip_group_check=True),
                            [bf[4], bf[5], u["ready"]] if (br, blk, j) == (0, 0, 0) else None,
                            inc=(br, blk, j) == (len(u["br"]) - 1, 1, len(pr) - 1))
            st[i]["S"] = tk

        def softmax1(i):
            u, q = units[i], i % 3
            nb = len(u["br"])
            stt = stat[:, q, :, :]
            ts = []
            for br, b in enumerate(u["br"]):
                for blk in (1, 0):
                    n = 128 * (blk + 1)
                    j = br if blk else 2 + br
                    o = 256 * br if blk else 512 + 128 * br
                    src = bank[5][:, 256 * br:256 * br + 256] if blk else bank[4][:, 128 * br:128 * br + 128]
                    bias = b["bias"] if blk else b["bias"][:, 128:256]
                    least = b["least"](j) if b["least"] else -3.0e38
                    ts.append(dve(lambda e, n=n, j=j, o=o, src=src, bias=bias, b=b, least=least: e.tensor_tensor_reduce(
                        out=SPb[q][:, o:o + n], in0=src, in1=bias, scale=b["scale"], scalar=least,
                        op0=ALU.add, op1=ALU.max, accum_out=stt[:, 0, j:j + 1]),
                        st[i]["S"], used["SP"][q], u["bias_tok"]))
            bf[4] = bf[5] = ts[-1]
            t = dve(lambda e: e.tensor_scalar(stt[:, 1, :], stt[:, 0, :], -1.0, None, ALU.mult), ts) if nb == 2 else \
                dve(lambda e: e.tensor_scalar(stt[:, 1, 0:3:2], stt[:, 0, 0:3:2], -1.0, None, ALU.mult), ts)
            st[i]["nm"] = t
            if u["sink"] is not None:
                st[i]["sk"] = dve(lambda e: e.tensor_tensor(stt[:, 4, :], stt[:, 1, :], u["sink"], ALU.add), t)

        def softmax2(i):
            u, q = units[i], i % 3
            stt = stat[:, q, :, :]
            t = None
            for br in range(len(u["br"])):
                for blk in (1, 0):
                    n = 128 * (blk + 1)
                    j = br if blk else 2 + br
                    o = 256 * br if blk else 512 + 128 * br
                    t = act(lambda e, n=n, j=j, o=o: e.activation(
                        SPb[q][:, o:o + n], SPb[q][:, o:o + n], ACT.Exp, bias=stt[:, 1, j:j + 1],
                        accum_out=stt[:, 2, j:j + 1]), st[i]["nm"])
            if u["sink"] is not None:
                t = act(lambda e: e.activation(stt[:, 5, :], stt[:, 4, :], ACT.Exp), st[i]["sk"])
            st[i]["exp"] = t

        def softmax3(i):
            u, q = units[i], i % 3
            stt = stat[:, q, :, :]
            step = slice(0, 4) if len(u["br"]) == 2 else slice(0, 3, 2)
            t = st[i]["exp"]
            if u["sink"] is not None:
                t = dve(lambda e: e.tensor_tensor(stt[:, 2, :], stt[:, 2, :], stt[:, 5, :], ALU.add), t)
            t = dve(lambda e: e.reciprocal(stt[:, 3, step], stt[:, 2, step]), t)
            if u["gate"] is not None:
                t = dve(lambda e: e.tensor_tensor(stt[:, 3, :], stt[:, 3, :], u["gate"], ALU.mult), t, u["gate_tok"])
            ts = []
            for br in range(len(u["br"])):
                for blk in (1, 0):
                    n = 128 * (blk + 1)
                    j = br if blk else 2 + br
                    o = 256 * br if blk else 512 + 128 * br
                    ts.append(dve(lambda e, n=n, j=j, o=o: e.tensor_scalar(
                        SPb[q][:, o:o + n], SPb[q][:, o:o + n], stt[:, 3, j:j + 1], None, ALU.mult), t))
            st[i]["P"] = ts[-1]

        def turn(i, br):
            u, q, p = units[i], i % 3, i % 2
            for n, (dst, src) in enumerate(((0, 512 + 128 * br), (128, 256 * br), (256, 256 * br + 128))):
                tk = pe(lambda e, dst=dst, src=src: e.transpose(
                    bank[6][:, dst:dst + 128], SPb[q][:, src:src + 128], ident[:, :]),
                    [st[i]["P"], bf[6]], inc=n == 2)
            used["SP"][q] = tk
            t = act(lambda e: e.activation(PTb[p][:, br, :], bank[6][:, 0:384], ACT.Copy), tk, used["PTS"][p][br])
            bf[6] = t
            st[i][f"PT{br}"] = t

        def values(i):
            u, p = units[i], i % 2
            o = bank[7]
            mm = []
            if u["more"] is not None:
                mm.append((o[:, 0:S], *u["more"], u["v_ready"]()))
            for br, b in enumerate(u["br"]):
                mm.append((o[:, 0:S], b["v"](0), PTb[p][:, br, 0:256], [st[i][f"PT{br}"], u["v_ready"]()]))
                mm.append((o[:, 128:S], b["v"](1), PTb[p][:, br, 256:384], None))
            for j, (dst, l, r_, w) in enumerate(mm):
                tk = pe(lambda e, dst=dst, l=l, r_=r_, j=j: e.matmul(
                    dst, l, r_, start=j == 0, stop=j == len(mm) - 1, skip_group_check=True),
                    w, bf[7] if j == 0 else None, inc=j == len(mm) - 1)
            st[i]["O"] = tk
            used["PTS"][p] = [tk, tk]

        def finish(i):
            bf[7] = units[i]["put"](st[i]["O"])

        def steps(new, last):
            lo = len(units)
            units.extend(new)
            st.extend(dict() for _ in new)
            n = len(units)
            for i in range(lo, n + 2 if last else n):
                def s0(i=i):
                    if i < n:
                        scores(i)
                        softmax1(i)
                        softmax2(i)
                yield s0
                for br in range(2):
                    def s1(i=i, br=br):
                        if 0 <= i - 1 < len(units) and br < len(units[i - 1]["br"]):
                            turn(i - 1, br)
                    if len(units[0]["br"]) > br:
                        yield s1

                def s3(i=i):
                    if 0 <= i - 2:
                        values(i - 2)
                        finish(i - 2)
                    if i < n:
                        softmax3(i)
                yield s3

        return steps

    h_tok = {}

    t_rstd = rstd_of(box, D)
    h1["t"] = norm_apply(g_mix, t_cols, t_rstd, None)
    h1["ht"] = [ht_free[0], ht_free[1], sq_free, sr_free]

    zfree = [None]
    cz = {}

    def make_z(kv):
        src = (kcT, vcT)[kv][:, :, :]
        ap0 = list(src.ap[0])
        win = bass.AP(tensor=src.tensor, offset=src.offset, ap=[ap0, [S, 4], [1, 32], [16, 15]])
        ps = posT[:, 32 * kv:32 * kv + 32]
        pos = bass.AP(tensor=ps.tensor, offset=ps.offset, ap=[list(ps.ap[0]), [0, 4], [1, 32], [0, 15]])
        z = Z[:, :, :]
        o = bass.AP(tensor=z.tensor, offset=z.offset, ap=[list(z.ap[0]), [15, 4], [60, 32], [1, 15]])
        t = None
        for g in range(4):
            def sub(a, g=g):
                return bass.AP(tensor=a.tensor, offset=a.offset + g * a.ap[1][0], ap=[list(a.ap[0])] + [list(d) for d in a.ap[2:]])
            t = dve(lambda e, o=sub(o), w=sub(win), q=sub(pos): e.tensor_tensor(o, w, q, ALU.add),
                    tk1["kc" if kv == 0 else "vc"], T["posT"], zfree[0], h1["ht"])
        cz["z"] = t

    def cmp_step(kv, i):
        def go():
            if i == 0:
                make_z(kv)
            w = A["cmp_w1_k" if kv == 0 else "cmp_w1_v"][0]
            src = w[i * 1024:(i + 1) * 1024, :].rearrange("(l p) n -> p l n", p=128)
            raw, landed, slot = load(lambda t: t[:, :].rearrange("p (l n) -> p l n", l=8), src)
            rv = raw[:, :].rearrange("p (l n) -> p l n", l=8)
            for l in range(8):
                for m in range(2):
                    tk = pe(lambda e, l=l, m=m: e.matmul(
                        bank[4][:, 60 * m:60 * m + 60], rv[:, l, 128 * m:128 * m + 128], Z[:, 8 * i + l, :],
                        start=(i, l, m) == (0, 0, 0), stop=(i, l) == (3, 7), skip_group_check=True),
                        [landed, cz["z"], bf[4]] if (l, m) == (0, 0) else None, inc=(l, m) == (7, 1))
            raw_free[slot] = tk
            if i == 3:
                zfree[0] = tk
                t = act(lambda e: e.activation(hidT[:, kv, :, :], bank[4][:, 0:120].rearrange("p (m c) -> p m c", m=2),
                                               ACT.Gelu_apprx_tanh), tk)
                bf[4] = t
                cz[f"hid{kv}"] = t
        return go

    cmps = [cmp_step(0, i) for i in range(4)] + [cmp_step(1, i) for i in range(4)]
    def compressed():
        for k in range(2):
            tk = pe(lambda e, k=k: e.matmul(bank[4][:, 128:188], w2[:, 0, k, :], hidT[:, 0, k, :], start=k == 0,
                                            stop=k == 1, skip_group_check=True),
                    [w2_in, cz["hid0"], cz["hid1"], bf[4]], inc=k == 1)
        cz["kcc"] = bf[4] = act(lambda e: e.activation(kccT[:, :], bank[4][:, 128:188], ACT.Copy), tk)
        for g in range(4):
            for k in range(2):
                tk = pe(lambda e, g=g, k=k: e.matmul(
                    bank[5][0:15, 128 * g:128 * g + 128], hidT[:, 1, k, 15 * g:15 * g + 15],
                    w2[:, 1, k, :], start=k == 0, stop=k == 1, skip_group_check=True),
                    bf[5], inc=(g, k) == (3, 1))
        t_vz = dve(lambda e: e.memset(Vpad[:, :, :], 0.0), h1["ht"])
        t_vp = None
        for g in range(4):
            for j in range(4):
                t_vp = dve(lambda e, g=g, j=j: e.tensor_copy(Vpad[32 * j:32 * j + 15, 4 * g + j, :],
                                                             bank[5][0:15, 128 * g:128 * g + 128]), tk, t_vz)
        cz["vp"] = bf[5] = t_vp
        cz["pc0"] = dve(lambda e: e.memset(Pc[:, :, :, :], 0.0), zfree[0])

    def spread(a):
        return bass.AP(tensor=a.tensor, offset=a.offset, ap=[list(d) for d in a.ap] + [[0, 15]])

    def cmp_scores(g):
        for b in range(2):
            for i in range(4):
                n = 15 * (4 * b + i)
                tk = pe(lambda e, b=b, n=n, h=4 * g + i: e.matmul(
                    bank[6][:, n:n + 15], qT[:, h, 128 * b:128 * b + 128], kccT[:, 15 * g:15 * g + 15],
                    start=n == 0, stop=True, skip_group_check=True),
                    [cz["kcc"], tk1[f"q{g}"], bf[6]], inc=(b, i) == (1, 3))
        pv = [Pc[:, b, :, 0:15] for b in range(2)]
        cv = cmpb[:, :, :].rearrange("p (b h) c -> p b h c", b=2)[:, :, 4 * g:4 * g + 4, :]
        c4 = cst[:, :, :].rearrange("p r (b h) -> p r b h", b=2)[:, :, :, 4 * g:4 * g + 4]
        t = [dve(lambda e, b=b: e.tensor_tensor(
            pv[b], bank[6][:, 60 * b:60 * b + 60].rearrange("p (h c) -> p h c", c=15), cv[:, b, :, :], ALU.add),
            tk, cz["pc0"], cz.get("turned"), T["cmpb"]) for b in range(2)]
        bf[6] = t
        t = [dve(lambda e, b=b: e.tensor_reduce(c4[:, 0, b, :], pv[b], AX_X, ALU.max), t[b]) for b in range(2)]
        t = dve(lambda e: e.tensor_scalar(c4[:, 1, :, :], c4[:, 0, :, :], -1e29, None, ALU.max), t)
        t = [dve(lambda e, b=b: e.tensor_tensor(pv[b], pv[b], spread(c4[:, 1, b, :]), ALU.subtract), t) for b in range(2)]
        t = [act(lambda e, b=b: e.activation(pv[b], pv[b], ACT.Exp), t[b]) for b in range(2)]
        t = [dve(lambda e, b=b: e.tensor_reduce(c4[:, 2, b, :], pv[b], AX_X, ALU.add), t[b]) for b in range(2)]
        t = dve(lambda e: e.tensor_scalar(c4[:, 0, :, :], c4[:, 2, :, :], 1e-30, None, ALU.max), t)
        t = dve(lambda e: e.reciprocal(c4[:, 3, :, :], c4[:, 0, :, :]), t)
        t = dve(lambda e: e.tensor_tensor(c4[:, 1, :, :], c4[:, 3, :, :],
                                          gates[:, 0, 4 * g:4 * g + 4, 0:2].rearrange("p h b -> p b h"), ALU.mult),
                t, tk1["gates"])
        cz[f"p{g}"] = [dve(lambda e, b=b: e.tensor_tensor(pv[b], pv[b], spread(c4[:, 1, b, :]), ALU.mult), t)
                       for b in range(2)]

    def cmp_turn(g):
        for b in range(2):
            tk = pe(lambda e, b=b: e.transpose(
                bank[6][:, 128 * b:128 * b + 128], Pc[:, b, :, :], ident[:, :]),
                cz[f"p{g}"], bf[6], inc=b == 1)
        cz["turned"] = tk
        cz[f"pct{g}"] = bf[6] = act(lambda e: e.activation(PcT[:, g, :], bank[6][:, 0:256], ACT.Copy), tk, h1["ht"])

    extra["gemv"] = 0.6
    run(nsa[0], nsa[1])
    drain()
    extra["every"].extend(cmps)
    run(*nsa[2:7])
    assert not extra["every"]
    side.append(compressed)
    run(nsa[7])
    drain()
    ready1 = [tk1["ks"], tk1["kw"]]

    def unit1(h):
        g = h // 4

        def br(kT, v):
            return dict(qk=lambda blk, n: [(qT[:, h, 128 * blk:128 * blk + 128], kT[:, g, 0:n])],
                        bias=biasA[:, h, :], scale=1.0, least=None,
                        v=lambda k: v[:, k, 128 * g:128 * g + 128])
        return dict(br=[br(ksT, vs), br(kwT, vw)], ready=[ready1, tk1[f"q{g}"]],
                    v_ready=lambda: [tk1["vs"], tk1["vw"], cz["vp"], cz[f"pct{g}"]],
                    bias_tok=T["biasA"], sink=None, gate=gates[:, 1, h, :], gate_tok=tk1["gates"],
                    more=(Vpad[:, h, :], PcT[:, g, :]), put=put1(h))

    def split4(HIs, LOs, src, k, toks, *waits):
        t_hi = act(lambda e: e.activation(HIs[:, k:k + 4, :], src, ACT.Copy), *waits)
        t_lo = dve(lambda e: e.tensor_tensor(LOs[:, k:k + 4, :], src, HIs[:, k:k + 4, :].bitcast(F32), ALU.subtract),
                   t_hi, *waits)
        toks["t"][k // 4] = [t_hi, t_lo]

    def collect(buf, toks, read):
        got, ready = {}, []

        def put(k):
            def go(o_tok):
                t = act(lambda e: e.activation(buf[:, k, :], bank[7][:, 0:S], ACT.Copy), o_tok)
                got[k] = t
                att["O"] = o_tok
                if k % 4 == 3:
                    ready.append(k - 3)
                    flush()
                return t
            return go

        def flush():
            while ready and "done" in read:
                k = ready.pop(0)
                split4(HI, LO, buf[:, k:k + 4, :], k, toks, [got[k + i] for i in range(4)], read["done"])
                if toks is h2 and k == 12:
                    first_block_over()
        return put, flush

    att = {}
    h2["t"] = [None] * 4
    nsa_read = {}

    def first_block_over():
        free = [att["O"], h2["t"]]
        sq_free[:] = [free, free]
        sr_free[:] = [[sr_free[0], free], [sr_free[1], free]]
        ht_free[:] = [[ht_free[0], free], [ht_free[1], free]]
        hid["free"] = hid["ufree"] = free

    put1, flush1 = collect(qT, h2, nsa_read)
    steps1 = attention(SP1, PT1, [zfree[0], tk1["kc"], tk1["vc"], cz["z"]])
    extra["rate"] = 1.15
    extra["gemv"] = 0.4
    for g in range(4):
        side.extend([lambda g=g: cmp_scores(g), lambda g=g: cmp_turn(g)])
        side.extend(steps1([unit1(h) for h in range(4 * g, 4 * g + 4)], g == 3))
        if g < 3:
            run(nsa[8 + g])
    nsa_read["done"] = chunk_done[cursor[0] - 1]
    flush1()
    xb1["free"] = rstd_free[0]
    run(out1[0], out1[1])
    drain()
    extra["gemv"] = 0.6
    run(out1[2], out1[3])
    out1_done = chunk_done[cursor[0] - 1]
    pe_later()

    t_rstd = rstd_of(xb1["box"], D)
    h3["t"] = norm_apply(g_ffn, t_cols, t_rstd, out1_done)
    hid["free"] = [out1_done, hid["free"]]
    xb2["free"] = rstd_free[0]
    for pi, (up, down) in enumerate(ffn1):
        run(*up)
        run(*down)
        hid["free"] = chunk_done[cursor[0] - 1]
    ffn1_done = chunk_done[cursor[0] - 1]
    extra["gemv"] = 0.0
    pe_later()
    while True:
        f = next(gq_iter, 0)
        if f == 0:
            break
        if f is not None:
            f()
        pe_later()

    t_rstd = rstd_of(xb2["box"], D)
    boxes = None
    for b in range(4):
        for i in range(4):
            m = 4 * b + i
            t = dve(lambda e, m=m: e.scalar_tensor_tensor(xT[:, m, :], xT[:, m, :], g_fin[:, m:m + 1], rstd[:, :],
                                                          ALU.mult, ALU.mult), t_rstd, xb2["x"])
        boxes = ssq_add(4 * b, t, b == 0, b == 3, now=True)
    rstd_free[0] = t
    tg = [dve(lambda e, o=o, g=g, c=c: e.scalar_tensor_tensor(o[:, :], mod[:, c:c + 16], 1.0, g, ALU.add, ALU.mult),
              mod_tok, t_cols) for o, g, c in ((G1c, g_att2, 16), (G2c, g_mlp2, 64))]
    t_rstd = rstd_of(boxes, D)
    h4["t"] = norm_apply(G1c, tg, t_rstd, ffn1_done, shcol=mod[:, 0:16])

    att2["free"] = [ffn1_done, h4["t"], hid["t"], sq_free, sr_free, ht_free, acc_free[0]]
    L_rope = Landing(sem("l_rope"))
    L_rope.start(pool, cosT[:, :], A["c_cos"], att2["free"])
    L_rope.start(pool, causal[:, :], A["c_causal"], att2["free"])
    att2["rope_in"] = L_rope.start(pool, sinT[:, :], A["c_sin"], att2["free"])
    biasB_in = L_bB.start(pool, biasB[:, :, :], toeplitz(toepB), T["tB"], att2["free"])
    att2["pad0"] = [dve(lambda e, t_=t_: e.memset(t_, 0.0), att2["free"]) for t_ in
                    (Kpad[:, :, :, :], Vpad2[:, :, :, :, :], krp[0:64, :], qrT[0:64, :, :])]
    t_sk = None
    for j in range(4):
        t_sk = dve(lambda e, j=j: e.tensor_copy(SK[:, :, j], sinkr[:, j % 2:16:2]), k_in)

    def latent(ms, name, n, gcols, ready):
        a, b = ms[0], ms[-1] + 1
        sq_t = act(lambda e: e.activation(CSQ[:, a:b, :], CQ[:, a:b, :], ACT.Square), ready, att2["free"])

        def go():
            for j, m in enumerate(ms):
                tk = pe(lambda e, m=m, j=j: e.matmul(ss, ones[:, :], CSQ[:, m, :], start=j == 0, stop=j == len(ms) - 1,
                                                     skip_group_check=True), [sq_t, bf[6]], inc=j == len(ms) - 1)
            tr = rstd_of({"tok": tk}, n)
            for j, m in enumerate(ms):
                t = dve(lambda e, m=m, j=j: e.scalar_tensor_tensor(CQ[:, m, :], CQ[:, m, :], gcols[:, j:j + 1],
                                                                   rstd[:, :], ALU.mult, ALU.mult), tr, sq_t)
            rstd_free[0] = t
            t_hi = act(lambda e: e.activation(CQH[:, a:b, :], CQ[:, a:b, :], ACT.Copy), t, att2["free"])
            t_lo = dve(lambda e: e.tensor_tensor(CQL[:, a:b, :], CQ[:, a:b, :], CQH[:, a:b, :].bitcast(F32),
                                                 ALU.subtract), t, t_hi, att2["free"])
            hq[name] = [t_hi, t_lo]
        later.append(go)

    run(sl_ka, sl_cq)
    latent([0, 1, 2], "q", 384, gq, att2["cq"])
    run(sl_ckv)
    latent([3], "kv", 128, gkv, att2["ckv"])
    run(sl_qa[0])

    h5["t"] = [None] * 4
    in2_read = {}
    put2, flush2 = collect(qaT, h5, in2_read)
    h_tok = {}

    def put3(k):
        def go(o_tok):
            t_hi = act(lambda e: e.activation(HI[:, k, :], bank[7][:, 0:S], ACT.Copy), o_tok, in2_read["done"])
            t_lo = dve(lambda e: e.tensor_tensor(LO[:, k, :], bank[7][:, 0:S], HI[:, k, :].bitcast(F32),
                                                 ALU.subtract), t_hi, o_tok, in2_read["done"])
            h_tok[k] = [t_hi, t_lo]
            att["O"] = o_tok
            if k % 4 == 3:
                h5["t"][k // 4] = [h_tok[k - i] for i in range(4)]
            if k == 15:
                second_block_over()
            return [t_hi, t_lo]
        return go

    def second_block_over():
        free = [att["O"], h5["t"], att2["ropefree"]]
        sq_free[:] = [free, free]
        sr_free[:] = [[sr_free[0], free], [sr_free[1], free]]
        ht_free[:] = [[ht_free[0], free], [ht_free[1], free]]
        sa_tok[:] = [[sa_tok[0], free], [sa_tok[1], free]]
        hid["free"] = free

    steps2 = attention(SP2, PT2, [hq["q"], hq["kv"], att2["free"]])

    def unit2(i):
        kv = i // 4

        def br(par):
            return dict(qk=lambda blk, n: [(qaT[:, i, 128 * blk:128 * blk + 128], Kpad[:, kv, par, 0:n])],
                        bias=biasB[:, 2 * i + par, :], scale=1.0, least=lambda j: SK[:, i, j:j + 1],
                        v=lambda k: Vpad2[:, kv, par, k, :])
        return dict(br=[br(0), br(1)], ready=[tk1[f"qa{kv}"], att2["kv"], att2["pad0"]], v_ready=lambda: att2["kv"],
                    bias_tok=[biasB_in, t_sk], sink=SK[:, i, :], gate=None, gate_tok=None, more=None, put=put2(i))

    def unit3(h):
        b = dict(qk=lambda blk, n: [(qnT[:, h, 128 * blk:128 * blk + 128], knT[:, h, 0:n]),
                                    (qrT[:, h, 128 * blk:128 * blk + 128], krp[:, 0:n])],
                 bias=causal[:, :], scale=192.0 ** -0.5, least=None,
                 v=lambda k: vb[:, k, 128 * h:128 * h + 128])
        return dict(br=[b], ready=[tk1[f"qm{h // 2}"], tk1[f"km{h // 2}"], att2["kr"]],
                    v_ready=lambda: tk1[f"km{h // 2}"], bias_tok=att2["rope_in"], sink=None, gate=None,
                    gate_tok=None, more=None, put=put3(8 + h))

    extra["rate"] = 1.15
    side.extend(steps2([unit2(i) for i in range(4)], False))
    run(sl_qa[1])
    in2_read["done"] = chunk_done[cursor[0] - 1]
    side.extend(steps2([unit2(i) for i in range(4, 8)], False))
    run(*uq)
    drain()
    att2["swa_done"] = bf[5]
    run(*ukv)
    extra["rate"] = 1.5
    side.extend(steps2([unit3(h) for h in range(8)], True))
    xb3["free"] = rstd_free[0]
    run(out2[0], out2[1])
    drain()
    run(out2[2], out2[3])
    out2_done = chunk_done[cursor[0] - 1]
    pe_later()

    t_rstd = rstd_of(xb3["box"], D)
    h6["t"] = norm_apply(G2c, tg, t_rstd, out2_done, shcol=mod[:, 48:64])
    hid["free"] = [out2_done, hid["free"]]
    xb4["free"] = rstd_free[0]
    for pi, (up, down) in enumerate(ffn2):
        run(*up)
        run(*down)
        hid["free"] = chunk_done[cursor[0] - 1]
    ffn2_done = chunk_done[cursor[0] - 1]
    pe_later()

    t_rstd = rstd_of(xb4["box"], D)
    L_out = Landing(sem("l_out"))
    y_free = [region_free[0], region_free[0], region_free[1], region_free[1]]
    y_tok = None
    out_rows = out[0].rearrange("(t p) d -> p t d", p=128)
    for m0 in range(0, KT, 4):
        for i in range(4):
            m = m0 + i
            t = dve(lambda e, m=m: e.scalar_tensor_tensor(xT[:, m, :], xT[:, m, :], g_fin2[:, m:m + 1], rstd[:, :],
                                                          ALU.mult, ALU.mult), t_rstd, xb4["x"])
        ys = []
        for h in range(2):
            i = (m0 // 4 * 2 + h) % 4
            for j in range(4):
                tk = pe(lambda e, i=i, j=j, m=m0 + j, h=h: e.transpose(
                    bank[i][:, 128 * j:128 * j + 128], xT[:, m, 128 * h:128 * h + 128], ident[:, :]),
                    t, y_free[i], inc=j == 3)
            dst = YROW[:, h, 128 * m0:128 * m0 + 512]
            if h == 0:
                ty = act(lambda e, dst=dst, i=i: e.activation(dst, bank[i][:, :], ACT.Copy), tk, ffn2_done)
            else:
                ty = dve(lambda e, dst=dst, i=i: e.tensor_copy(dst, bank[i][:, :]), tk, ffn2_done)
            y_free[i] = ty
            ys.append(ty)
        y_tok = L_out.start(sp, out_rows[:, :, 128 * m0:128 * m0 + 512], YROW[:, :, 128 * m0:128 * m0 + 512], ys)

    assert cursor[0] == len(chunks)

    with nc.Block() as block:
        @block.tensor
        def _(e):
            pe.play(e)

        @block.scalar
        def _(e):
            act.play(e)

        @block.vector
        def _(e):
            dve.play(e)

        @block.gpsimd
        def _(e):
            pool.play(e)

        @block.sync
        def _(e):
            sp.play(e)
            e.wait_ge(*T["tA"])
            e.wait_ge(*T["tB"])
            e.wait_ge(*y_tok)


def kernel(**inputs):
    import concourse.bacc as _bacc
    from concourse.bass_utils import run_bass_kernel_spmd as _run

    nc = _bacc.Bacc("TRN2", target_bir_lowering=False, num_devices=1)
    arrays = {n: np.ascontiguousarray(inputs[n]) for n in IN_NAMES}
    arrays.update(shape_constants())
    A = {}
    for name, a in arrays.items():
        A[name] = nc.dram_tensor(f"in_{name}", a.shape, F32, kind="ExternalInput").ap()
    out = nc.dram_tensor("out_y", (1, S, D), F32, kind="ExternalOutput").ap()
    build(nc, A, out)
    r = _run(nc, [{f"in_{n}": a for n, a in arrays.items()}], core_ids=[0])
    return r.results[0]["out_y"]
```

```python
import math
from collections import deque

import numpy as np

import concourse.bass as bass
from concourse import mybir

F32 = mybir.dt.float32
F32R = mybir.dt.float32r
ALU = mybir.AluOpType
ACT = mybir.ActivationFunctionType
AX_X = mybir.AxisListType.X

S = 256
D = 2048
KT = D // 128
FF1 = 5632
FF2 = 8192
NEG = -1e30
EPS = 1e-6
NRAW = 4
KB = 1024
BASE = 16 * KB + 128

IN_NAMES = [
    "x", "rel_bias", "mix_norm_g", "ffn_norm_g", "final_norm_g", "nsa_w_in", "nsa_w_out",
    "cmp_pos_k", "cmp_w1_k", "cmp_w2_k", "cmp_pos_v", "cmp_w1_v", "cmp_w2_v", "ffn_w_in", "ffn_w_out",
    "c_2", "w_mod_2", "b_mod_2", "attn_norm_g_2", "w_in_2", "swa_sinks_2", "rel_bias_2",
    "mla_q_norm_g_2", "w_uq_2", "mla_kv_norm_g_2", "w_ukv_2", "w_out_2", "mlp_norm_g_2",
    "w_ff1_2", "w_ff2_2", "final_norm_g_2",
]


def shape_constants():
    n = np.arange(0, 256)
    large = 16 + (np.log(np.maximum(n, 1).astype(np.float32) / np.float32(16))
                  / np.float32(math.log(128 / 16)) * np.float32(16)).astype(np.int32)
    bucket = np.where(n < 16, n, np.minimum(large, 31))

    def onehot(dist, far):
        t = np.zeros((33, len(dist)), np.float32)
        for i, d in enumerate(dist):
            if 0 <= d < far:
                t[bucket[d], i] = 1.0
            else:
                t[32, i] = 1.0
        return t

    down = np.clip(255 - np.arange(384), -127, 255)
    oh = np.concatenate([onehot(down, 256), onehot(down, 128)], axis=1)
    inv = (10000.0 ** (-np.arange(32, dtype=np.float32) / np.float32(32))).astype(np.float32)
    ang = inv[:, None] * np.arange(S, dtype=np.float32)[None, :]
    cos, sin = np.cos(ang).astype(np.float32), np.sin(ang).astype(np.float32)
    t = np.arange(128)[:, None]
    j = np.arange(256)[None, :]
    return {
        "c_ident": np.eye(128, dtype=np.float32),
        "c_onehot": oh,
        "c_cos": np.concatenate([cos] * 4, axis=0),
        "c_sin": np.concatenate([-sin, sin, -sin, sin], axis=0),
        "c_causal": np.where(128 + t - j >= 0, 0.0, NEG).astype(np.float32),
    }


def flat(waits):
    for w in waits:
        if w is None:
            continue
        if isinstance(w, list):
            yield from flat(w)
        else:
            yield w


class Queue:

    def __init__(self, sem):
        self.sem, self.n, self.ops = sem, 0, []

    def __call__(self, fn, *waits, inc=True):
        self.n += inc
        self.ops.append((fn, list(flat(waits)), inc))
        return (self.sem, self.n) if inc else None

    def play(self, eng):
        seen = {}
        for fn, waits, inc in self.ops:
            need = {}
            for sem, v in waits:
                if v > seen.get(sem.num, 0) and v > need.get(sem.num, (sem, 0))[1]:
                    need[sem.num] = (sem, v)
            for num, (sem, v) in need.items():
                eng.wait_ge(sem, v)
                seen[num] = v
            ins = fn(eng)
            if inc:
                ins.then_inc(self.sem, 1)


class Landing:

    def __init__(self, sem):
        self.sem, self.n = sem, 0

    def start(self, q, dst, src, *waits):
        self.n += 16
        q(lambda e: e.dma_start(dst, src).then_inc(self.sem, 16), *waits, inc=False)
        return (self.sem, self.n)


def build(nc, A, out):
    sems = [0]

    def sem(name):
        sems[0] += 1
        return nc.alloc_semaphore(name)

    at = [BASE]

    def sb(name, shape, dt=F32, offset=None):
        size = int(np.prod(shape[1:])) * 4
        if offset is None:
            offset = at[0]
            at[0] += (size + 31) // 32 * 32
        return nc.alloc_sbuf_tensor_at("m_" + name, shape, dt, offset=offset)

    pe, act, dve = Queue(sem("s_pe")), Queue(sem("s_act")), Queue(sem("s_dve"))
    pool, sp = Queue(sem("s_pool")), Queue(sem("s_sp"))

    xT = sb("xT", [128, KT, S])
    HI = sb("HI", [128, KT, S], F32R)
    LO = sb("LO", [128, KT, S], F32R)
    RAW = [sb(f"RAW{i}", [128, 2048]) for i in range(NRAW)]
    WHI = [sb(f"WHI{i}", [128, 1024], F32R) for i in range(4)]
    WLO = [sb(f"WLO{i}", [128, 1024], F32R) for i in range(4)]
    acc_at = at[0]
    ACC = sb("ACC", [128, 2048])
    ident = sb("ident", [128, 128])
    ones = sb("ones", [128, 128])
    cols = sb("cols", [128, 116])
    cact = sb("cact", [128, 16])
    bmod = sb("bmod", [128, 96])
    mod = sb("mod", [128, 96])
    G1c = sb("G1c", [128, 16])
    G2c = sb("G2c", [128, 16])
    G12 = sb("G12", [128, 16])
    gates = sb("gates", [128, 3, 16, 4])
    rstd = sb("rstd", [128, S])
    std = sb("std", [128, S])
    w2 = sb("w2", [128, 2, 2, 128])
    hidT = sb("hidT", [128, 2, 2, 60])
    kccT = sb("kccT", [128, 60])
    posT = sb("posT", [128, 64])
    epsc = sb("epsc", [128, 1])
    eps2c = sb("eps2c", [128, 1])
    sinkr = sb("sinkr", [128, 16])
    SK = sb("SK", [128, 8, 4])
    rela = sb("rela", [33, 16])
    relb = sb("relb", [33, 16])
    stat = sb("stat", [128, 3, 6, 4])
    cst = sb("cst", [128, 4, 32])
    rstdc = sb("rstdc", [128, 2])
    stdc = sb("stdc", [128, 2])
    gmix = sb("gmix", [128, 16])
    spare = sb("spare", [128, 1])
    R16b = sb("R16b", [16, 384])
    U = at[0]
    assert U + 76 * KB <= 229344, (U, 229344 - U)

    def un(name, shape, kb, dt=F32):
        return sb(name, shape, dt, offset=U + int(kb * KB))

    XROW = un("XROW", [128, 2, D], 0)
    OH = un("OH", [33, 768], 16)
    rowsA = un("rowsA", [116, 128], 21)
    rowsM = un("rowsM", [16, 128], 22.5)
    rowsB = un("rowsB", [96, 128], 21.5)
    rowsP = un("rowsP", [64, 128], 22)
    R16a = un("R16a", [16, 384], 24)
    qT = un("qT", [128, 16, S], 0)
    ksT = un("ksT", [128, 4, S], 16)
    kwT = un("kwT", [128, 4, S], 20)
    vs = un("vs", [128, 2, 512], 24)
    vw = un("vw", [128, 2, 512], 28)
    biasA = un("biasA", [128, 16, S], 32)
    Vpad = un("Vpad", [128, 16, 128], 48)
    glT = un("glT", [128, S], 56)
    PcT = un("PcT", [128, 4, S], 56)
    kcT = un("kcT", [128, 4, S], 60)
    vcT = un("vcT", [128, 4, S], 64)
    Z = un("Z", [128, 32, 60], 68)
    SP1 = [un(f"SP1_{i}", [128, 768], 60 + 3 * i) for i in range(3)]
    PT1 = [un(f"PT1_{i}", [128, 2, 384], 69 + 3 * i) for i in range(2)]
    Pc = un("Pc", [128, 2, 4, 32], 75)
    HIDH = un("HIDH", [128, 24, S], 0, F32R)
    HIDL = un("HIDL", [128, 24, S], 24, F32R)
    H3H = un("H3H", [128, 16, S], 0, F32R)
    H3L = un("H3L", [128, 16, S], 16, F32R)
    HXH = un("HXH", [128, 8, S], 32, F32R)
    HXL = un("HXL", [128, 8, S], 40, F32R)
    SA = [un(f"SA{i}", [128, 4, S], 48 + 4 * i) for i in range(2)]
    HT = [un(f"HT{i}", [128, 4, S], 56 + 4 * i) for i in range(2)]
    SQ = [un(f"SQ{i}", [128, 4, S], 64 + 4 * i) for i in range(2)]
    std2, rstd2 = un("std2", [128, S], 74), un("rstd2", [128, S], 75)
    SR = [un(f"SR{i}", [128, S], 72 + i) for i in range(2)]
    qaT = un("qaT", [128, 8, S], 0)
    Kpad = un("Kpad", [128, 2, 2, S], 8)
    Vpad2 = un("Vpad2", [128, 2, 2, 2, 128], 12)
    CQH = un("CQH", [128, 4, S], 16, F32R)
    CQL = un("CQL", [128, 4, S], 20, F32R)
    krp = un("krp", [128, S], 24)
    SP2 = [un(f"SP2_{i}", [128, 768], 64 + 3 * i) for i in range(3)]
    PT2 = [un("PT2_0", [128, 2, 384], 73), un("PT2_1", [128, 2, 384], 25)]
    ropeX, ropeT, ropeU = [sb(n, [128, 2, S], offset=acc_at + 2 * KB * i) for i, n in enumerate(("ropeX", "ropeT", "ropeU"))]
    vT2 = un("vT2", [128, S], 31)
    causal = un("causal", [128, S], 28)
    cosT = un("cosT", [128, S], 29)
    sinT = un("sinT", [128, S], 30)
    biasB = un("biasB", [128, 16, S], 32)
    CQ = un("CQ", [128, 4, S], 48)
    CSQ = un("CSQ", [128, 4, S], 52)
    qnT = un("qnT", [128, 8, S], 48)
    qrT = un("qrT", [128, 8, S], 56)
    knT = un("knT", [128, 8, S], 32)
    vb = un("vb", [128, 2, 1024], 40)
    YROW = un("YROW", [128, 2, D], 48)
    XG = [un(f"XG{i}", [128, 4, S], 20 + 24 * i) for i in range(2)]

    bank = [nc.alloc_psum_tensor(f"bank{i}", [128, 512], F32) for i in range(8)]
    region = [(bank[0], bank[1]), (bank[2], bank[3])]

    toepA = nc.dram_tensor("toepA", [16, 128, 384], F32, kind="Internal").ap()
    toepB = nc.dram_tensor("toepB", [16, 128, 384], F32, kind="Internal").ap()

    L_x = [Landing(sem(f"l_x{i}")) for i in range(4)]
    L_c, L_k = Landing(sem("l_c")), Landing(sem("l_k"))
    L_rows, L_rowP = Landing(sem("l_rows")), Landing(sem("l_rowP"))
    L_mix = Landing(sem("l_mix"))
    L_w2 = Landing(sem("l_w2"))
    x_rows = A["x"][0].rearrange("(t p) d -> p t d", p=128)
    c_in = L_c.start(act, ident[:, :], A["c_ident"])
    mix_in = L_mix.start(act, rowsM[:, :], A["mix_norm_g"][0].rearrange("(r c) -> r c", c=128))
    ones_set = dve(lambda e: e.memset(ones[:, :], 1.0))
    act(lambda e: e.activation(spare[:, :], ones[:, 0:1], ACT.Square), ones_set)
    x_in = [L_x[i].start(sp, XROW[:, :, 512 * i:512 * i + 512], x_rows[:, :, 512 * i:512 * i + 512]) for i in range(4)]
    r = 0
    for name in ("mix_norm_g", "ffn_norm_g", "final_norm_g", "attn_norm_g_2", "mlp_norm_g_2",
                 "final_norm_g_2", "c_2", "mla_q_norm_g_2", "mla_kv_norm_g_2"):
        a = A[name]
        v = a if len(a.shape) == 1 else a[0]
        n = v.shape[0] // 128
        rows_in = L_rows.start(pool, rowsA[r:r + n, :], v.rearrange("(r c) -> r c", c=128))
        r += n
    L_k.start(pool, OH[:, :], A["c_onehot"])
    L_k.start(pool, rela[0:32, :], A["rel_bias"])
    L_k.start(pool, relb[0:32, :], A["rel_bias_2"])
    sk = A["swa_sinks_2"][0]
    k_in = L_k.start(pool, sinkr[:, :], bass.AP(tensor=sk.tensor, offset=sk.offset, ap=[[0, 128], [1, 16]]))
    L_rowP.start(pool, rowsB[:, :], A["b_mod_2"][0].rearrange("(r c) -> r c", c=128))
    L_rowP.start(pool, rowsP[0:32, :], A["cmp_pos_k"][0])
    rowP_in = L_rowP.start(pool, rowsP[32:64, :], A["cmp_pos_v"][0])
    L_w2.start(pool, w2[:, 0, :, :], A["cmp_w2_k"][0].rearrange("(k p) n -> p k n", p=128))
    w2_in = L_w2.start(pool, w2[:, 1, :, :], A["cmp_w2_v"][0].rearrange("(k p) n -> p k n", p=128))

    dve(lambda e: e.memset(eps2c[:, :], EPS * EPS))
    eps_set = dve(lambda e: e.memset(epsc[:, :], EPS))
    relm = [dve(lambda e, t=t: e.memset(t[32:33, :], NEG)) for t in (rela, relb)]

    L_raw = [Landing(sem(f"l_raw{i}")) for i in range(NRAW)]
    raw_free = [None] * NRAW
    n_loads = [0]

    def load(view, src):
        slot = n_loads[0] % NRAW
        n_loads[0] += 1
        tok = L_raw[slot].start(sp, view(RAW[slot]), src, raw_free[slot])
        return RAW[slot], tok, slot

    slabs, chunks = [], []
    bf = {b: None for b in range(4, 8)}

    def slab(w, row0, kts, c0, ncol, groups, rhs, evac, per=None):
        per = per or max(1, min(8, 2048 // ncol))
        s = dict(w=w, row0=row0, c0=c0, nc=ncol, groups=groups, rhs=rhs, evac=evac, reg=len(slabs) % 2, opened=set())
        slabs.append(s)
        s["list"] = [(s, k, min(per, kts - k), k + per >= kts) for k in range(0, kts, per)]
        return s

    def queue(*together):
        for i in range(max(len(s["list"]) for s in together)):
            chunks.extend(s["list"][i] for s in together if i < len(s["list"]))

    def feat(c, b, off):
        return ("f", lambda v, k: v[:, k, c:c + 128], b, off, S)

    def tokh(c, n, half, b, off):
        return ("t%d" % half, lambda v, k: v[:, k, c:c + n], b, off, n)

    FEAT4 = [feat(128 * i, i // 2, 256 * (i % 2)) for i in range(4)]
    TOK512 = [tokh(0, 512, 0, 0, 0), tokh(0, 512, 1, 1, 0)]

    parts, split_tok, part_done, chunk_done = [], [], [], {}
    chunk_raw = {}

    def split():
        u = len(split_tok)
        while u >= len(parts):
            n = parts[-1][0] + 1 if parts else 0
            if n >= len(chunks):
                return
            nk = chunks[n][2]
            h = (nk + 1) // 2
            parts.extend((n, a, z) for a, z in ((0, h), (h, nk)) if z > a)
        n, a, z = parts[u]
        s, k, nk, _ = chunks[n]
        ncol = s["nc"]
        if a == 0:
            src = s["w"][(s["row0"] + k) * 128:(s["row0"] + k + nk) * 128, :]
            src = src[:, s["c0"]:s["c0"] + ncol].rearrange("(k p) n -> p k n", p=128)
            chunk_raw[n] = load(lambda t: t[:, 0:nk * ncol].rearrange("p (k n) -> p k n", k=nk), src)
        raw, landed, slot = chunk_raw[n]
        hi, lo, m = WHI[u % 4], WLO[u % 4], (z - a) * ncol
        part = raw[:, a * ncol:z * ncol]
        free = part_done[u - 4] if u >= 4 else None
        t_hi = act(lambda e: e.activation(hi[:, 0:m], part, ACT.Copy), landed, free)
        t_lo = dve(lambda e: e.tensor_tensor(lo[:, 0:m], part, hi[:, 0:m].bitcast(F32), ALU.subtract),
                   landed, free, t_hi)
        raw_free[slot] = [t_hi, t_lo]
        split_tok.append([t_hi, t_lo])

    region_free = [None, None]
    later = []
    side = deque()
    cursor = [0]
    extra = {"every": [], "rate": 1, "gemv": 0.0, "credit": 0.0, "due": 0.0}

    def pe_later():
        todo = later[:]
        later.clear()
        for f in todo:
            f()

    def tick():
        extra["due"] += extra["rate"]
        while extra["due"] >= 1:
            extra["due"] -= 1
            if side:
                side.popleft()()

    def pause():
        pass

    def drain():
        while side:
            side.popleft()()

    def run_chunk():
        n = cursor[0]
        cursor[0] += 1
        while len(split_tok) < 4:
            split()
        s, k, nk, last = chunks[n]
        reg = region[s["reg"]]
        for kk in range(nk):
            u = len(part_done)
            while len(split_tok) <= u:
                split()
            _, a, z = parts[u]
            view = [t[:, 0:(z - a) * s["nc"]].rearrange("p (k n) -> p k n", k=z - a) for t in (WHI[u % 4], WLO[u % 4])]
            waits = [split_tok[u], region_free[s["reg"]] if k == 0 else None]
            xh, xl, x_tok = s["rhs"](k + kk)
            todo = []
            for kind, cut, b, off, w in s["groups"]:
                start = b not in s["opened"]
                s["opened"].add(b)
                for i, (wv, xv) in enumerate(((view[0], xh), (view[0], xl), (view[1], xh))):
                    wa = cut(wv, kk - a)
                    if kind == "f":
                        lhs, rhs = wa, xv
                    else:
                        h = 128 * int(kind[1])
                        lhs, rhs = xv[:, h:h + 128], wa
                    todo.append((reg[b][:, off:off + w], lhs, rhs, start and i == 0, last and kk == nk - 1 and i == 2))
            for j, (o, lhs, rhs, st, fin) in enumerate(todo):
                end = kk == z - 1 and j == len(todo) - 1
                tk = pe(lambda e, o=o, lhs=lhs, rhs=rhs, st=st, fin=fin: e.matmul(
                    o, lhs, rhs, start=st, stop=fin, skip_group_check=True),
                    waits if j == 0 else None, x_tok if j == 0 else None, inc=end)
            if kk == z - 1:
                part_done.append(tk)
                if kk < nk - 1:
                    split()
            if kk < nk - 1:
                tick()
        chunk_done[n] = tk
        pe_later()
        if last:
            region_free[s["reg"]] = s["evac"](reg, tk)
        split()
        tick()
        if extra["every"]:
            extra["every"].pop(0)()
        extra["credit"] += extra["gemv"]
        while extra["credit"] >= 1:
            extra["credit"] -= 1
            next_gemv()

    def run(*ss_):
        for _ in range(sum(len(s["list"]) for s in ss_)):
            run_chunk()

    sq_free = [None, None]
    sr_free = [None, None]
    sq_n = [0]
    ss = bank[6][:, 0:S]

    def ssq_add(m0, x_tok, first, last, gcol=None, columns=False, soon=False):
        b = sq_n[0] % 2
        sq_n[0] += 1
        sq, x = SQ[b][:, :, :], xT[:, m0:m0 + 4, :]
        if columns == "only" and last:
            t_sq = act(lambda e: e.activation(sq, x, ACT.Square), x_tok, sq_free[b])
            t_sr = dve(lambda e: e.tensor_reduce(SR[b][:, :], sq.rearrange("p m s -> p s m"), AX_X, ALU.add),
                       t_sq, sr_free[b])
        else:
            src = x
            if gcol is not None:
                g = gcol[:, m0:m0 + 4]
                g = bass.AP(tensor=g.tensor, offset=g.offset, ap=[list(d) for d in g.ap] + [[0, S]])
                x_tok = pool(lambda e: e.tensor_tensor(sq, x, g, ALU.mult), x_tok, sq_free[b], T["cols"])
                src = sq
            t_sq = pool(lambda e: e.tensor_tensor(sq, src, src, ALU.mult), x_tok, sq_free[b])
            t_sq = pool(lambda e: e.tensor_tensor(sq[:, 0:2, :], sq[:, 0:2, :], sq[:, 2:4, :], ALU.add), t_sq)
            t_sr = pool(lambda e: e.tensor_tensor(SR[b][:, :], sq[:, 0, :], sq[:, 1, :], ALU.add), t_sq, sr_free[b])
        sq_free[b] = t_sr
        box = {}
        dst = ss if gcol is None else bank[6][:, S:2 * S]

        def go():
            if columns != "only":
                start = first and gcol is None
                tk = pe(lambda e: e.matmul(dst, ones[:, :], SR[b][:, :], start=start, stop=last, skip_group_check=True),
                        t_sr, ones_set, bf[6] if start else None)
            if columns:
                for h in range(2):
                    start = columns == "only" and first and h == 0
                    tk = pe(lambda e, h=h, start=start: e.matmul(
                        bank[6][:, S + h:S + h + 1], SR[b][:, 128 * h:128 * h + 128], ones[:, 0:1],
                        start=start, stop=last, skip_group_check=True), t_sr, ones_set, bf[6] if start else None)
            sr_free[b] = tk
            box["tok"] = tk
        if soon:
            later.append(go)
        else:
            side.extend([pause] * max(0, 12 - len(side)) + [go])
        return box

    def ssq_last(m0, x_tok, first, last, gcol=None, both=False):
        b = sq_n[0] % 2
        sq_n[0] += 1
        dst = ss if gcol is None else bank[6][:, S:2 * S]
        for i in range(4):
            if gcol is not None:
                t = act(lambda e, i=i: e.activation(SQ[b][:, i, :], xT[:, m0 + i, :], ACT.Square,
                                                    scale=gcol[:, m0 + i:m0 + i + 1]), x_tok[i], sq_free[b], T["cols"])
            elif both:
                t = dve(lambda e, i=i: e.tensor_tensor(SQ[b][:, i, :], xT[:, m0 + i, :], xT[:, m0 + i, :], ALU.mult),
                        x_tok[i], sq_free[b])
            else:
                t = act(lambda e, i=i: e.activation(SQ[b][:, i, :], xT[:, m0 + i, :], ACT.Square), x_tok[i], sq_free[b])

            def go(i=i, t=t):
                tk = pe(lambda e: e.matmul(dst, ones[:, :], SQ[b][:, i, :], start=False, stop=i == 3,
                                           skip_group_check=True), t, ones_set)
                sq_free[b] = box["tok"] = tk
            side.append(go)
        box = {}
        return box

    rstd_free = [None]

    def rstd_of(box, n, columns=False):
        t_std = act(lambda e: e.activation(std[:, :], ss, ACT.Sqrt, bias=epsc[:, 0:1], scale=1.0 / n),
                    box["tok"], eps_set, rstd_free[0])
        if columns:
            t_std = act(lambda e: e.activation(stdc[:, :], bank[6][:, S:S + 2], ACT.Sqrt, bias=epsc[:, 0:1],
                                               scale=1.0 / n), box["tok"])
            dve(lambda e: e.reciprocal(rstdc[:, :], stdc[:, :]), t_std)
        bf[6] = t_std
        return dve(lambda e: e.reciprocal(rstd[:, :], std[:, :]), t_std, rstd_free[0])

    def scaled_parts(HIs, LOs, m0, gcol, x_tok, free=None):
        for i in range(4):
            m = m0 + i
            t_hi = act(lambda e, m=m: e.activation(HIs[:, m, :], xT[:, m, :], ACT.Copy, scale=gcol[:, m:m + 1]),
                       x_tok, free)
        for i in range(4):
            m = m0 + i
            t_lo = dve(lambda e, m=m: e.scalar_tensor_tensor(
                LOs[:, m, :], xT[:, m, :], gcol[:, m:m + 1], HIs[:, m, :].bitcast(F32), ALU.mult, ALU.subtract),
                x_tok, t_hi, free)
        return [t_hi, t_lo]

    def by_token(t, n):
        a = t[:, :]
        return bass.AP(tensor=a.tensor, offset=a.offset, ap=[list(a.ap[0]), [0, n], [1, S]])

    ht_free = [None, None]

    def normed(box, gcol, factor, shcol, *waits):
        waits = list(waits)
        box.update(n=0, tok=[None] * KT, y=None)
        slot = [ht_free[i // 4] for i in range(8)]

        def low(m):
            t = dve(lambda e: e.scalar_tensor_tensor(
                LO[:, m, :], HT[m % 8 // 4][:, m % 4, :], shcol[:, m:m + 1], HI[:, m, :].bitcast(F32), ALU.add, ALU.subtract),
                box["tok"][m], waits)
            slot[m % 8] = [box["tok"][m], t]
            box["tok"][m] = slot[m % 8]
            ht_free[m % 8 // 4] = [slot[m % 8 // 4 * 4 + i] for i in range(4)]

        def emit():
            m = box["n"]
            box["n"] += 1
            t = dve(lambda e: e.scalar_tensor_tensor(HT[m % 8 // 4][:, m % 4, :], xT[:, m, :], gcol[:, m:m + 1], factor[:, :],
                                                     ALU.mult, ALU.mult), waits, slot[m % 8])
            box["y"] = t
            box["tok"][m] = act(lambda e: e.activation(HI[:, m, :], HT[m % 8 // 4][:, m % 4, :], ACT.Identity,
                                                       bias=shcol[:, m:m + 1]), t, waits)
            if m > 0:
                low(m - 1)
            if m == KT - 1:
                low(m)
        box["emit"] = emit

    def rhs_normed(box):
        def get(k):
            while box["n"] < min(KT, k + 9):
                box["emit"]()
            return HI[:, k, :], LO[:, k, :], box["tok"][k]
        return get

    def rhs_of(hi, lo, toks, base=0):
        def get(k):
            while toks["t"][(base + k) // 4] is None:
                side.popleft()()
            return hi[:, base + k, :], lo[:, base + k, :], toks["t"][(base + k) // 4]
        return get

    g_mix, g_ffn, g_fin, g_att2, g_mlp2, g_fin2 = [cols[:, 16 * i:16 * i + 16] for i in range(6)]
    gq, gkv = cols[:, 112:115], cols[:, 115:116]
    h1 = {"t": [None] * 4}
    x_turned, x_new = [], []
    for m0 in range(0, KT, 4):
        for t in range(2):
            i = m0 // 4 * 2 + t
            for j in range(4):
                tp = pe(lambda e, i=i, j=j, m=m0 + j, t=t: e.transpose(
                    bank[i][:, 128 * j:128 * j + 128], XROW[:, t, 128 * m:128 * m + 128], ident[:, :]),
                    x_in[m0 // 4], c_in, t_mix if i == 7 else None, inc=j == 3)
            x_turned.append(tp)
        if m0 == 0:
            tp = pe(lambda e: e.transpose(bank[7][:, 0:16], rowsM[:, :], ident[0:16, 0:16]), c_in, mix_in)
            t_mix = act(lambda e: e.activation(gmix[:, :], bank[7][:, 0:16], ACT.Copy), tp)

    def x_to_sbuf(m0):
        tt = []
        for t in range(2):
            i = m0 // 4 * 2 + t
            dst = xT[:, m0:m0 + 4, 128 * t:128 * t + 128]
            src = bank[i][:, :].rearrange("p (m s) -> p m s", m=4)
            if t == 0:
                tt.append(act(lambda e, dst=dst, src=src: e.activation(dst, src, ACT.Copy), x_turned[i]))
            else:
                tt.append(dve(lambda e, dst=dst, src=src: e.tensor_copy(dst, src), x_turned[i]))
        return tt


    L_tA, L_tB = Landing(sem("l_tA")), Landing(sem("l_tB"))
    L_bA, L_bB = Landing(sem("l_bA")), Landing(sem("l_bB"))
    T = {}

    def repeated(t):
        return bass.AP(tensor=t.tensor, offset=t.offset, ap=[list(t.ap[0]), [0, 128], [1, 384]])

    def toeplitz(t, h0, n):
        return bass.AP(tensor=t.tensor, offset=t.offset + 127 + h0 * 128 * 384, ap=[[383, 128], [128 * 384, n], [1, 256]])

    def table_out(name, landing, dst, src, i):
        def go():
            T[name] = landing.start(pool, dst[4 * i:4 * i + 4], repeated(src[4 * i:4 * i + 4, :]),
                                    T["R16"], chunk_done[cursor[0] - 1])
        return go

    def table_in(i):
        def go():
            T["biasA"] = L_bA.start(pool, biasA[:, 4 * i:4 * i + 4, :], toeplitz(toepA, 4 * i, 4), T["tA"],
                                    chunk_done[cursor[0] - 1])
        return go

    def tables_cols():
        pe(lambda e: e.transpose(bank[4][:, 0:116], rowsA[:, :], ident[0:116, 0:116]), c_in, rows_in, bf[4], inc=False)
        pe(lambda e: e.transpose(bank[4][:, 128:224], rowsB[:, :], ident[0:96, 0:96]), rowP_in, bf[4], inc=False)
        tk = pe(lambda e: e.transpose(bank[4][:, 256:320], rowsP[:, :], ident[0:64, 0:64]))
        T["cols"] = act(lambda e: e.activation(cols[:, :], bank[4][:, 0:116], ACT.Copy), tk)
        T["cact"] = act(lambda e: e.activation(cact[:, :], cols[:, 96:112], ACT.Silu), T["cols"])
        T["bmod"] = act(lambda e: e.activation(bmod[:, :], bank[4][:, 128:224], ACT.Copy), tk)
        T["posT"] = bf[4] = act(lambda e: e.activation(posT[:, :], bank[4][:, 256:320], ACT.Copy), tk)

    def tables_toeplitz():
        pe(lambda e: e.matmul(bank[5][0:16, 0:384], rela[:, :], OH[:, 0:384], start=True, stop=True),
           k_in, relm, bf[5], inc=False)
        tk = pe(lambda e: e.matmul(bank[7][0:16, 0:384], relb[:, :], OH[:, 384:768], start=True, stop=True), bf[7])
        ta = bf[5] = act(lambda e: e.activation(R16a[:, :], bank[5][0:16, 0:384], ACT.Copy), tk)
        tb = bf[7] = act(lambda e: e.activation(R16b[:, :], bank[7][0:16, 0:384], ACT.Copy), tk)
        T["R16"] = [ta, tb]

    mod_tok = [None] * 6
    acc_free = [None]

    def gemv(p, k):
        def go():
            while acc_busy[0]:
                side.popleft()()
            raw, landed, slot = load(lambda t: t[:, :],
                                     A["w_mod_2"][0][k * 128:(k + 1) * 128, p * 2048:(p + 1) * 2048])
            if k == 0:
                t = dve(lambda e: e.tensor_scalar(ACC[:, :], raw[:, :], cact[:, 0:1], None, ALU.mult),
                        landed, T["cact"], acc_free[0])
            else:
                t = dve(lambda e: e.scalar_tensor_tensor(ACC[:, :], raw[:, :], cact[:, k:k + 1], ACC[:, :],
                                                         ALU.mult, ALU.add), landed, acc_tok[0])
            acc_tok[0] = t
            raw_free[slot] = t
            if k == 15:
                acc_busy[0] = True

                def reduce(q):
                    for j in range(4):
                        o = 512 * q + 128 * j
                        tk = pe(lambda e, j=j, o=o: e.transpose(bank[7][:, 128 * j:128 * j + 128], ACC[:, o:o + 128],
                                                                ident[:, :]), t, bf[7], inc=j == 3)
                    c = 16 * p + 4 * q
                    tr = dve(lambda e: e.tensor_reduce(mod[:, c:c + 4], bank[7][:, :].rearrange("p (j k) -> p j k", j=4),
                                                       AX_X, ALU.add), tk)
                    bf[7] = tr
                    if q == 3:
                        acc_free[0], acc_busy[0] = tk, False
                        sl = slice(16 * p, 16 * p + 16)
                        mod_tok[p] = dve(lambda e: e.tensor_tensor(mod[:, sl], mod[:, sl], bmod[:, sl], ALU.add),
                                         tr, mod_part, T["bmod"])
                    else:
                        mod_part.append(tr)
                mod_part = []
                for q in range(4):
                    side.extend([pause] * (5 if q == 0 else 2) + [lambda q=q: reduce(q)])
        return go

    acc_tok, acc_busy = [None], [False]
    gemvs = []
    for p in range(6):
        gemvs += [gemv(p, k) for k in range(16)] + [None, None]

    gq_iter = iter(gemvs)

    def next_gemv():
        f = next(gq_iter, None)
        if f is not None:
            f()

    declare = slab

    rhs1 = rhs_of(HI, LO, h1)
    tk1 = {}

    def to_feat(dst, name, scale=1.0, tiles=4, free=lambda: None):
        def evac(reg, done):
            t = None
            for b in range(tiles // 2):
                src = reg[b][:, :].rearrange("p (m s) -> p m s", m=2)
                d = dst[:, 2 * b:2 * b + 2, :]
                t = act(lambda e, d=d, src=src: e.activation(d, src, ACT.Copy, scale=scale), done, free())
            tk1[name] = t
            return t
        return evac

    def to_feat1(dst, name, scale=1.0, free=lambda: None):
        def evac(reg, done):
            t = None
            for b in range(2):
                src = reg[b][:, :].rearrange("p (m s) -> p m s", m=2)
                d = dst[:, 2 * b:2 * b + 2, :]
                t = dve(lambda e, d=d, src=src: e.scalar_tensor_tensor(d, src, scale, by_token(rstd, 2), ALU.mult, ALU.mult),
                        done, free(), T["rstd1"])
            tk1[name] = rstd_free[0] = t
            return t
        return evac

    def to_tok(dst, name, free=lambda: None):
        def evac(reg, done):
            t = None
            for b in range(2):
                t = act(lambda e, b=b: e.activation(dst[:, b, :], reg[b][:, :], ACT.Copy, scale=rstdc[:, b:b + 1]),
                        done, free(), T["rstd1"])
            tk1[name] = t
            return t
        return evac

    def gate_evac(reg, done):
        t = act(lambda e: e.activation(glT[:, :], reg[0][:, 0:S], ACT.Copy), done, h1["ht"])

        def to_rows():
            for b in range(2):
                tk = pe(lambda e, b=b: e.transpose(bank[5][:, 128 * b:128 * b + 128], glT[:, 128 * b:128 * b + 128],
                                                   ident[:, :]), t, bf[5], inc=b == 1)
            for b in range(2):
                for br in range(3):
                    o = gates[:, br, :, b] if br == 0 else gates[:, 1, :, 2 * (1 - b) + br - 1]
                    src = bank[5][:, 128 * b + 80 + 16 * br:128 * b + 96 + 16 * br]
                    bf[5] = act(lambda e, o=o, src=src, b=b: e.activation(o, src, ACT.Sigmoid, scale=rstdc[:, b:b + 1]),
                                tk, T["rstd1"])
            tk1["gates"] = bf[5]
        side.extend([pause, to_rows])
        return t

    W = A["nsa_w_in"][0]
    def tables_done():
        return [T[n] for n in ("R16", "posT", "bmod")]

    nsa = [
        declare(W, 0, KT, 2048, 512, FEAT4, rhs1, to_feat1(kcT, "kc", free=lambda: h1["ht"])),
        declare(W, 0, KT, 2560, 512, FEAT4, rhs1, to_feat1(vcT, "vc", free=lambda: h1["ht"])),
        declare(W, 0, KT, 3072, 512, FEAT4, rhs1, to_feat1(ksT, "ks", free=tables_done)),
        declare(W, 0, KT, 4096, 512, FEAT4, rhs1, to_feat1(kwT, "kw", free=tables_done)),
        declare(W, 0, KT, 3584, 512, TOK512, rhs1, to_tok(vs, "vs", free=lambda: T["tA"])),
        declare(W, 0, KT, 4608, 512, TOK512, rhs1, to_tok(vw, "vw", free=tables_done)),
        declare(W, 0, KT, 5040, 128, [feat(0, 0, 0)], rhs1, gate_evac),
    ]
    for i in range(4):
        nsa.append(declare(W, 0, KT, 512 * i, 512, FEAT4, rhs1,
                           to_feat1(qT[:, 4 * i:4 * i + 4, :], f"q{i}", scale=128.0 ** -0.5, free=lambda: x_new[3])))
    for s_ in nsa[:5]:
        queue(s_)
    queue(nsa[5], nsa[6])
    for s_ in nsa[7:]:
        queue(s_)

    ONCE, NO_HURRY, COLUMNS = "plain squares", "nothing waits for the last ones", "as columns only"

    def residual(xbox, gcol=None, g_tok=None, ssq=ONCE, after=None):
        def at_tile(m0, first, last):
            def evac(reg, done):
                ts = []
                for i in range(4):
                    m = m0 + i
                    src = reg[i // 2][:, S * (i % 2):S * (i % 2) + S]
                    if gcol is None:
                        ts.append(dve(lambda e, m=m, src=src: e.tensor_tensor(xT[:, m, :], src, xT[:, m, :], ALU.add),
                                      done, xbox.get("free")))
                    else:
                        ts.append(dve(lambda e, m=m, src=src: e.scalar_tensor_tensor(
                            xT[:, m, :], src, gcol[:, m:m + 1], xT[:, m, :], ALU.mult, ALU.add),
                            done, xbox.get("free"), mod_tok[g_tok]))
                xbox["x"] = ts[-1]
                if after is not None:
                    after(m0, ts)
                if ssq is COLUMNS:
                    xbox["box"] = ssq_add(m0, ts, first, last, columns="only")
                elif ssq is not None:
                    two = not isinstance(ssq, str)
                    add = ssq_add if not last or ssq is NO_HURRY else ssq_last
                    xbox["box"] = add(m0, ts, first, last, **(dict(both=True) if two and add is ssq_last else {}))
                    if two:
                        xbox["box2"] = add(m0, ts, first, last, gcol=ssq)
                return ts[-1]
            return evac
        return at_tile

    xb1, xb2, xb3, xb4 = {}, {}, {}, {}

    def declare_out(w, row0, kts, rhs, maker, pair=False):
        new = [declare(w, row0, kts, 512 * i, 512, FEAT4, rhs, maker(4 * i, i == 0, i == 3)) for i in range(4)]
        if pair:
            queue(new[0], new[1])
        else:
            queue(new[0])
            queue(new[1])
        queue(new[2])
        queue(new[3])
        return new

    h2 = {}
    out1 = declare_out(A["nsa_w_out"][0], 0, KT, rhs_of(HI, LO, h2),
                       residual(xb1, ssq=NO_HURRY, after=lambda m0, t: h3_parts(m0, t)), pair=True)

    h3 = {"t": [None] * 4}

    def h3_parts(m0, t):
        h3["t"][m0 // 4] = scaled_parts(H3H, H3L, m0, g_ffn, t, [hid["ufree"], T["cols"]])

    hid = {}
    sa_n, sa_tok = [0], [None, None]
    ht2_n = [0]

    def hid_split(ht, b, base, t_h, first=False):
        hh, hl, k = (HIDH, HIDL, base) if not first else (HI, LO, base) if base < 16 else (HXH, HXL, base - 16)
        t_hi = act(lambda e: e.activation(hh[:, k:k + 4, :], ht[:, :, :], ACT.Copy), t_h, hid["free"])
        t_lo = dve(lambda e: e.tensor_tensor(hl[:, k:k + 4, :], ht[:, :, :], hh[:, k:k + 4, :].bitcast(F32),
                                             ALU.subtract), t_h, t_hi, hid["free"])
        ht_free[b] = [t_hi, t_lo]
        hid["t"][base // 4] = [t_hi, t_lo]

    def hid_rhs(k):
        hh, hl, j = (HI, LO, k) if k < 16 else (HXH, HXL, k - 16)
        return hh[:, j, :], hl[:, j, :], hid["t"][k // 4]

    def scaled(dst, reg, done, *free):
        for b in range(2):
            t = dve(lambda e, b=b: e.tensor_tensor(
                dst[:, 2 * b:2 * b + 2, :], reg[b][:, :].rearrange("p (m s) -> p m s", m=2), by_token(rstd, 2),
                ALU.mult), done, T["rstd3"], *free)
        rstd_free[0] = t
        return t

    def silu_evac(reg, done):
        i = sa_n[0] % 2
        t = scaled(SA[i], reg, done, sa_tok[i], hid.get("ufree"))
        hid["sa"] = act(lambda e: e.activation(SA[i][:, :, :], SA[i][:, :, :], ACT.Silu), t)
        return t

    def glu_evac(base):
        def evac(reg, done):
            i = sa_n[0] % 2
            sa_n[0] += 1
            t = scaled(HT[i], reg, done, ht_free[i])
            t_h = dve(lambda e: e.tensor_tensor(HT[i][:, :, :], HT[i][:, :, :], SA[i][:, :, :], ALU.mult),
                      t, hid["sa"])
            sa_tok[i] = t_h
            hid_split(HT[i], i, base, t_h, first=True)
            return t
        return evac

    def relu2_evac(base):
        def evac(reg, done):
            i = sa_n[0] % 2
            sa_n[0] += 1
            t = None
            for b in range(2):
                t = act(lambda e, b=b: e.activation(SA[i][:, 2 * b:2 * b + 2, :],
                                                    reg[b][:, :].rearrange("p (m s) -> p m s", m=2), ACT.Relu),
                        done, sa_tok[i])
            t_h = dve(lambda e: e.tensor_tensor(HT[i][:, :, :], SA[i][:, :, :], SA[i][:, :, :], ALU.mult),
                      t, ht_free[i])
            sa_tok[i] = t_h
            hid_split(HT[i], i, base, t_h)
            return t
        return evac

    rhs3 = rhs_of(H3H, H3L, h3)
    ffn1 = []
    W1, W2 = A["ffn_w_in"][0], A["ffn_w_out"][0]
    parts1 = [(0, 6), (6, 5)]
    hidv = {"t": [None] * 6}
    hid["t"] = [None] * 6
    for pi, (s0, n) in enumerate(parts1):
        up = []
        for j in range(n):
            c = 512 * (s0 + j)
            up.append(declare(W1, 0, KT, c, 512, FEAT4, rhs3, silu_evac))
            up.append(declare(W1, 0, KT, FF1 + c, 512, FEAT4, rhs3, glu_evac(4 * j)))
            queue(up[-2])
            queue(up[-1])
        down = declare_out(W2, 4 * s0, 4 * n, hid_rhs,
                           residual(xb2, ssq=g_fin if pi == len(parts1) - 1 else None))
        ffn1.append((up, down))

    h4 = {}
    rhs4 = rhs_normed(h4)
    W = A["w_in_2"][0]

    att2 = {}

    def ka_evac(reg, done):
        for kv in range(2):
            for par in range(2):
                t = act(lambda e, kv=kv, par=par: e.activation(
                    Kpad[64 * par:64 * par + 64, kv, par, :], reg[0][64 * kv:64 * kv + 64, 0:S], ACT.Copy),
                    done, att2["pad0"])
        att2["k"] = t
        t = act(lambda e: e.activation(vT2[:, :], reg[0][:, S:2 * S], ACT.Copy), done, att2["free"])

        def to_rows():
            for half in range(2):
                tk = pe(lambda e, half=half: e.transpose(
                    bank[5][:, 128 * half:128 * half + 128], vT2[:, 128 * half:128 * half + 128], ident[:, :]),
                    t, bf[5], inc=half == 1)
            for kv in range(2):
                for par in range(2):
                    src = bank[5][:, 0:256].rearrange("p (h c) -> p h c", h=2)[:, :, 64 * kv:64 * kv + 64]
                    bf[5] = act(lambda e, kv=kv, par=par, src=src: e.activation(
                        Vpad2[:, kv, par, :, 64 * par:64 * par + 64], src, ACT.Copy), tk, att2["pad0"])
            att2["kv"] = bf[5]
        side.extend([pause, to_rows])
        return t

    def cq_evac(reg, done):
        t = None
        for m in range(3):
            t = act(lambda e, m=m: e.activation(CQ[:, m, :], reg[m // 2][:, 256 * (m % 2):256 * (m % 2) + 256],
                                                ACT.Copy), done, att2["free"])
        att2["cq"] = t
        return t

    def rope_apply(src, n, dst, done, free):
        for q in (2, 3):
            p = q ^ 1
            t = act(lambda e, q=q, p=p: e.activation(
                ropeX[32 * q:32 * q + 32, 0:n, :], src[32 * p:32 * p + 32, :].rearrange("p (h s) -> p h s", h=n), ACT.Copy),
                done, att2.get("ropefree"), att2["free"])
        t1 = t2 = None
        for h in range(n):
            t1 = dve(lambda e, h=h: e.tensor_tensor(ropeT[64:128, h, :], src[64:128, S * h:S * h + S], cosT[64:128, :], ALU.mult),
                     done, t, att2["rope_in"], att2.get("ropefree"))
            t2 = dve(lambda e, h=h: e.tensor_tensor(ropeU[64:128, h, :], ropeX[64:128, h, :], sinT[64:128, :], ALU.mult),
                     t, att2["rope_in"], att2.get("ropefree"))
        t3 = dve(lambda e: e.tensor_tensor(dst3(dst), ropeT[64:128, 0:n, :], ropeU[64:128, 0:n, :], ALU.add), t1, t2, free)
        att2["ropefree"] = t3
        return t1, t3

    def dst3(d):
        return d if len(d.shape) == 3 else d.rearrange("p (h s) -> p h s", h=1)

    def ckv_evac(reg, done):
        t = act(lambda e: e.activation(CQ[:, 3, :], reg[0][:, 0:S], ACT.Copy), done, att2["free"])
        att2["ckv"] = t
        t1, t3 = rope_apply(reg[0][:, 256:512], 1, krp[64:128, :], [done, t], att2["pad0"])
        att2["kr"] = t3
        return [t, t1]

    def declare_qa(i):
        return declare(W, 0, KT, 512 * i, 512, FEAT4, rhs4,
                       to_feat(qaT[:, 4 * i:4 * i + 4, :], f"qa{i}", scale=0.125, free=lambda: att2["free"]))

    sl_qa = [declare_qa(0)]
    sl_ka = declare(W, 0, KT, 1024, 256, [feat(0, 0, 0), feat(128, 0, 256)], rhs4, ka_evac)
    sl_qa.append(declare_qa(1))
    sl_cq = declare(W, 0, KT, 1280, 384, [feat(0, 0, 0), feat(128, 0, 256), feat(256, 1, 0)], rhs4, cq_evac, per=4)
    sl_ckv = declare(W, 0, KT, 1664, 192, [feat(0, 0, 0), feat(64, 0, 256)], rhs4, ckv_evac)
    for s_ in (sl_qa[0], sl_ka, sl_qa[1], sl_cq, sl_ckv):
        queue(s_)
    hq = {}

    def uq_evac(j):
        def evac(reg, done):
            ta = act(lambda e: e.activation(qnT[:, 2 * j:2 * j + 2, :],
                                            reg[0][:, :].rearrange("p (m s) -> p m s", m=2), ACT.Copy),
                     done, att2["free"], hq["kv"])
            t1, t3 = rope_apply(reg[1][:, :], 2, qrT[64:128, 2 * j:2 * j + 2, :], done, att2["pad0"])
            tk1[f"qm{j}"] = [ta, t3]
            return [ta, t1]
        return evac

    uq = [declare(A["w_uq_2"][0], 0, 3, 384 * j, 384,
                  [feat(0, 0, 0), feat(192, 0, 256), feat(64, 1, 0), feat(256, 1, 256)],
                  lambda k: (CQH[:, k, :], CQL[:, k, :], hq["q"]), uq_evac(j), per=3) for j in range(4)]

    def ukv_evac(j):
        def evac(reg, done):
            ta = act(lambda e: e.activation(knT[:, 2 * j:2 * j + 2, :],
                                            reg[0][:, :].rearrange("p (m s) -> p m s", m=2), ACT.Copy),
                     done, att2["swa_done"])
            tb = act(lambda e: e.activation(vb[:, :, 256 * j:256 * j + 256],
                                            reg[1][:, :].rearrange("p (t c) -> p t c", t=2), ACT.Copy),
                     done, att2["swa_done"])
            tk1[f"km{j}"] = tb
            return tb
        return evac

    def ukv_v(half):
        return ("t%d" % half, lambda v, k: v[:, k, :].rearrange("p (h c) -> p h c", h=2)[:, :, 128:256],
                1, 256 * half, 256)

    ukv = [declare(A["w_ukv_2"][0], 0, 1, 512 * j, 512,
                   [feat(0, 0, 0), feat(256, 0, 256), ukv_v(0), ukv_v(1)],
                   lambda k: (CQH[:, 3, :], CQL[:, 3, :], hq["kv"]), ukv_evac(j), per=1) for j in range(4)]

    for s_ in uq + ukv:
        queue(s_)

    y_rows = {}
    xg_free = [None, None]

    def turn_back(m0, x_tok):
        xg = XG[m0 // 4 % 2]
        free = [hid["xg"], xg_free[m0 // 4 % 2]]
        for i in range(4):
            if m0 < 12:
                t = act(lambda e, i=i: e.activation(xg[:, i, :], xT[:, m0 + i, :], ACT.Copy,
                                                    scale=g_fin2[:, m0 + i:m0 + i + 1]), x_tok[i], free)
            else:
                t = dve(lambda e, i=i: e.tensor_scalar(xg[:, i, :], xT[:, m0 + i, :], g_fin2[:, m0 + i:m0 + i + 1], None,
                                                       ALU.mult), x_tok[i], free)

        def go():
            tk = []
            for h in range(2):
                for i in range(4):
                    p = pe(lambda e, h=h, i=i: e.transpose(bank[4 + h][:, 128 * i:128 * i + 128],
                                                           xg[:, i, 128 * h:128 * h + 128], ident[:, :]),
                           t, bf[4 + h], inc=i == 3)
                tk.append(p)
            xg_free[m0 // 4 % 2] = tk
            if m0 < 12:
                sl = slice(128 * m0, 128 * m0 + 512)
                for h in range(2):
                    bf[4 + h] = act(lambda e, h=h: e.activation(YROW[:, h, sl], bank[4 + h][:, :], ACT.Copy),
                                    tk[h], hid["yrow"])
                y_rows[m0] = [bf[4], bf[5]]
            else:
                y_rows[m0] = tk
        side.extend([pause] * (8 if m0 < 12 else 0) + [go])

    h5, h6 = {}, {}
    out2 = declare_out(A["w_out_2"][0], 0, KT, rhs_of(HI, LO, h5), residual(xb3, mod[:, 32:48], 2), pair=True)
    rhs6 = rhs_normed(h6)
    ffn2 = []
    W1, W2 = A["w_ff1_2"][0], A["w_ff2_2"][0]
    parts2 = [(0, 6), (6, 5), (11, 5)]
    for pi, (s0, n) in enumerate(parts2):
        up = [declare(W1, 0, KT, 512 * (s0 + j), 512, FEAT4, rhs6, relu2_evac(4 * j)) for j in range(n)]
        for s_ in up:
            queue(s_)
        down = declare_out(W2, 4 * s0, 4 * n, rhs_of(HIDH, HIDL, hid),
                           residual(xb4, mod[:, 80:96], 5, ssq=COLUMNS if pi == len(parts2) - 1 else None,
                                    after=turn_back if pi == len(parts2) - 1 else None))
        ffn2.append((up, down))

    def attention(SPb, PTb, free):
        units, st = [], []
        used = {"SP": [free] * 3, "PTS": [[free, free], [free, free]]}

        def scores(i):
            u = units[i]
            for br, b in enumerate(u["br"]):
                for blk, bk, o, n in ((0, bank[4], 128 * br, 128), (1, bank[5], 256 * br, 256)):
                    pr = b["qk"](blk, n)
                    for j, (l, r_) in enumerate(pr):
                        tk = pe(lambda e, bk=bk, o=o, n=n, l=l, r_=r_, j=j, pr=pr: e.matmul(
                            bk[:, o:o + n], l, r_, start=j == 0, stop=j == len(pr) - 1, skip_group_check=True),
                            [bf[4], bf[5], u["ready"]] if (br, blk, j) == (0, 0, 0) else None,
                            inc=(br, blk, j) == (len(u["br"]) - 1, 1, len(pr) - 1))
            st[i]["S"] = tk

        def softmax1(i):
            u, q = units[i], i % 3
            nb = len(u["br"])
            stt = stat[:, q, :, :]
            ts = []
            for br, b in enumerate(u["br"]):
                for blk in (1, 0):
                    n = 128 * (blk + 1)
                    j = br if blk else 2 + br
                    o = 256 * br if blk else 512 + 128 * br
                    src = bank[5][:, 256 * br:256 * br + 256] if blk else bank[4][:, 128 * br:128 * br + 128]
                    bias = b["bias"] if blk else b["bias"][:, 128:256]
                    least = b["least"](j) if b["least"] else -3.0e38
                    ts.append(dve(lambda e, n=n, j=j, o=o, src=src, bias=bias, b=b, least=least: e.tensor_tensor_reduce(
                        out=SPb[q][:, o:o + n], in0=src, in1=bias, scale=b["scale"], scalar=least,
                        op0=ALU.add, op1=ALU.max, accum_out=stt[:, 0, j:j + 1]),
                        st[i]["S"], used["SP"][q], u["bias_tok"]))
            bf[4] = bf[5] = ts[-1]
            t = dve(lambda e: e.tensor_scalar(stt[:, 1, :], stt[:, 0, :], -1.0, None, ALU.mult), ts) if nb == 2 else \
                dve(lambda e: e.tensor_scalar(stt[:, 1, 0:3:2], stt[:, 0, 0:3:2], -1.0, None, ALU.mult), ts)
            st[i]["nm"] = t
            if u["sink"] is not None:
                st[i]["sk"] = dve(lambda e: e.tensor_tensor(stt[:, 4, :], stt[:, 1, :], u["sink"], ALU.add), t)

        def softmax2(i):
            u, q = units[i], i % 3
            stt = stat[:, q, :, :]
            t = None
            for br in range(len(u["br"])):
                for blk in (1, 0):
                    n = 128 * (blk + 1)
                    j = br if blk else 2 + br
                    o = 256 * br if blk else 512 + 128 * br
                    t = act(lambda e, n=n, j=j, o=o: e.activation(
                        SPb[q][:, o:o + n], SPb[q][:, o:o + n], ACT.Exp, bias=stt[:, 1, j:j + 1],
                        accum_out=stt[:, 2, j:j + 1]), st[i]["nm"])
            if u["sink"] is not None:
                t = act(lambda e: e.activation(stt[:, 5, :], stt[:, 4, :], ACT.Exp), st[i]["sk"])
            st[i]["exp"] = t

        def softmax3(i):
            u, q = units[i], i % 3
            stt = stat[:, q, :, :]
            step = slice(0, 4) if len(u["br"]) == 2 else slice(0, 3, 2)
            t = st[i]["exp"]
            if u["sink"] is not None:
                t = dve(lambda e: e.tensor_tensor(stt[:, 2, :], stt[:, 2, :], stt[:, 5, :], ALU.add), t)
            t = dve(lambda e: e.reciprocal(stt[:, 3, step], stt[:, 2, step]), t)
            if u["gate"] is not None:
                t = dve(lambda e: e.tensor_tensor(stt[:, 3, :], stt[:, 3, :], u["gate"], ALU.mult), t, u["gate_tok"])
            ts = []
            for br in range(len(u["br"])):
                for blk in (1, 0):
                    n = 128 * (blk + 1)
                    j = br if blk else 2 + br
                    o = 256 * br if blk else 512 + 128 * br
                    ts.append(dve(lambda e, n=n, j=j, o=o: e.tensor_scalar(
                        SPb[q][:, o:o + n], SPb[q][:, o:o + n], stt[:, 3, j:j + 1], None, ALU.mult), t))
            st[i]["P"] = ts[-1]

        def turn(i, br):
            u, q, p = units[i], i % 3, i % 2
            for n, (dst, src) in enumerate(((0, 512 + 128 * br), (128, 256 * br), (256, 256 * br + 128))):
                tk = pe(lambda e, dst=dst, src=src: e.transpose(
                    bank[6][:, dst:dst + 128], SPb[q][:, src:src + 128], ident[:, :]),
                    [st[i]["P"], bf[6]], inc=n == 2)
            used["SP"][q] = tk
            t = act(lambda e: e.activation(PTb[p][:, br, :], bank[6][:, 0:384], ACT.Copy), tk, used["PTS"][p][br])
            bf[6] = t
            st[i][f"PT{br}"] = t

        def values(i):
            u, p = units[i], i % 2
            o = bank[7]
            mm = []
            if u["more"] is not None:
                mm.append((o[:, 0:S], *u["more"], u["v_ready"]()))
            for br, b in enumerate(u["br"]):
                mm.append((o[:, 0:S], b["v"](0), PTb[p][:, br, 0:256], [st[i][f"PT{br}"], u["v_ready"]()]))
                mm.append((o[:, 128:S], b["v"](1), PTb[p][:, br, 256:384], None))
            for j, (dst, l, r_, w) in enumerate(mm):
                tk = pe(lambda e, dst=dst, l=l, r_=r_, j=j: e.matmul(
                    dst, l, r_, start=j == 0, stop=j == len(mm) - 1, skip_group_check=True),
                    w, bf[7] if j == 0 else None, inc=j == len(mm) - 1)
            st[i]["O"] = tk
            used["PTS"][p] = [tk, tk]

        def finish(i):
            bf[7] = units[i]["put"](st[i]["O"])

        def steps(new, last):
            lo = len(units)
            units.extend(new)
            st.extend(dict() for _ in new)
            n = len(units)
            for i in range(lo, n + 3 if last else n):
                def s0(i=i):
                    if i - 1 < len(units):
                        softmax3(i - 1)
                    if i - 2 < len(units):
                        turn(i - 2, 0)

                def s1(i=i):
                    if i < n:
                        scores(i)
                        softmax1(i)

                def s2(i=i):
                    if 0 <= i - 2 < len(units) and len(units[i - 2]["br"]) > 1:
                        turn(i - 2, 1)
                    if i < n:
                        softmax2(i)

                def s3(i=i):
                    values(i - 3)
                    finish(i - 3)
                if i >= 2:
                    yield s0
                elif i == 1:
                    yield lambda: softmax3(0)
                yield s1
                yield s2
                if i >= 3:
                    yield s3

        return steps

    h_tok = {}

    x_new.append(x_to_sbuf(0))
    for m0 in range(0, KT, 4):
        if m0 < 12:
            x_new.append(x_to_sbuf(m0 + 4))
        h1["t"][m0 // 4] = scaled_parts(HI, LO, m0, gmix, x_new[m0 // 4], t_mix)
        split()
    for i in range(4, 8):
        bf[i] = x_new[i // 2][i % 2]
    region_free[0], region_free[1] = x_new[0], x_new[1]
    h1["ht"] = [sq_free, sr_free]

    def ssq_x(m0):
        T["ssq"] = ssq_add(m0, x_new[m0 // 4], m0 == 0, m0 == 12, columns=True, soon=True)

    def rstd_x():
        T["rstd1"] = rstd_of(T["ssq"], D, columns=True)

    side.extend([pause, lambda: ssq_x(0), pause, lambda: ssq_x(4), pause, pause, pause, pe_later, lambda: ssq_x(8), lambda: ssq_x(12),
                 pause, pause, pe_later, rstd_x, tables_cols, tables_toeplitz])

    zfree = [None]
    cz = {}

    def make_z(kv):
        src = (kcT, vcT)[kv][:, :, :]
        ap0 = list(src.ap[0])
        win = bass.AP(tensor=src.tensor, offset=src.offset, ap=[ap0, [S, 4], [1, 32], [16, 15]])
        ps = posT[:, 32 * kv:32 * kv + 32]
        pos = bass.AP(tensor=ps.tensor, offset=ps.offset, ap=[list(ps.ap[0]), [0, 4], [1, 32], [0, 15]])
        z = Z[:, :, :]
        o = bass.AP(tensor=z.tensor, offset=z.offset, ap=[list(z.ap[0]), [15, 4], [60, 32], [1, 15]])
        t = None
        for g in range(4):
            def sub(a, g=g):
                return bass.AP(tensor=a.tensor, offset=a.offset + g * a.ap[1][0], ap=[list(a.ap[0])] + [list(d) for d in a.ap[2:]])
            t = dve(lambda e, o=sub(o), w=sub(win), q=sub(pos): e.tensor_tensor(o, w, q, ALU.add),
                    tk1["kc" if kv == 0 else "vc"], T["posT"], zfree[0], h1["ht"])
        cz["z"] = t

    def cmp_step(kv, i):
        def go():
            w = A["cmp_w1_k" if kv == 0 else "cmp_w1_v"][0]
            src = w[i * 1024:(i + 1) * 1024, :].rearrange("(l p) n -> p l n", p=128)
            raw, landed, slot = load(lambda t: t[:, :].rearrange("p (l n) -> p l n", l=8), src)
            rv = raw[:, :].rearrange("p (l n) -> p l n", l=8)
            for l in range(8):
                for m in range(2):
                    tk = pe(lambda e, l=l, m=m: e.matmul(
                        bank[4][:, 60 * m:60 * m + 60], rv[:, l, 128 * m:128 * m + 128], Z[:, 8 * i + l, :],
                        start=(i, l, m) == (0, 0, 0), stop=(i, l) == (3, 7), skip_group_check=True),
                        [landed, cz["z"], bf[4]] if (l, m) == (0, 0) else None, inc=(l, m) == (7, 1))
            raw_free[slot] = tk
            if i == 3:
                zfree[0] = tk
                t = act(lambda e: e.activation(hidT[:, kv, :, :], bank[4][:, 0:120].rearrange("p (m c) -> p m c", m=2),
                                               ACT.Gelu_apprx_tanh), tk)
                bf[4] = t
                cz[f"hid{kv}"] = t
        return go

    cmps = [lambda: make_z(0)] + [cmp_step(0, i) for i in range(4)]
    cmps += [lambda: make_z(1)] + [cmp_step(1, i) for i in range(4)]
    def compressed():
        for k in range(2):
            tk = pe(lambda e, k=k: e.matmul(bank[4][:, 128:188], w2[:, 0, k, :], hidT[:, 0, k, :], start=k == 0,
                                            stop=k == 1, skip_group_check=True),
                    [w2_in, cz["hid0"], cz["hid1"], bf[4]], inc=k == 1)
        cz["kcc"] = bf[4] = act(lambda e: e.activation(kccT[:, :], bank[4][:, 128:188], ACT.Copy), tk)
        for g in range(4):
            for k in range(2):
                tk = pe(lambda e, g=g, k=k: e.matmul(
                    bank[5][0:15, 128 * g:128 * g + 128], hidT[:, 1, k, 15 * g:15 * g + 15],
                    w2[:, 1, k, :], start=k == 0, stop=k == 1, skip_group_check=True),
                    bf[5], inc=(g, k) == (3, 1))
        t_vz = dve(lambda e: e.memset(Vpad[:, :, :], 0.0), h1["ht"])
        t_vp = None
        for g in range(4):
            for j in range(4):
                t_vp = dve(lambda e, g=g, j=j: e.tensor_copy(Vpad[32 * j:32 * j + 15, 4 * g + j, :],
                                                             bank[5][0:15, 128 * g:128 * g + 128]), tk, t_vz)
        cz["vp"] = bf[5] = t_vp
        cz["pc0"] = dve(lambda e: e.memset(Pc[:, :, :, :], 0.0), zfree[0])

    def spread(a, n):
        return bass.AP(tensor=a.tensor, offset=a.offset, ap=[list(d) for d in a.ap] + [[0, n]])

    def cmp_scores(g):
        for b in range(2):
            for i in range(4):
                n = 15 * (4 * b + i)
                tk = pe(lambda e, b=b, n=n, h=4 * g + i: e.matmul(
                    bank[6][:, n:n + 15], qT[:, h, 128 * b:128 * b + 128], kccT[:, 15 * g:15 * g + 15],
                    start=n == 0, stop=True, skip_group_check=True),
                    [cz["kcc"], tk1[f"q{g}"], bf[6]], inc=(b, i) == (1, 3))
        ncm = (7, 15)
        pv = [Pc[:, b, :, 0:ncm[b]] for b in range(2)]
        cv = [biasA[:, 4 * g:4 * g + 4, o:256:16] for o in (159, 31)]
        c4 = cst[:, :, :].rearrange("p r (b h) -> p r b h", b=2)[:, :, :, 4 * g:4 * g + 4]
        t = [dve(lambda e, b=b: e.tensor_tensor(
            pv[b], bank[6][:, 60 * b:60 * b + 60].rearrange("p (h c) -> p h c", c=15)[:, :, 0:ncm[b]], cv[b], ALU.add),
            tk, cz["pc0"], cz.get("turned"), T["biasA"]) for b in range(2)]
        bf[6] = t
        t = [dve(lambda e, b=b: e.tensor_reduce(c4[:, 0, b, :], pv[b], AX_X, ALU.max), t[b]) for b in range(2)]
        t = dve(lambda e: e.tensor_scalar(c4[:, 1, :, :], c4[:, 0, :, :], -1e29, None, ALU.max), t)
        t = [dve(lambda e, b=b: e.tensor_tensor(pv[b], pv[b], spread(c4[:, 1, b, :], ncm[b]), ALU.subtract), t) for b in range(2)]
        t = [act(lambda e, b=b: e.activation(pv[b], pv[b], ACT.Exp), t[b]) for b in range(2)]
        t = [dve(lambda e, b=b: e.tensor_reduce(c4[:, 2, b, :], pv[b], AX_X, ALU.add), t[b]) for b in range(2)]
        t = dve(lambda e: e.tensor_scalar(c4[:, 0, :, :], c4[:, 2, :, :], 1e-30, None, ALU.max), t)
        t = dve(lambda e: e.reciprocal(c4[:, 3, :, :], c4[:, 0, :, :]), t)
        t = dve(lambda e: e.tensor_tensor(c4[:, 1, :, :], c4[:, 3, :, :],
                                          gates[:, 0, 4 * g:4 * g + 4, 0:2].rearrange("p h b -> p b h"), ALU.mult),
                t, tk1["gates"])
        cz[f"p{g}"] = [dve(lambda e, b=b: e.tensor_tensor(pv[b], pv[b], spread(c4[:, 1, b, :], ncm[b]), ALU.mult), t)
                       for b in range(2)]

    def cmp_turn(g):
        for b in range(2):
            tk = pe(lambda e, b=b: e.transpose(
                bank[6][:, 128 * b:128 * b + 128], Pc[:, b, :, :], ident[:, :]),
                cz[f"p{g}"], bf[6], inc=b == 1)
        cz["turned"] = tk
        cz[f"pct{g}"] = bf[6] = act(lambda e: e.activation(PcT[:, g, :], bank[6][:, 0:256], ACT.Copy), tk, h1["ht"])

    extra["gemv"], extra["credit"] = 0.4, -0.8
    extra["every"].extend([pause] * 4)
    extra["every"].extend(table_out("tA", L_tA, toepA, R16a, i) for i in range(4))
    extra["every"].extend(cmps)
    extra["every"].extend(table_in(i) for i in range(4))
    extra["every"].extend([pause] * 6)
    extra["every"].extend(table_out("tB", L_tB, toepB, R16b, i) for i in range(4))
    run(nsa[0], nsa[1])
    drain()
    run(*nsa[2:7])
    side.append(compressed)
    run(nsa[7])
    drain()
    ready1 = [tk1["ks"], tk1["kw"]]

    def unit1(h):
        g = h // 4

        def br(kT, v):
            return dict(qk=lambda blk, n: [(qT[:, h, 128 * blk:128 * blk + 128], kT[:, g, 0:n])],
                        bias=biasA[:, h, :], scale=1.0, least=None,
                        v=lambda k: v[:, k, 128 * g:128 * g + 128])
        return dict(br=[br(ksT, vs), br(kwT, vw)], ready=[ready1, tk1[f"q{g}"]],
                    v_ready=lambda: [tk1["vs"], tk1["vw"], cz["vp"], cz[f"pct{g}"]],
                    bias_tok=T["biasA"], sink=None, gate=gates[:, 1, h, :], gate_tok=tk1["gates"],
                    more=(Vpad[:, h, :], PcT[:, g, :]), put=put1(h))

    def split4(HIs, LOs, src, k, toks, *waits):
        t_hi = act(lambda e: e.activation(HIs[:, k:k + 4, :], src, ACT.Copy), *waits)
        t_lo = dve(lambda e: e.tensor_tensor(LOs[:, k:k + 4, :], src, HIs[:, k:k + 4, :].bitcast(F32), ALU.subtract),
                   t_hi, *waits)
        toks["t"][k // 4] = [t_hi, t_lo]

    def collect(buf, toks, read):
        got, ready = {}, []

        def put(k):
            def go(o_tok):
                t = act(lambda e: e.activation(buf[:, k, :], bank[7][:, 0:S], ACT.Copy), o_tok)
                got[k] = t
                att["O"] = o_tok
                if k % 4 == 3:
                    ready.append(k - 3)
                    flush()
                return t
            return go

        def flush():
            while ready and "done" in read:
                k = ready.pop(0)
                split4(HI, LO, buf[:, k:k + 4, :], k, toks, [got[k + i] for i in range(4)], read["done"])
                if toks is h2 and k == 12:
                    first_block_over()
        return put, flush

    att = {}
    h2["t"] = [None] * 4
    nsa_read = {}

    def warm_sqrt():
        act(lambda e: e.activation(spare[:, :], epsc[:, :], ACT.Sqrt), eps_set)

    def first_block_over():
        free = [att["O"], h2["t"]]
        sq_free[:] = [free, free]
        sr_free[:] = [[sr_free[0], free], [sr_free[1], free]]
        ht_free[:] = [[ht_free[0], free], [ht_free[1], free]]
        hid["free"] = hid["ufree"] = free

    put1, flush1 = collect(qT, h2, nsa_read)
    steps1 = attention(SP1, PT1, [zfree[0], tk1["kc"], tk1["vc"], cz["z"]])
    extra["rate"] = 1.3
    extra["gemv"] = 0.3
    for g in range(4):
        side.extend([pause, pause, lambda g=g: cmp_scores(g), pause, lambda g=g: cmp_turn(g)])
        side.extend(steps1([unit1(h) for h in range(4 * g, 4 * g + 4)], g == 3))
        if g < 3:
            run(nsa[8 + g])
    nsa_read["done"] = chunk_done[cursor[0] - 1]
    flush1()
    xb1["free"] = rstd_free[0]
    run(out1[0], out1[1])
    extra["gemv"] = 0.66
    run(out1[2], out1[3])
    out1_done = chunk_done[cursor[0] - 1]

    def rstd_3():
        T["rstd3"] = rstd_of(xb1["box"], D)
    side.append(rstd_3)
    hid["free"] = [out1_done, hid["free"]]
    for pi, (up, down) in enumerate(ffn1):
        run(*up)
        xb2["free"] = h3["t"]
        side.extend([pause] * 8 + [warm_sqrt])
        run(*down)
        hid["free"] = chunk_done[cursor[0] - 1]
    ffn1_done = chunk_done[cursor[0] - 1]
    extra["gemv"] = 0.0
    drain()
    pe_later()
    while True:
        f = next(gq_iter, 0)
        if f == 0:
            break
        if f is not None:
            f()
    drain()

    tg = [dve(lambda e, o=o, g=g, c=c: e.scalar_tensor_tensor(o[:, :], mod[:, c:c + 16], 1.0, g, ALU.add, ALU.mult),
              mod_tok, T["cols"]) for o, g, c in ((G1c, g_att2, 16), (G2c, g_mlp2, 64))]
    tg12 = dve(lambda e: e.tensor_tensor(G12[:, :], G1c[:, :], g_fin, ALU.mult), tg)
    sums2 = bank[6][:, S:2 * S]
    t = dve(lambda e: e.tensor_scalar(std2[:, :], ss, EPS / D, None, ALU.mult), xb2["box"]["tok"], xb2["box2"]["tok"], sr_free)
    t2 = dve(lambda e: e.scalar_tensor_tensor(std2[:, :], sums2, 1.0 / D, std2[:, :], ALU.mult, ALU.add), t)
    t = act(lambda e: e.activation(std2[:, :], std2[:, :], ACT.Sqrt, bias=eps2c[:, 0:1]), t2, eps_set)
    t12 = dve(lambda e: e.reciprocal(rstd2[:, :], std2[:, :]), t)
    bf[6] = [bf[6], t2]
    t1_box = {}
    normed(h4, G12, rstd2, mod[:, 0:16], t12, tg12, ffn1_done)

    def final_rstd():
        bf6 = bf[6]
        t1_box["t"] = rstd_of(xb2["box"], D)
        bf[6] = [bf6, bf[6]]

    def final_norm(m0):
        for m in range(m0, m0 + 4):
            t = dve(lambda e, m=m: e.scalar_tensor_tensor(xT[:, m, :], xT[:, m, :], g_fin[:, m:m + 1], rstd[:, :],
                                                          ALU.mult, ALU.mult), t1_box["t"], xb2["x"], h4["y"])
        rstd_free[0] = xb3["free"] = t

    att2["free"] = [ffn1_done, hid["t"], sq_free, sr_free, sa_tok, acc_free[0]]
    L_rope = Landing(sem("l_rope"))
    L_rope.start(pool, cosT[:, :], A["c_cos"], att2["free"])
    L_rope.start(pool, causal[:, :], A["c_causal"], att2["free"])
    att2["rope_in"] = L_rope.start(pool, sinT[:, :], A["c_sin"], att2["free"])
    biasB_in = L_bB.start(pool, biasB[:, :, :], toeplitz(toepB, 0, 16), T["tB"], att2["free"])
    att2["pad0"] = [pool(lambda e, t_=t_: e.memset(t_, 0.0), att2["free"]) for t_ in
                    (Kpad[:, :, :, :], Vpad2[:, :, :, :, :], krp[0:64, :])]
    t_sk = None
    for j in range(4):
        t_sk = dve(lambda e, j=j: e.tensor_copy(SK[:, :, j], sinkr[:, j % 2:16:2]), k_in)

    def latent(ms, name, n, gcols, ready):
        a, b = ms[0], ms[-1] + 1
        sq_t = act(lambda e: e.activation(CSQ[:, a:b, :], CQ[:, a:b, :], ACT.Square), ready, att2["free"])

        def go():
            for j, m in enumerate(ms):
                tk = pe(lambda e, m=m, j=j: e.matmul(ss, ones[:, :], CSQ[:, m, :], start=j == 0, stop=j == len(ms) - 1,
                                                     skip_group_check=True), [sq_t, bf[6]], inc=j == len(ms) - 1)
            tr = rstd_of({"tok": tk}, n)
            for j, m in enumerate(ms):
                t = dve(lambda e, m=m, j=j: e.scalar_tensor_tensor(CQ[:, m, :], CQ[:, m, :], gcols[:, j:j + 1],
                                                                   rstd[:, :], ALU.mult, ALU.mult), tr, sq_t)
            rstd_free[0] = t
            t_hi = act(lambda e: e.activation(CQH[:, a:b, :], CQ[:, a:b, :], ACT.Copy), t, att2["free"])
            t_lo = dve(lambda e: e.tensor_tensor(CQL[:, a:b, :], CQ[:, a:b, :], CQH[:, a:b, :].bitcast(F32),
                                                 ALU.subtract), t, t_hi, att2["free"])
            hq[name] = [t_hi, t_lo]
        later.append(go)

    run(sl_qa[0])
    side.append(final_rstd)
    side.extend(lambda m0=m0: final_norm(m0) for m0 in range(0, KT, 4))
    att2["free"] = [att2["free"], ht_free]
    att2["pad0"] = [att2["pad0"], pool(lambda e: e.memset(qrT[0:64, :, :], 0.0), att2["free"])]
    run(sl_ka)

    h5["t"] = [None] * 4
    in2_read = {}
    put2, flush2 = collect(qaT, h5, in2_read)
    h_tok = {}

    def put3(k):
        def go(o_tok):
            t_hi = act(lambda e: e.activation(HI[:, k, :], bank[7][:, 0:S], ACT.Copy), o_tok, in2_read["done"])
            t_lo = dve(lambda e: e.tensor_tensor(LO[:, k, :], bank[7][:, 0:S], HI[:, k, :].bitcast(F32),
                                                 ALU.subtract), t_hi, o_tok, in2_read["done"])
            h_tok[k] = [t_hi, t_lo]
            att["O"] = o_tok
            if k % 4 == 3:
                h5["t"][k // 4] = [h_tok[k - i] for i in range(4)]
            if k == 15:
                second_block_over()
            return [t_hi, t_lo]
        return go

    def second_block_over():
        free = [att["O"], h5["t"], att2["ropefree"]]
        sq_free[:] = [free, free]
        sr_free[:] = [[sr_free[0], free], [sr_free[1], free]]
        ht_free[:] = [[ht_free[0], free], [ht_free[1], free]]
        sa_tok[:] = [[sa_tok[0], free], [sa_tok[1], free]]
        hid["free"] = free
        warm_sqrt()

    steps2 = attention(SP2, PT2, [att2["free"]])

    def unit2(i):
        kv = i // 4

        def br(par):
            return dict(qk=lambda blk, n: [(qaT[:, i, 128 * blk:128 * blk + 128], Kpad[:, kv, par, 0:n])],
                        bias=biasB[:, 2 * i + par, :], scale=1.0, least=lambda j: SK[:, i, j:j + 1],
                        v=lambda k: Vpad2[:, kv, par, k, :])
        return dict(br=[br(0), br(1)], ready=[tk1[f"qa{kv}"], att2["k"], att2["pad0"]], v_ready=lambda: att2["kv"],
                    bias_tok=[biasB_in, t_sk], sink=SK[:, i, :], gate=None, gate_tok=None, more=None, put=put2(i))

    def unit3(h):
        b = dict(qk=lambda blk, n: [(qnT[:, h, 128 * blk:128 * blk + 128], knT[:, h, 0:n]),
                                    (qrT[:, h, 128 * blk:128 * blk + 128], krp[:, 0:n])],
                 bias=causal[:, :], scale=192.0 ** -0.5, least=None,
                 v=lambda k: vb[:, k, 128 * h:128 * h + 128])
        return dict(br=[b], ready=[tk1[f"qm{h // 2}"], tk1[f"km{h // 2}"], att2["kr"]],
                    v_ready=lambda: tk1[f"km{h // 2}"], bias_tok=att2["rope_in"], sink=None, gate=None,
                    gate_tok=None, more=None, put=put3(8 + h))

    extra["rate"] = 2
    side.extend(steps2([unit2(i) for i in range(4)], False))
    run(sl_qa[1])
    side.extend(steps2([unit2(i) for i in range(4, 8)], False))
    run(sl_cq)
    latent([0, 1, 2], "q", 384, gq, att2["cq"])
    run(sl_ckv)
    in2_read["done"] = chunk_done[cursor[0] - 1]
    flush2()
    latent([3], "kv", 128, gkv, att2["ckv"])
    run(*uq)
    drain()
    att2["swa_done"] = bf[5]
    run(*ukv)
    extra["rate"] = 2
    side.extend(steps2([unit3(h) for h in range(8)], True))
    run(out2[0], out2[1])
    run(out2[2], out2[3])
    out2_done = chunk_done[cursor[0] - 1]
    drain()
    pe_later()

    t_rstd = rstd_of(xb3["box"], D)
    normed(h6, G2c, rstd, mod[:, 48:64], t_rstd, tg, out2_done)
    hid["free"] = [out2_done, hid["free"]]
    for pi, (up, down) in enumerate(ffn2):
        hid["xg"] = hid["free"]
        run(*up)
        hid["yrow"] = [hid["t"], sa_tok, ht_free]
        xb4["free"] = h6["y"]
        run(*down)
        hid["free"] = chunk_done[cursor[0] - 1]
    ffn2_done = chunk_done[cursor[0] - 1]
    drain()
    pe_later()

    t = act(lambda e: e.activation(stdc[:, :], bank[6][:, S:S + 2], ACT.Sqrt, bias=epsc[:, 0:1], scale=1.0 / D),
            xb4["box"]["tok"], eps_set)
    t = dve(lambda e: e.reciprocal(rstdc[:, :], stdc[:, :]), t)
    L_out = Landing(sem("l_out"))
    out_rows = out[0].rearrange("(t p) d -> p t d", p=128)
    for m0 in (0, 4, 8, 12):
        sl = slice(128 * m0, 128 * m0 + 512)
        src = [YROW[:, h, sl] if m0 < 12 else bank[4 + h][:, :] for h in range(2)]
        ts = [act(lambda e, sl=sl, src=src: e.activation(YROW[:, 0, sl], src[0], ACT.Copy, scale=rstdc[:, 0:1]), t, y_rows[m0]),
              dve(lambda e, sl=sl, src=src: e.tensor_scalar(YROW[:, 1, sl], src[1], rstdc[:, 1:2], None, ALU.mult), t,
                  y_rows[m0])]
        y_tok = L_out.start(sp, out_rows[:, :, sl], YROW[:, :, sl], ts)

    assert cursor[0] == len(chunks)

    with nc.Block() as block:
        @block.tensor
        def _(e):
            pe.play(e)

        @block.scalar
        def _(e):
            act.play(e)

        @block.vector
        def _(e):
            dve.play(e)

        @block.gpsimd
        def _(e):
            pool.play(e)

        @block.sync
        def _(e):
            sp.play(e)
            e.wait_ge(*T["tA"])
            e.wait_ge(*T["tB"])
            e.wait_ge(*y_tok)


def kernel(**inputs):
    import concourse.bacc as _bacc
    from concourse.bass_utils import run_bass_kernel_spmd as _run

    nc = _bacc.Bacc("TRN2", target_bir_lowering=False, num_devices=1)
    arrays = {n: np.ascontiguousarray(inputs[n]) for n in IN_NAMES}
    arrays.update(shape_constants())
    A = {}
    for name, a in arrays.items():
        A[name] = nc.dram_tensor(f"in_{name}", a.shape, F32, kind="ExternalInput").ap()
    out = nc.dram_tensor("out_y", (1, S, D), F32, kind="ExternalOutput").ap()
    build(nc, A, out)
    r = _run(nc, [{f"in_{n}": a for n, a in arrays.items()}], core_ids=[0])
    return r.results[0]["out_y"]
```
